# Optimizing a Trainium2 kernel written in Bass

```python
import jax, jax.numpy as jnp
from jax import lax
import numpy as np

D_MODEL = 2048
BATCH = 1
SEQ = 256
DEPTH = 2

N_MIXERS = 3
EPS = 1e-6
M_HEADS = 8
M_DV = D_MODEL // M_HEADS
M_DQK = M_DV // 2
M_CHUNK = 64
F_BIAS_INIT = 3.0
A_HEADS = 16
A_DHEAD = D_MODEL // A_HEADS
IDX_HEADS = 16
IDX_DIM = 64
TOPK_MAX = 256
Q_BLOCK = 128
CONV_WIDTH = 31
D_FF = 5632
FFN_CONV_WIDTH = 3

kernel_name = "hybrid_mlstm_dsa_conformer_convffn"

def n_layers_of(kind):
    return (DEPTH - kind + N_MIXERS - 1) // N_MIXERS

def rms_norm(x, g):
    xf = x.astype(jnp.float32)
    y = xf * lax.rsqrt(jnp.mean(xf * xf, -1, keepdims=True) + EPS)
    return (y * g.astype(jnp.float32)).astype(x.dtype)

def layer_norm(x, g, b):
    xf = x.astype(jnp.float32)
    mu = jnp.mean(xf, -1, keepdims=True)
    xc = xf - mu
    y = xc * lax.rsqrt(jnp.mean(xc * xc, -1, keepdims=True) + EPS)
    return (y * g.astype(jnp.float32) + b.astype(jnp.float32)).astype(x.dtype)

def causal_depthwise_conv(x, w):
    width, ch = w.shape
    return lax.conv_general_dilated(
        x, w[:, None, :].astype(x.dtype), window_strides=(1,), padding=[(width - 1, 0)],
        dimension_numbers=('NWC', 'WIO', 'NWC'), feature_group_count=ch)

def mlstm_chunkwise(q, k, v, log_i, log_f):
    B, H, T, dk = q.shape
    dv = v.shape[-1]
    L = M_CHUNK
    nc = T // L

    def chunks(a):
        return jnp.moveaxis(a.reshape(B, H, nc, L, *a.shape[3:]), 2, 0)

    causal = jnp.tril(jnp.ones((L, L), dtype=bool))

    def step(carry, xs):
        C, n, m = carry
        qb, kb, vb, ib, fb = xs
        b = jnp.cumsum(fb, axis=-1)
        d = b[..., :, None] - b[..., None, :] + ib[..., None, :]
        d = jnp.where(causal, d, -jnp.inf)
        inter = b + m[..., None]
        m_t = jnp.maximum(inter, jnp.max(d, axis=-1))
        w_intra = jnp.exp(d - m_t[..., None])
        w_inter = jnp.exp(inter - m_t)
        s = jnp.einsum('bhtd,bhsd->bhts', qb, kb) * w_intra
        num = (w_inter[..., None] * jnp.einsum('bhtd,bhde->bhte', qb, C)
               + jnp.einsum('bhts,bhse->bhte', s, vb))
        den = w_inter * jnp.einsum('bhtd,bhd->bht', qb, n) + jnp.sum(s, axis=-1)
        h = num / jnp.maximum(jnp.abs(den), jnp.exp(-m_t))[..., None]
        bl = b[..., -1]
        g = bl[..., None] - b + ib
        m_new = jnp.maximum(bl + m, jnp.max(g, axis=-1))
        a_prev = jnp.exp(bl + m - m_new)
        a_s = jnp.exp(g - m_new[..., None])
        C_new = a_prev[..., None, None] * C + jnp.einsum('bhs,bhsd,bhse->bhde', a_s, kb, vb)
        n_new = a_prev[..., None] * n + jnp.einsum('bhs,bhsd->bhd', a_s, kb)
        return (C_new, n_new, m_new), h

    init = (jnp.zeros((B, H, dk, dv), jnp.float32), jnp.zeros((B, H, dk), jnp.float32),
            jnp.zeros((B, H), jnp.float32))
    _, h = lax.scan(step, init, tuple(map(chunks, (q, k, v, log_i, log_f))))
    return jnp.moveaxis(h, 0, 2).reshape(B, H, T, dv)

def mlstm_mixer(x, w_in, gate_b, head_g, w_out):
    B, T, _ = x.shape
    hk = M_HEADS * M_DQK
    hv = M_HEADS * M_DV
    proj = x @ w_in
    q, k, v, o, gates = jnp.split(proj, [hk, 2 * hk, 2 * hk + hv, 2 * hk + 2 * hv], axis=-1)

    def heads(a, d):
        return a.reshape(B, T, M_HEADS, d).transpose(0, 2, 1, 3).astype(jnp.float32)

    q = heads(q, M_DQK) * (M_DQK ** -0.5)
    k = heads(k, M_DQK)
    v = heads(v, M_DV)
    gates = (gates + gate_b).astype(jnp.float32).transpose(0, 2, 1)
    log_i = gates[:, :M_HEADS]
    log_f = jax.nn.log_sigmoid(gates[:, M_HEADS:])
    h = mlstm_chunkwise(q, k, v, log_i, log_f).transpose(0, 2, 1, 3)
    h = h * lax.rsqrt(jnp.mean(h * h, -1, keepdims=True) + EPS) * head_g.reshape(M_HEADS, M_DV).astype(jnp.float32)
    h = h.reshape(B, T, hv) * jax.nn.sigmoid(o.astype(jnp.float32))
    return h.astype(x.dtype) @ w_out

def dsa_mixer(x, w_in, q_g, k_g, w_out):
    B, T, _ = x.shape
    topk = min(TOPK_MAX, T // 4)
    qd = A_HEADS * A_DHEAD
    qid = IDX_HEADS * IDX_DIM
    cuts = list(np.cumsum([qd, A_DHEAD, A_DHEAD, qid, IDX_DIM]))
    q, k, v, qi, ki, wi = jnp.split(x @ w_in, [int(c) for c in cuts], axis=-1)
    q = rms_norm(q.reshape(B, T, A_HEADS, A_DHEAD), q_g) * (A_DHEAD ** -0.5)
    k = rms_norm(k, k_g)
    qi = qi.reshape(B, T, IDX_HEADS, IDX_DIM)
    wi = wi.astype(jnp.float32) * ((IDX_HEADS * IDX_DIM) ** -0.5)
    nb = T // Q_BLOCK
    key_pos = jnp.arange(T)

    def blocks(a):
        return jnp.moveaxis(a.reshape(B, nb, Q_BLOCK, *a.shape[2:]), 1, 0)

    def attend(xs):
        qb, qib, wib, q0 = xs
        qpos = q0 + jnp.arange(Q_BLOCK)
        idx_logits = jnp.einsum('bqhd,bsd->bqhs', qib, ki)
        score = jnp.einsum('bqhs,bqh->bqs', jax.nn.relu(idx_logits).astype(jnp.float32), wib)
        score = jnp.where(key_pos[None, None, :] <= qpos[None, :, None], score, -jnp.inf)
        _, sel = lax.top_k(score, topk)
        valid = sel <= qpos[None, :, None]
        k_sel = jax.vmap(lambda kk, ii: kk[ii])(k, sel)
        v_sel = jax.vmap(lambda vv, ii: vv[ii])(v, sel)
        logits = jnp.einsum('bqhd,bqkd->bhqk', qb, k_sel).astype(jnp.float32)
        logits = jnp.where(valid[:, None], logits, -jnp.inf)
        p = jax.nn.softmax(logits, axis=-1).astype(v.dtype)
        return jnp.einsum('bhqk,bqkd->bqhd', p, v_sel)

    out = lax.map(attend, (blocks(q), blocks(qi), blocks(wi), jnp.arange(nb) * Q_BLOCK))
    out = jnp.moveaxis(out, 0, 1).reshape(B, T, qd)
    return out @ w_out

def conv_mixer(x, w_in, dw_w, dw_b, ln_g, ln_b, w_out):
    a, g = jnp.split(x @ w_in, 2, axis=-1)
    u = a * jax.nn.sigmoid(g)
    u = causal_depthwise_conv(u, dw_w) + dw_b
    u = jax.nn.silu(layer_norm(u, ln_g, ln_b))
    return u @ w_out

def conv_ffn(x, w_up, dw_w, w_down):
    h = causal_depthwise_conv(x @ w_up, dw_w)
    a, b = jnp.split(h, 2, axis=-1)
    return (jax.nn.silu(a) * b) @ w_down

def setup_inputs(seed: int = 0) -> dict:
    key = jax.random.key(seed)
    ks = jax.random.split(key, 24)
    D = D_MODEL
    na, nb_, nc = n_layers_of(0), n_layers_of(1), n_layers_of(2)
    out_scale = (2 * DEPTH) ** -0.5

    def nrm(k, shape, scale):
        return jax.random.normal(k, shape, jnp.float32) * scale

    pa = 2 * M_HEADS * M_DQK + 2 * M_HEADS * M_DV + 2 * M_HEADS
    pb = A_HEADS * A_DHEAD + 2 * A_DHEAD + IDX_HEADS * IDX_DIM + IDX_DIM + IDX_HEADS
    gate_b = jnp.concatenate([nrm(ks[3], (na, M_HEADS), 0.1),
                              F_BIAS_INIT + nrm(ks[4], (na, M_HEADS), 0.1)], axis=-1)
    return {
        'x': nrm(ks[0], (BATCH, SEQ, D), 1.0),
        'mix_norm_g': 1.0 + nrm(ks[1], (DEPTH, D), 0.02),
        'ffn_norm_g': 1.0 + nrm(ks[2], (DEPTH, D), 0.02),
        'mlstm_w_in': nrm(ks[5], (na, D, pa), D ** -0.5),
        'mlstm_gate_b': gate_b,
        'mlstm_head_g': 1.0 + nrm(ks[6], (na, M_HEADS * M_DV), 0.02),
        'mlstm_w_out': nrm(ks[7], (na, M_HEADS * M_DV, D), (M_HEADS * M_DV) ** -0.5 * out_scale),
        'dsa_w_in': nrm(ks[8], (nb_, D, pb), D ** -0.5),
        'dsa_q_g': 1.0 + nrm(ks[9], (nb_, A_DHEAD), 0.02),
        'dsa_k_g': 1.0 + nrm(ks[10], (nb_, A_DHEAD), 0.02),
        'dsa_w_out': nrm(ks[11], (nb_, A_HEADS * A_DHEAD, D), (A_HEADS * A_DHEAD) ** -0.5 * out_scale),
        'conv_w_in': nrm(ks[12], (nc, D, 2 * D), D ** -0.5),
        'conv_dw_w': nrm(ks[13], (nc, CONV_WIDTH, D), CONV_WIDTH ** -0.5),
        'conv_dw_b': nrm(ks[14], (nc, D), 0.02),
        'conv_ln_g': 1.0 + nrm(ks[15], (nc, D), 0.02),
        'conv_ln_b': nrm(ks[16], (nc, D), 0.02),
        'conv_w_out': nrm(ks[17], (nc, D, D), D ** -0.5 * out_scale),
        'ffn_w_up': nrm(ks[18], (DEPTH, D, 2 * D_FF), D ** -0.5),
        'ffn_dw_w': nrm(ks[19], (DEPTH, FFN_CONV_WIDTH, 2 * D_FF), FFN_CONV_WIDTH ** -0.5),
        'ffn_w_down': nrm(ks[20], (DEPTH, D_FF, D), D_FF ** -0.5 * out_scale),
    }

def reference(x, mix_norm_g, ffn_norm_g, mlstm_w_in, mlstm_gate_b, mlstm_head_g, mlstm_w_out,
              dsa_w_in, dsa_q_g, dsa_k_g, dsa_w_out, conv_w_in, conv_dw_w, conv_dw_b,
              conv_ln_g, conv_ln_b, conv_w_out, ffn_w_up, ffn_dw_w, ffn_w_down):
    for i in range(DEPTH):
        kind = i % N_MIXERS
        j = i // N_MIXERS
        h = rms_norm(x, mix_norm_g[i])
        if kind == 0:
            y = mlstm_mixer(h, mlstm_w_in[j], mlstm_gate_b[j], mlstm_head_g[j], mlstm_w_out[j])
        elif kind == 1:
            y = dsa_mixer(h, dsa_w_in[j], dsa_q_g[j], dsa_k_g[j], dsa_w_out[j])
        else:
            y = conv_mixer(h, conv_w_in[j], conv_dw_w[j], conv_dw_b[j], conv_ln_g[j],
                           conv_ln_b[j], conv_w_out[j])
        x = x + y
        x = x + conv_ffn(rms_norm(x, ffn_norm_g[i]), ffn_w_up[i], ffn_dw_w[i], ffn_w_down[i])
    return x


_drawn_inputs = setup_inputs


def setup_inputs(seed=0):
    import zlib

    import numpy as np

    out = dict(_drawn_inputs(seed))
    spreads = {}
    factors = {'mix_norm_g': 3.073,
     'ffn_norm_g': 4.041,
     'mlstm_head_g': 6.163,
     'dsa_q_g': 8.0,
     'dsa_k_g': 8.0}
    for name, (base, spread) in spreads.items():
        noise = np.random.default_rng([zlib.crc32(name.encode()), seed]).standard_normal(out[name].shape)
        drawn = base * np.exp(spread * noise) if base else spread * noise
        out[name] = __import__('jax').numpy.asarray(drawn.astype(out[name].dtype))
    for name, factor in factors.items():
        out[name] = (out[name] * factor).astype(out[name].dtype)
    return out
```

```python
from contextlib import ExitStack

import numpy as np

import concourse.bass as bass
from concourse import mybir

F32 = mybir.dt.float32
F32R = mybir.dt.float32r
ALU = mybir.AluOpType
ACT = mybir.ActivationFunctionType
AX = mybir.AxisListType

P = 128
T = 256
D = 2048
KT = D // P
EPS = 1e-6
M_HEADS, DK, DV = 8, 128, 256
A_HEADS, DH = 16, 128
I_HEADS, I_DIM = 16, 64
TOPK = T // 4
D_FF = 5632
UP_TILES = 2 * D_FF // P
GROUP = 4
GROUPS = D_FF // P // GROUP
TAPS = 3
NEG = -1e30

BLK = 8
LEAD = 3
RING = 4

H_MLSTM = 0
H_WOUT0 = H_MLSTM + 12 * M_HEADS
H_FFN0 = H_WOUT0 + 2 * KT
H_DSA_QI = H_FFN0 + 24 * GROUPS
H_DSA_KV = H_DSA_QI + 16
H_DSA_Q = H_DSA_KV + 4
H_WOUT1 = H_DSA_Q + 2 * A_HEADS
H_FFN1 = H_WOUT1 + 2 * KT
H_END = H_FFN1 + 24 * GROUPS

D_MLSTM = 0
D_WOUT0 = D_MLSTM + 3 * M_HEADS
D_FFN0 = D_WOUT0 + KT // 2
D_DSA_QI = D_FFN0 + 8 * GROUPS
D_DSA_KV = D_DSA_QI + 4
D_DSA_Q = D_DSA_KV + 1
D_WOUT1 = D_DSA_Q + A_HEADS // 2
D_FFN1 = D_WOUT1 + KT // 2

C_MLSTM = 0
C_FFN0 = C_MLSTM + 3 * M_HEADS
C_DSA_QI = C_FFN0 + 4 * GROUPS
C_DSA_KV = C_DSA_QI + 4
C_DSA_Q = C_DSA_KV + 1
C_FFN1 = C_DSA_Q + A_HEADS // 2

M_K, M_V, M_O, M_GATE = M_HEADS * DK, 2 * M_HEADS * DK, 2 * M_HEADS * DK + M_HEADS * DV, 2 * M_HEADS * (DK + DV)
A_KV, A_QI = A_HEADS * DH, A_HEADS * DH + 2 * DH
A_KW = A_QI + I_HEADS * I_DIM

V_MIXG, V_FFNG, V_HEADG, V_QG, V_KG, V_ROWS = 0, 2 * KT, 4 * KT, 5 * KT, 5 * KT + 1, 5 * KT + 2


def trunk(nc, x, mix_norm_g, ffn_norm_g, mlstm_w_in, mlstm_gate_b, mlstm_head_g, mlstm_w_out,
          dsa_w_in, dsa_q_g, dsa_k_g, dsa_w_out, ffn_w_up, ffn_dw_w, ffn_w_down, out):
    ctx = ExitStack()
    with ctx:
        def sb(name, shape, dt=F32):
            return ctx.enter_context(nc.sbuf_tensor(name, shape, dt))

        def sem(name):
            return ctx.enter_context(nc.semaphore(name))

        raw = sb("raw", [P, RING, 2 * BLK * P])
        w_hi = sb("w_hi", [P, RING, BLK, P], F32R)
        w_lo = sb("w_lo", [P, RING, BLK, P], F32R)
        X = sb("X", [P, KT, T])
        xs = sb("xs", [P, KT, 2, T], F32R)
        mix = sb("mix", [P, KT, 2, T], F32R)
        hid = sb("hid", [P, GROUP, 2, T], F32R)
        rms_scale = sb("rms_scale", [P, T])
        ident = sb("ident", [P, P])
        ones = sb("ones", [P, T])
        neg_future = sb("neg_future", [P, T])
        mask_q = sb("mask_q", [P, 3 * P])
        vecs = sb("vecs", [P, V_ROWS])
        taps = sb("taps", [P, 2, TAPS, UP_TILES])
        gate_b = sb("gate_b", [40, 1])
        power = sb("power", [P, 2 * T])
        var_x = sb("var_x", [P, T])
        tail = sb("tail", [P, 2, T])
        both = sb("both", [P, 2, T])
        pads = sb("pads", [P, 2, T + TAPS - 1])
        sq = sb("sq", [P, 4, T])
        sq_sum = sb("sq_sum", [P, 4, T])
        scratch = sb("scratch", [P, 7400])

        def part(at, *shape, rows=P):
            n = int(np.prod(shape))
            v = scratch[0:rows, at:at + n]
            if len(shape) == 2:
                v = v.rearrange("p (a b) -> p a b", a=shape[0])
            return v

        x_tok = part(0, 2, D)
        vec_rows = part(4096, P, rows=V_ROWS)
        tap_rows = part(4224, 2 * TAPS, P, rows=UP_TILES)
        QK = part(0, 2, T)
        vT = part(512, 2, T)
        V = part(1024, 2, DV)
        og = part(1536, 2, T)
        rows_m = part(2048, 512, rows=M_HEADS)
        head_rows = part(2560, 512, rows=M_HEADS)
        em = part(3072, T)
        E = part(3328, 3 * P)
        S = part(3712, 3 * P)
        den = part(4096, T)
        H = part(4352, 2, T)
        var = part(4864, T)
        rh = part(5120, T)
        HG = part(5376, 2, T)
        a_tok = part(5888, 2, M_HEADS)
        gate_raw = part(5904, KT, 16)
        gates = part(6160, T, rows=40)
        gA = part(6416, T, rows=M_HEADS)
        gB = part(6672, T, rows=M_HEADS)
        gC = part(6928, T, rows=M_HEADS)
        gF = part(4352, T, rows=M_HEADS)
        gate_tail = part(4864, T, rows=40)
        kw_raw = part(2048, KT, 80)
        QI = part(1280, 8, T)
        KI = part(3328, T)
        wiT = part(3584, T)
        WI = part(3840, 2, I_HEADS)
        relu = part(3872, 2, T)
        score = part(4384, 3 * P)
        work = part(4768, 3 * P)
        best = part(5152, 2, 8)
        KV = part(5168, 2, T)
        KN = part(5680, T)
        VA = part(5936, 2, DH)
        qg = part(6192, 1)
        QT = part(0, 2, T)
        var_k = part(1024, T)
        QN = part(512, 2, T)
        var2 = part(1280, 2, T)
        rq = part(1792, 2, T)
        LM = part(2304, 2, 3 * P)
        PT = part(6200, 2, 3 * P)
        rk = part(6968, T)
        mx = part(3072, 2, 2)
        sums = part(3076, 2, 2)
        CA = part(0, 2, T)
        CB = part(512, 2, T)
        SA = part(1024, 2, T)
        G = part(1536, 2, T)

        side_w = [mix[:, 4 * j:4 * j + 4].rearrange("p a b t -> p (a b t)").rearrange("p (k c) -> p k c", k=KT)
                  for j in range(2)]
        side_w_hi, side_w_lo = side_w

        ps = ctx.enter_context(nc.psum_tensor("ps", [P, 8, 512], F32))

        load_done = [sem(f"load_done{i}") for i in range(RING)]
        halves_hi = sem("halves_hi")
        halves_split = sem("halves_split")
        halves_used = sem("halves_used")
        psum_free = sem("psum_free")
        tails = sem("tails")
        chain = sem("chain")
        act_chain = sem("act_chain")
        small_in = sem("small_in")
        x_in = sem("x_in")
        gate_in = sem("gate_in")
        kw_in = sem("kw_in")
        consts_zero = sem("consts_zero")
        consts = sem("consts")
        x_turned = sem("x_turned")
        x_copied = sem("x_copied")
        vecs_turned = sem("vecs_turned")
        vecs_ready = sem("vecs_ready")
        qk_ready = sem("qk_ready")
        xs_hi = sem("xs_hi")
        squares = sem("squares")
        squares_used = sem("squares_used")
        xs_ready = sem("xs_ready")
        sq_ready = sem("sq_ready")
        sq_mm = sem("sq_mm")
        var_ready = sem("var_ready")
        scale_ready = sem("scale_ready")
        side_hi = sem("side_hi")
        side_split = sem("side_split")
        side_mm = sem("side_mm")
        side_tail = sem("side_tail")
        gate_zero = sem("gate_zero")
        gate_dve = sem("gate_dve")
        gate_act = sem("gate_act")
        a_ready = sem("a_ready")
        a_turned = sem("a_turned")
        a_tok_ready = sem("a_tok_ready")
        vT_ready = sem("vT_ready")
        v_turned = sem("v_turned")
        v_ready = sem("v_ready")
        og_ready = sem("og_ready")
        og_exp = sem("og_exp")
        rows_ready = sem("rows_ready")
        qk_mm = sem("qk_mm")
        em_ready = sem("em_ready")
        e_ready = sem("e_ready")
        w_ready = sem("w_ready")
        s_ready = sem("s_ready")
        pv_mm = sem("pv_mm")
        h_ready = sem("h_ready")
        h_sq = sem("h_sq")
        h_mm = sem("h_mm")
        h_var = sem("h_var")
        h_scale = sem("h_scale")
        hg_ready = sem("hg_ready")
        mix_hi = sem("mix_hi")
        mix_ready = sem("mix_ready")
        kw_ready = sem("kw_ready")
        wi_turned = sem("wi_turned")
        wi_ready = sem("wi_ready")
        qi_ready = sem("qi_ready")
        score_mm = sem("score_mm")
        relu_ready = sem("relu_ready")
        relu_used = sem("relu_used")
        kv_ready = sem("kv_ready")
        kv_sq = sem("kv_sq")
        kv_mm = sem("kv_mm")
        kv_var = sem("kv_var")
        kv_scale = sem("kv_scale")
        va_ready = sem("va_ready")
        kn_ready = sem("kn_ready")
        qg_ready = sem("qg_ready")
        q_ready = sem("q_ready")
        q_sq = sem("q_sq")
        q_mm = sem("q_mm")
        q_var = sem("q_var")
        q_scale = sem("q_scale")
        qn_ready = sem("qn_ready")
        logit_mm = sem("logit_mm")
        max_ready = sem("max_ready")
        exp_ready = sem("exp_ready")
        inv_ready = sem("inv_ready")
        probs_ready = sem("probs_ready")
        probs_turned = sem("probs_turned")
        pt_ready = sem("pt_ready")
        av_mm = sem("av_mm")
        up_ready = sem("up_ready")
        tap2_ready = sem("tap2_ready")
        conv_a = sem("conv_a")
        silu_ready = sem("silu_ready")
        gated = sem("gated")
        hid_hi = sem("hid_hi")
        hid_ready = sem("hid_ready")
        y_turned = sem("y_turned")
        y_copied = sem("y_copied")
        stored = sem("stored")

        block = ctx.enter_context(nc.Block())

        w_in0 = mlstm_w_in[0].rearrange("(k p) n -> p k n", p=P)
        w_in1 = dsa_w_in[0].rearrange("(k p) n -> p k n", p=P)
        w_out = [mlstm_w_out[0].rearrange("(k p) n -> p k n", p=P), dsa_w_out[0].rearrange("(k p) n -> p k n", p=P)]
        w_up = [ffn_w_up[l].rearrange("(k p) n -> p k n", p=P) for l in range(2)]
        w_down = [ffn_w_down[l].rearrange("(k p) n -> p k n", p=P) for l in range(2)]

        @block.sync
        def _(sp):
            def load(base, per, i, c, src, cols):
                first = base + c
                number = first + per * i
                assert per % RING == 0
                if first >= RING:
                    sp.wait_ge(halves_split, 2 * (number - RING) + 2)
                dst = raw[:, first % RING].rearrange("p (k n) -> p k n", n=cols)
                sp.dma_start(dst, src).then_inc(load_done[first % RING], 16)

            def pair(base, per, i, c, w, col):
                for hf in range(2):
                    load(base, per, i, c + hf, w[:, BLK * hf:BLK * hf + BLK, bass.ds(col, 2 * P)], 2 * P)

            def head(base, per, i, c, h):
                load(base, per, i, c, w_in0[:, :, bass.ds(h * DK, DK)], DK)
                load(base, per, i, c + 1, w_in0[:, :, bass.ds(M_K + h * DK, DK)], DK)
                pair(base, per, i, c + 2, w_in0, M_V + h * DV)
                pair(base, per, i, c + 4, w_in0, M_O + h * DV)

            def ffn(base, l):
                def group(b, i, g):
                    c = 0
                    for q in range(2):
                        for ab in range(2):
                            pair(b, 12, i, c, w_up[l], ab * D_FF + g * GROUP * P + q * 2 * P)
                            c += 2
                    for q in range(2):
                        for kk in range(2):
                            load(b, 12, i, c, w_down[l][:, bass.ds(g * GROUP + 2 * kk, 2), q * 1024:q * 1024 + 1024], 1024)
                            c += 1
                with sp.Fori(0, GROUPS) as g:
                    group(base, g, g)

            head(0, 12, 0, 0, 0)
            with sp.Fori(0, 3) as i:
                head(6, 12, i, 0, 2 * i + 1)
                head(6, 12, i, 6, 2 * i + 2)
            head(42, 12, 0, 0, 7)
            with sp.Fori(0, 4) as i:
                pair(H_WOUT0 // 2, 4, i, 0, w_out[0], i * 4 * P)
                pair(H_WOUT0 // 2, 4, i, 2, w_out[0], i * 4 * P + 2 * P)
            ffn(H_FFN0 // 2, 0)
            with sp.Fori(0, 2) as i:
                pair(H_DSA_QI // 2, 4, i, 0, w_in1, A_QI + i * 4 * P)
                pair(H_DSA_QI // 2, 4, i, 2, w_in1, A_QI + i * 4 * P + 2 * P)
            pair(H_DSA_KV // 2, 4, 0, 0, w_in1, A_KV)
            with sp.Fori(0, 4) as i:
                pair(H_DSA_Q // 2, 4, i, 0, w_in1, i * 4 * P)
                pair(H_DSA_Q // 2, 4, i, 2, w_in1, i * 4 * P + 2 * P)
            with sp.Fori(0, 4) as i:
                pair(H_WOUT1 // 2, 4, i, 0, w_out[1], i * 4 * P)
                pair(H_WOUT1 // 2, 4, i, 2, w_out[1], i * 4 * P + 2 * P)
            ffn(H_FFN1 // 2, 1)
            for b in range(2):
                sp.wait_ge(y_copied, 4 * (b + 1))
                sp.dma_start(out[0, b * P:(b + 1) * P, :], x_tok[:, b]).then_inc(stored, 16)
            sp.wait_ge(stored, 32)

        PAIR, UNIT, DOWN = range(3)

        def layout(n):
            if n < H_WOUT0:
                return UNIT if n % 12 < 4 else PAIR
            for base in (H_FFN0, H_FFN1):
                if base <= n < base + 24 * GROUPS and (n - base) % 24 >= 16:
                    return DOWN
            return PAIR

        def raw_half(n):
            slot, j = n // 2 % RING, n % 2
            if layout(n) == UNIT:
                return raw[:, slot].rearrange("p (j k n) -> p j k n", j=2, k=BLK)[:, j]
            return raw[:, slot].rearrange("p (k u n) -> p k u n", k=2 if layout(n) == DOWN else BLK, u=2)[:, :, j]

        def split_half(t, n):
            v = t[:, n % RING]
            return v.rearrange("p (k d) n -> p k (d n)", k=2) if layout(n) == DOWN else v

        def act_split(act, n, off):
            if n >= H_END:
                return
            load = n // 2
            act.wait_ge(load_done[load % RING], 16 * (load // RING + 1) + off * 2)
            if n >= RING:
                act.wait_ge(halves_used, n - RING + 1 + off)
            act.activation(split_half(w_hi, n), raw_half(n), ACT.Copy).then_inc(halves_hi, 1)

        def dve_split(dve, n, off):
            if n >= H_END:
                return
            dve.wait_ge(halves_hi, n + 1 + off)
            dve.tensor_tensor(split_half(w_lo, n), raw_half(n), split_half(w_hi, n).bitcast(F32), ALU.subtract).then_inc(halves_split, 1)

        @block.tensor
        def _(pe):
            def hi_lo(bank, wh, wl, mv, first, last):
                def wide():
                    return pe.matmul(ps[:, bank], wh, mv.rearrange("p a t -> p (a t)"), start=first, stop=last)

                def narrow():
                    pe.matmul(ps[:, bank, 0:T], wl, mv[:, 0], start=False, stop=False, skip_group_check=True)
                if first:
                    wide()
                    narrow()
                    return None
                narrow()
                return wide()

            def half(n, off, j, bank, mv):
                pe.wait_ge(halves_split, n + 1 + off)
                for b in range(BLK):
                    k = BLK * j + b
                    mm = hi_lo(bank, w_hi[:, n % RING, b], w_lo[:, n % RING, b], mv[:, k], k == 0, k == KT - 1)
                mm.then_inc(halves_used, 1)

            def pair(n, off, d, doff, mv, before=(None,) * 4, wait_mv=None):
                bank = 2 * (d % 2)
                if d >= 2:
                    pe.wait_ge(psum_free, d - 1 + doff)
                for c in range(4):
                    if before[c]:
                        before[c]()
                    if wait_mv:
                        wait_mv(c)
                    unit, j = (c // 2, c % 2) if layout(n) == UNIT else (c % 2, c // 2)
                    half(n + c, off, j, bank + unit, mv)

            def norm_sum(i):
                pe.wait_ge(sq_ready, i + 1)
                if i in (1, 3):
                    pe.wait_ge(psum_free, D_FFN0 if i == 1 else D_FFN1)
                pe.matmul(ps[:, 7, 0:T], ones[:, 0:P], sq_sum[:, 0], start=True, stop=True).then_inc(sq_mm, 1)

            def xs_wait(i):
                def w(c):
                    if c in (0, 2):
                        pe.wait_ge(xs_ready, 4 * i + (2 if c == 0 else 4))
                return w

            pe.wait_ge(consts, 1)
            pe.wait_ge(small_in, 96)
            pe.transpose(ps[:, 0, 0:V_ROWS], vec_rows, ident[0:V_ROWS, 0:V_ROWS])
            for l in range(2):
                for t in range(TAPS):
                    mm = pe.transpose(ps[:, 1 + l, t * UP_TILES:(t + 1) * UP_TILES], tap_rows[:, l * TAPS + t],
                                      ident[0:UP_TILES, 0:UP_TILES])
            mm.then_inc(vecs_turned, 1)
            pe.wait_ge(x_in, 16)
            pe.wait_ge(vecs_ready, 1)
            for r in range(KT // 2):
                for kk in range(2):
                    for b in range(2):
                        k = 2 * r + kk
                        mm = pe.transpose(ps[:, r, kk * T + b * P:kk * T + (b + 1) * P],
                                          x_tok[:, b, k * P:(k + 1) * P], ident[:])
                mm.then_inc(x_turned, 1)

            pe.wait_ge(x_copied, KT // 2)
            pe.wait_ge(side_split, 1)
            for k in range(KT):
                if k % 4 == 0:
                    pe.wait_ge(xs_ready, k // 4 + 1)
                mm = hi_lo(4, side_w_hi[:, k], side_w_lo[:, k], xs[:, k], k == 0, k == KT - 1)
            mm.then_inc(side_mm, 1)

            def causal(bank, c, v0, v1, s):
                pe.matmul(ps[:, bank, c:c + P], v0, s[:, 0:P], start=True, stop=True)
                pe.matmul(ps[:, bank, c + P:c + T], v0, s[:, P:T], start=True, stop=False)
                return pe.matmul(ps[:, bank, c + P:c + T], v1, s[:, T:T + P], start=False, stop=True)

            def head_scores(h):
                pe.wait_ge(rows_ready, h + 1)
                pe.wait_ge(qk_ready, h + 1)
                pe.wait_ge(v_ready, h + 1)
                pe.matmul(ps[:, 4], ones[0:M_HEADS, 0:P], head_rows, start=True, stop=True)
                pe.matmul(ps[:, 5, 0:T], QK[:, 1, 0:P], QK[:, 0], start=True, stop=True)
                pe.matmul(ps[:, 5, T:T + P], QK[:, 1, P:T], QK[:, 0, P:T], start=True, stop=True).then_inc(qk_mm, 1)

            def head_values(h):
                pe.wait_ge(s_ready, h + 1)
                for j in range(2):
                    causal(6, j * T, V[:, 0, j * P:(j + 1) * P], V[:, 1, j * P:(j + 1) * P], S)
                causal(7, 0, ones[:, 0:P], ones[:, 0:P], S).then_inc(pv_mm, 1)

            def head_square(h):
                pe.wait_ge(h_sq, h + 1)
                pe.matmul(ps[:, 7, T:2 * T], ones[:, 0:P], sq[:, 0], start=True, stop=False)
                pe.matmul(ps[:, 7, T:2 * T], ones[:, 0:P], sq[:, 1], start=False, stop=True).then_inc(h_mm, 1)

            def head_turn_v(h):
                pe.wait_ge(vT_ready, h + 1)
                for s in range(2):
                    for j in range(2):
                        mm = pe.transpose(ps[:, 4, s * DV + j * P:s * DV + (j + 1) * P],
                                          vT[:, j, s * P:(s + 1) * P], ident[:])
                mm.then_inc(v_turned, 1)

            def head(n, off, d, doff, h, prev):
                a = [None] * 12
                if prev is not None:
                    a[1] = lambda: head_scores(prev)
                    a[3] = lambda: head_values(prev)
                    a[5] = lambda: head_square(prev)
                a[10] = lambda: head_turn_v(h)
                for c in range(3):
                    pair(n + 4 * c, off, d + c, doff, xs, a[4 * c:4 * c + 4])

            def turn_a():
                pe.wait_ge(a_ready, 1)
                for b in range(2):
                    mm = pe.transpose(ps[:, 5, b * M_HEADS:(b + 1) * M_HEADS], gA[:, b * P:(b + 1) * P],
                                      ident[0:M_HEADS, 0:M_HEADS])
                mm.then_inc(a_turned, 1)

            pair(0, 0, 0, 0, xs, (lambda: norm_sum(0), None, None, None))
            pair(4, 0, 1, 0, xs)
            pair(8, 0, 2, 0, xs, (None, turn_a, lambda: head_turn_v(0), None))
            with pe.Fori(0, 3) as i:
                head(12, 24 * i, 3, 6 * i, 2 * i + 1, 2 * i)
                head(24, 24 * i, 6, 6 * i, 2 * i + 2, 2 * i + 1)
            head(84, 0, 21, 0, 7, 6)

            def out_proj(n, d, last, ready, first_before):
                def w(c):
                    if c == 2:
                        pe.wait_ge(mix_ready, last)
                    if c == 0:
                        pe.wait_ge(mix_ready, ready)
                pair(n, 0, d, 0, mix, first_before, wait_mv=w)
                pair(n + 4, 0, d + 1, 0, mix)
                with pe.Fori(0, 3) as i:
                    pair(n + 8, 8 * i, d + 2, 2 * i, mix)
                    pair(n + 12, 8 * i, d + 3, 2 * i, mix)

            out_proj(H_WOUT0, D_WOUT0, M_HEADS, M_HEADS // 2,
                     (lambda: head_scores(7), lambda: head_values(7), lambda: head_square(7), None))

            def ffn(n0, d0, norm, done):
                def first(c):
                    if c == 0:
                        pe.wait_ge(xs_ready, 4 * norm + 2)
                    if c == 1:
                        norm_sum(norm)
                    if c == 2:
                        pe.wait_ge(xs_ready, 4 * norm + 4)

                def group(n0, off, d0, doff, g, peel):
                    for q in range(4):
                        pe.wait_ge(psum_free, d0 - (1 if q == 0 else 0) + doff)
                        for c in range(4):
                            if peel and q == 0:
                                first(c)
                            half(n0 + 4 * q + c, off, c // 2, 2 * q + c % 2, xs)
                    for q in range(2):
                        for kk in range(2):
                            if q == 0:
                                pe.wait_ge(hid_ready, done + 2 * g + kk + 1)
                            for u in range(2):
                                n = n0 + 16 + 4 * q + 2 * kk + u
                                if kk == 0:
                                    pe.wait_ge(psum_free, d0 + (2, 4, 5, 6)[2 * q + u] + doff)
                                pe.wait_ge(halves_split, n + 1 + off)
                                for k2 in range(2):
                                    for dt in range(4):
                                        b = 4 * k2 + dt
                                        mm = hi_lo(4 * u + dt, w_hi[:, n % RING, b], w_lo[:, n % RING, b],
                                                   hid[:, 2 * kk + k2], kk == 0 and k2 == 0, kk == 1 and k2 == 1)
                                (mm if mm is not None else None).then_inc(halves_used, 1)

                group(n0, 0, d0, 0, 0, True)
                with pe.Fori(1, GROUPS) as g:
                    group(n0 + 24, 24 * g - 24, d0 + 8, 8 * g - 8, g, False)

            ffn(H_FFN0, D_FFN0, 1, 0)

            def kw_unit():
                norm_sum(2)
                pe.wait_ge(side_split, 2)
                pe.wait_ge(psum_free, D_DSA_QI)
                for k in range(KT):
                    mm = hi_lo(4, side_w_hi[:, k], side_w_lo[:, k], xs[:, k], k == 0, k == KT - 1)
                mm.then_inc(side_mm, 1)

            def turn_wi():
                pe.wait_ge(kw_ready, 1)
                for b in range(2):
                    mm = pe.transpose(ps[:, 7, b * I_HEADS:(b + 1) * I_HEADS], wiT[64:80, b * P:(b + 1) * P],
                                      ident[64:80, 64:80])
                mm.then_inc(wi_turned, 1)

            def scores(t):
                pe.wait_ge(qi_ready, t // 2 + 1)
                pe.wait_ge(kw_ready, 1)
                pe.wait_ge(wi_ready, 1)
                if t:
                    pe.wait_ge(relu_ready, 2 * t)
                for b in range(2):
                    w = (b + 1) * P
                    for s in range(2):
                        mm = pe.matmul(ps[:, 4 + 2 * b + s, 0:w], QI[64 * s:64 * s + 64, t, b * P:(b + 1) * P],
                                       KI[64 * s:64 * s + 64, 0:w], start=True, stop=True)
                    mm.then_inc(score_mm, 1)

            for j in range(4):
                t = 2 * (j - 1)
                if j == 0:
                    pair(H_DSA_QI, 0, D_DSA_QI, 0, xs, wait_mv=xs_wait(2))
                    kw_unit()
                else:
                    pair(H_DSA_QI + 4 * j, 0, D_DSA_QI + j, 0, xs,
                         (None, (lambda: turn_wi()) if j == 1 else None, lambda t=t: scores(t), lambda t=t: scores(t + 1)))

            def kv_sum():
                pe.wait_ge(kv_sq, 1)
                pe.matmul(ps[:, 4, 0:T], ones[:, 0:P], sq[:, 0], start=True, stop=True)
                for s in range(2):
                    mm = pe.transpose(ps[:, 4, T + s * P:T + (s + 1) * P], KV[:, 1, s * P:(s + 1) * P], ident[:])
                mm.then_inc(kv_mm, 1)

            def q_sum(p):
                pe.wait_ge(q_sq, p + 1)
                pe.matmul(ps[:, 4], ones[:, 0:P], sq[:, 0:2].rearrange("p a t -> p (a t)"), start=True, stop=True).then_inc(q_mm, 1)

            def logits(p):
                pe.wait_ge(qn_ready, p + 1)
                pe.wait_ge(kn_ready, 1)
                for a in range(2):
                    pe.matmul(ps[:, 5 + a, 0:P], QN[:, a, 0:P], KN[:, 0:P], start=True, stop=True)
                    mm = pe.matmul(ps[:, 5 + a, P:3 * P], QN[:, a, P:T], KN[:], start=True, stop=True)
                mm.then_inc(logit_mm, 1)

            def turn_probs(p):
                pe.wait_ge(probs_ready, p + 1)
                for a, bank in ((0, 7), (1, 5)):
                    for c in range(3):
                        mm = pe.transpose(ps[:, bank, c * P:(c + 1) * P], LM[:, a, c * P:(c + 1) * P], ident[:])
                mm.then_inc(probs_turned, 1)

            def values(p):
                pe.wait_ge(pt_ready, p + 1)
                pe.wait_ge(va_ready, 1)
                for a in range(2):
                    mm = causal(7, a * T, VA[:, 0], VA[:, 1], PT[:, a])
                mm.then_inc(av_mm, 1)

            pair(H_DSA_KV, 0, D_DSA_KV, 0, xs, (None, None, lambda: scores(6), lambda: scores(7)))
            pair(H_DSA_Q, 0, D_DSA_Q, 0, xs, (None, lambda: kv_sum(), None, None))
            pair(H_DSA_Q + 4, 0, D_DSA_Q + 1, 0, xs, (None, lambda: q_sum(0), None, lambda: logits(0)))

            def q_frame(n, off, d, doff, p):
                def b1():
                    q_sum(p - 1)
                    turn_probs(p - 2)
                pair(n, off, d, doff, xs, (None, b1, lambda: values(p - 2), lambda: (pe.wait_ge(pt_ready, p - 1), logits(p - 1))))

            with pe.Fori(0, 3) as i:
                q_frame(H_DSA_Q + 8, 8 * i, D_DSA_Q + 2, 2 * i, 2 * i + 2)
                q_frame(H_DSA_Q + 12, 8 * i, D_DSA_Q + 3, 2 * i, 2 * i + 3)

            out_proj(H_WOUT1, D_WOUT1, M_HEADS + 8, M_HEADS + 4,
                     (lambda: (q_sum(7), turn_probs(6)), lambda: (values(6), logits(7)),
                      lambda: (turn_probs(7), values(7)), None))
            ffn(H_FFN1, D_FFN1, 3, 2 * GROUPS)

            pe.wait_ge(psum_free, D_FFN1 + 8 * GROUPS)
            for b in range(2):
                for r in range(4):
                    bank = 4 * b + r
                    for k in range(4):
                        mm = pe.transpose(ps[:, bank, k * P:(k + 1) * P], X[:, 4 * r + k, b * P:(b + 1) * P], ident[:])
                    mm.then_inc(y_turned, 1)

        @block.scalar
        def _(act):
            def tail_copy(n, off, d, c, coff, doff, bank):
                act.wait_ge(halves_used, n + 1 + off)
                if c > 0:
                    act.wait_ge(psum_free, d + doff)
                act.activation(tail[:], ps[:, bank:bank + 2, T:2 * T], ACT.Copy).then_inc(tails, 1)

            def norm(i, g0, done, count):
                act.wait_ge(done, count)
                for r in range(4):
                    for k in range(4 * r, 4 * r + 4):
                        ins = act.activation(xs[:, k, 0], X[:, k], ACT.Copy, scale=vecs[:, g0 + k:g0 + k + 1])
                    ins.then_inc(xs_hi, 1)
                    if i or r:
                        act.wait_ge(squares_used, 4 * i + r)
                    act.activation(sq[:], X[:, 4 * r:4 * r + 4], ACT.Square).then_inc(squares, 1)

            act.dma_start(gate_raw, w_in0[:, :, M_GATE:M_GATE + 16]).then_inc(gate_in, 16)
            act.wait_ge(gate_zero, 1)
            act.dma_start(gate_b[0:8, :], mlstm_gate_b[0, 0:8].rearrange("(p a) -> p a", a=1)).then_inc(gate_in, 16)
            act.dma_start(gate_b[32:40, :], mlstm_gate_b[0, 8:16].rearrange("(p a) -> p a", a=1)).then_inc(gate_in, 16)
            for n in range(LEAD):
                act_split(act, n, 0)
            act.wait_ge(gate_in, 48)
            act.wait_ge(gate_zero, 2)
            act.activation(side_w_hi[:, :, 0:8], gate_raw[:, :, 0:8], ACT.Copy)
            act.activation(side_w_hi[:, :, 32:40], gate_raw[:, :, 8:16], ACT.Copy).then_inc(side_hi, 1)
            act.wait_ge(vecs_ready, 1)
            norm(0, V_MIXG, x_copied, KT // 2)
            act.wait_ge(side_mm, 1)
            act.activation(gate_tail, ps[0:40, 4, T:2 * T], ACT.Copy).then_inc(side_tail, 1)
            act.wait_ge(gate_dve, 1)
            act.activation(gC[:], gB[:], ACT.Exp, scale=-1.0).then_inc(act_chain, 1)
            act.wait_ge(act_chain, 1)
            act.activation(gC[:], gC[:], ACT.Ln, bias=1.0).then_inc(gate_act, 1)
            act.wait_ge(gate_dve, 2)
            act.activation(rows_m[:, T:2 * T], gB[:], ACT.Exp, scale=-1.0).then_inc(gate_act, 1)

            def og_neg_exp(h):
                act.wait_ge(og_ready, h + 1)
                act.activation(HG[:], og[:], ACT.Exp, scale=-1.0).then_inc(og_exp, 1)

            def head_weights(h):
                act.wait_ge(qk_mm, h + 1)
                act.activation(em[:], ps[:, 4, T:2 * T], ACT.Copy).then_inc(em_ready, 1)
                act.wait_ge(e_ready, h + 1)
                act.activation(E[:], E[:], ACT.Exp).then_inc(w_ready, 1)

            def head_squares(h):
                act.wait_ge(h_ready, h + 1)
                act.activation(sq[:, 0:2], H[:], ACT.Square).then_inc(h_sq, 1)

            def head_hi(h):
                act.wait_ge(hg_ready, h + 1)
                act.activation(mix[:, bass.ds(2 * h, 2), 0], HG[:], ACT.Copy).then_inc(mix_hi, 1)

            def head_v(h):
                act.wait_ge(v_turned, h + 1)
                act.activation(V[:].rearrange("p a b -> p (a b)"), ps[:, 4], ACT.Copy).then_inc(v_ready, 1)

            def head(n, off, c, coff, h, prev):
                bank0 = c % 2
                for k in range(12):
                    act_split(act, n + k + LEAD, off)
                    if prev is not None:
                        if k == 0:
                            og_neg_exp(prev)
                        if k == 1:
                            head_weights(prev)
                        if k == 3:
                            head_squares(prev)
                    if k % 4 == 3:
                        j = k // 4
                        tail_copy(n + k, off, c + j, c + j, coff, coff, 2 * ((c + j) % 2))
                    if prev is not None and k == 6:
                        head_hi(prev)
                    if k == 10:
                        head_v(h)

            head(0, 0, 0, 0, 0, None)
            with act.Fori(0, 3) as i:
                head(12, 24 * i, 3, 6 * i, 2 * i + 1, 2 * i)
                head(24, 24 * i, 6, 6 * i, 2 * i + 2, 2 * i + 1)
            head(84, 0, 21, 0, 7, 6)

            def out_proj(n, pre):
                for k in range(8):
                    for f in pre.get(k, ()):
                        f()
                    act_split(act, n + k + LEAD, 0)
                with act.Fori(0, 3) as i:
                    for k in range(8):
                        act_split(act, n + 8 + k + LEAD, 8 * i)

            out_proj(H_WOUT0, {0: (lambda: og_neg_exp(7), lambda: head_weights(7), lambda: head_squares(7),
                                   lambda: head_hi(7))})

            def ffn(n0, d0, c0, l, done, norm_i, last):
                norm(norm_i, V_FFNG + KT * l, psum_free, d0)

                def tap2(dst, tile0, count):
                    act.wait_ge(up_ready, count + 1)
                    for j in range(2):
                        ins = act.activation(dst[:, j], pads[:, j, TAPS - 1:], ACT.Copy,
                                             scale=taps[:, l, 2, bass.ds(tile0 + j, 1)])
                    ins.then_inc(tap2_ready, 1)

                def group(n0, off, d0, doff, c0, coff, g):
                    ups = 2 * done + 4 * g
                    for k in range(24):
                        act_split(act, n0 + k + LEAD, off)
                        if k < 16 and k % 4 == 3:
                            q = k // 4
                            tail_copy(n0 + k, off, d0 + q, c0 + q, coff, doff, 2 * q)
                        if k < 17 and k % 4 == 0 and k:
                            q = k // 4 - 1
                            ab, half_q = q % 2, q // 2
                            tap2((CA, CB)[ab], ab * (UP_TILES // 2) + g * GROUP + 2 * half_q, ups + q)
                        if k in (5, 13):
                            act.wait_ge(conv_a, done + 2 * g + k // 8 + 1)
                            act.activation(SA[:], CA[:], ACT.Silu).then_inc(silu_ready, 1)
                        if k in (9, 17):
                            q = k // 16
                            act.wait_ge(gated, done + 2 * g + q + 1)
                            if q == 0:
                                act.wait_ge(halves_used, n0 + off)
                            act.activation(hid[:, 2 * q:2 * q + 2, 0], G[:], ACT.Copy).then_inc(hid_hi, 1)

                n = GROUPS - 1 if last else GROUPS
                with act.Fori(0, n) as g:
                    group(n0, 24 * g, d0, 8 * g, c0, 4 * g, g)
                if last:
                    group(n0 + 24 * n, 0, d0 + 8 * n, 0, c0 + 4 * n, 0, n)

            ffn(H_FFN0, D_FFN0, C_FFN0, 0, 0, 1, False)

            norm(2, V_MIXG + KT, psum_free, D_DSA_QI)
            act.wait_ge(kw_in, 16)
            act.activation(side_w_hi[:, :, 0:80], kw_raw, ACT.Copy)
            act.activation(side_w_hi[:, :, 80:P], kw_raw[:, :, 0:48], ACT.Copy).then_inc(side_hi, 1)

            def kw_tail():
                act.wait_ge(side_mm, 2)
                act.activation(KI[0:80], ps[0:80, 4, T:2 * T], ACT.Copy).then_inc(side_tail, 1)

            def wi_copy():
                act.wait_ge(wi_turned, 1)
                act.activation(WI[:].rearrange("p a b -> p (a b)"), ps[:, 7, 0:2 * I_HEADS], ACT.Copy,
                               scale=float((I_HEADS * I_DIM) ** -0.5)).then_inc(wi_ready, 1)

            def relus(t):
                for b in range(2):
                    act.wait_ge(score_mm, 2 * t + b + 1)
                    if 2 * t + b:
                        act.wait_ge(relu_used, 2 * t + b)
                    w = (b + 1) * P
                    act.activation(relu[:, :, 0:w], ps[:, 4 + 2 * b:6 + 2 * b, 0:w], ACT.Relu).then_inc(relu_ready, 1)

            for j in range(5):
                n = H_DSA_QI + 4 * j
                for k in range(4):
                    act_split(act, n + k + LEAD, 0)
                    if j == 1 and k == 0:
                        kw_tail()
                    if j == 1 and k == 1:
                        wi_copy()
                    if j and k in (2, 3):
                        relus(2 * (j - 1) + k - 2)
                    if k == 3:
                        tail_copy(n + 3, 0, D_DSA_QI + j, C_DSA_QI + j, 0, 0, 2 * (j % 2))
            act.wait_ge(kv_ready, 1)
            act.activation(sq[:, 0], KV[:, 0], ACT.Square).then_inc(kv_sq, 1)

            def va_copy():
                act.wait_ge(kv_mm, 1)
                act.activation(VA[:].rearrange("p a b -> p (a b)"), ps[:, 4, T:2 * T], ACT.Copy).then_inc(va_ready, 1)

            def q_squares(p):
                act.wait_ge(q_ready, p + 1)
                act.activation(sq[:, 0:2], QT[:], ACT.Square).then_inc(q_sq, 1)

            def exps(p):
                act.wait_ge(max_ready, p + 1)
                for a in range(2):
                    for b in range(2):
                        c = slice(0, P) if b == 0 else slice(P, 3 * P)
                        ins = act.activation(LM[:, a, c], LM[:, a, c], ACT.Exp, bias=mx[:, a, b:b + 1],
                                             accum_out=sums[:, a, b:b + 1])
                ins.then_inc(exp_ready, 1)

            def probs(p):
                act.wait_ge(inv_ready, p + 1)
                for a in range(2):
                    for b in range(2):
                        c = slice(0, P) if b == 0 else slice(P, 3 * P)
                        ins = act.activation(LM[:, a, c], LM[:, a, c], ACT.Copy, scale=sums[:, a, b:b + 1])
                ins.then_inc(probs_ready, 1)

            def pt_copy(p):
                act.wait_ge(probs_turned, p + 1)
                act.activation(PT[:, 0], ps[:, 7, 0:3 * P], ACT.Copy)
                act.activation(PT[:, 1], ps[:, 5, 0:3 * P], ACT.Copy).then_inc(pt_ready, 1)

            def av_hi(p):
                act.wait_ge(av_mm, p + 1)
                act.activation(mix[:, bass.ds(2 * p, 2), 0], ps[:, 7].rearrange("p (a t) -> p a t", a=2),
                               ACT.Copy).then_inc(mix_hi, 1)

            def q_frame(n, off, d, c, doff, p, one, two):
                for k in range(4):
                    if two and k == 0:
                        probs(p - 2)
                    act_split(act, n + k + LEAD, off)
                    if two and k == 1:
                        pt_copy(p - 2)
                    if two and k == 2:
                        av_hi(p - 2)
                    if one and k == 3:
                        exps(p - 1)
                    if k == 3:
                        tail_copy(n + 3, off, d, c, doff, doff, 2 * (d % 2))
                        q_squares(p)

            for k in range(4):
                act_split(act, H_DSA_Q + k + LEAD, 0)
                if k == 1:
                    va_copy()
                if k == 3:
                    tail_copy(H_DSA_Q + 3, 0, D_DSA_Q, C_DSA_Q, 0, 0, 2 * (D_DSA_Q % 2))
                    q_squares(0)
            q_frame(H_DSA_Q + 4, 0, D_DSA_Q + 1, C_DSA_Q + 1, 0, 1, True, False)
            with act.Fori(0, 3) as i:
                q_frame(H_DSA_Q + 8, 8 * i, D_DSA_Q + 2, C_DSA_Q + 2, 2 * i, 2 * i + 2, True, True)
                q_frame(H_DSA_Q + 12, 8 * i, D_DSA_Q + 3, C_DSA_Q + 3, 2 * i, 2 * i + 3, True, True)

            out_proj(H_WOUT1, {0: (lambda: probs(6), lambda: pt_copy(6), lambda: av_hi(6), lambda: exps(7),
                                   lambda: probs(7), lambda: pt_copy(7), lambda: av_hi(7))})
            ffn(H_FFN1, D_FFN1, C_FFN1, 1, 2 * GROUPS, 3, True)

        @block.vector
        def _(dve):
            class Own:
                n = 0
                off = 0
            own = Own()

            def link(ins):
                own.n += 1
                ins.then_inc(chain, 1)
                dve.wait_ge(chain, own.n + own.off)

            def loop(count, per, body, start=0):
                at = own.n
                with dve.Fori(start, start + count) as i:
                    own.off = per * (i - start)
                    body(i)
                assert own.n - at == per, (own.n - at, per)
                own.n = at + per * count
                own.off = 0

            def drain(c, coff, bank):
                dve.wait_ge(tails, c + 1 + coff)
                ins = dve.tensor_tensor(both[:], ps[:, bank:bank + 2, 0:T], tail[:], ALU.add)
                ins.then_inc(psum_free, 1)
                return ins

            def scaled(dst, free_count):
                dve.wait_ge(psum_free, free_count)
                return dve.tensor_tensor(dst, both[:], rms_scale[:].rearrange("p (a t) -> p a t", a=1).broadcast_to([P, 2, T]), ALU.mult)

            def norm(i, g0):
                for r in range(4):
                    dve.wait_ge(xs_hi, 4 * i + r + 1)
                    for k in range(4 * r, 4 * r + 4):
                        ins = dve.scalar_tensor_tensor(xs[:, k, 1], X[:, k], vecs[:, g0 + k:g0 + k + 1],
                                                       xs[:, k, 0].bitcast(F32), ALU.mult, ALU.subtract)
                    ins.then_inc(xs_ready, 1)
                    dve.wait_ge(squares, 4 * i + r + 1)
                    if r == 0:
                        ins = dve.tensor_copy(sq_sum[:], sq[:])
                    else:
                        ins = dve.tensor_tensor(sq_sum[:], sq_sum[:], sq[:], ALU.add)
                    ins.then_inc(squares_used, 1)
                    dve.wait_ge(squares_used, 4 * i + r + 1)
                link(dve.tensor_tensor(sq_sum[:, 0:2], sq_sum[:, 0:2], sq_sum[:, 2:4], ALU.add))
                dve.tensor_tensor(sq_sum[:, 0], sq_sum[:, 0], sq_sum[:, 1], ALU.add).then_inc(sq_ready, 1)

            def norm_var(i):
                dve.wait_ge(sq_mm, i + 1)
                dve.tensor_scalar(var_x[:], ps[:, 7, 0:T], 1.0 / D, EPS, ALU.mult, ALU.add).then_inc(var_ready, 1)

            for n in range(LEAD):
                dve_split(dve, n, 0)
            dve.wait_ge(vecs_turned, 1)
            dve.tensor_copy(vecs[:], ps[:, 0, 0:V_ROWS])
            for l in range(2):
                ins = dve.tensor_copy(taps[:, l].rearrange("p a b -> p (a b)"), ps[:, 1 + l, 0:TAPS * UP_TILES])
            ins.then_inc(vecs_ready, 1)
            dve.wait_ge(vecs_ready, 1)
            dve.memset(pads[:, :, 0:TAPS - 1], 0.0)
            for r in range(KT // 2):
                dve.wait_ge(x_turned, r + 1)
                dve.tensor_copy(X[:, 2 * r:2 * r + 2].rearrange("p a t -> p (a t)"), ps[:, r]).then_inc(x_copied, 1)
            dve.wait_ge(x_copied, KT // 2)
            dve.wait_ge(side_hi, 1)
            dve.tensor_tensor(side_w_lo[:, :, 0:8], gate_raw[:, :, 0:8], side_w_hi[:, :, 0:8].bitcast(F32), ALU.subtract)
            dve.tensor_tensor(side_w_lo[:, :, 32:40], gate_raw[:, :, 8:16], side_w_hi[:, :, 32:40].bitcast(F32),
                              ALU.subtract).then_inc(side_split, 1)
            norm(0, V_MIXG)
            norm_var(0)
            dve.wait_ge(side_tail, 1)
            link(dve.tensor_tensor(gates[:], ps[0:40, 4, 0:T], gate_tail, ALU.add))
            dve.wait_ge(scale_ready, 1)
            link(dve.tensor_tensor(gates[:], gates[:], rms_scale[0:40], ALU.mult))
            link(dve.tensor_scalar(gates[:], gates[:], gate_b[:, 0:1], None, ALU.add))
            link(dve.tensor_scalar(gA[:], gates[32:40], -1.0, None, ALU.mult))
            link(dve.tensor_copy(gF[:], gates[32:40]))
            dve.tensor_tensor(gB[:], gF[:], gA[:], ALU.max).then_inc(gate_dve, 1)
            dve.wait_ge(gate_act, 1)
            link(dve.scalar_tensor_tensor(gB[:], gF[:], 0.0, gC[:], ALU.min, ALU.subtract))
            link(dve.tensor_tensor_scan(gF[:], ones[0:M_HEADS], gB[:], 0.0, ALU.mult, ALU.add))
            dve.tensor_tensor(gA[:], gates[0:8], gF[:], ALU.subtract).then_inc(a_ready, 1)
            dve.wait_ge(a_ready, 1)
            link(dve.tensor_tensor_scan(gC[:], ones[0:M_HEADS], gA[:], 0.0, ALU.mult, ALU.max))
            dve.tensor_scalar(rows_m[:, 0:T], gC[:], -1.0, None, ALU.mult)
            dve.tensor_tensor(gB[:], gF[:], gC[:], ALU.add).then_inc(gate_dve, 1)
            dve.wait_ge(gate_act, 2)
            link(dve.tensor_scalar(rows_m[:, T:2 * T], rows_m[:, T:2 * T], 1e37, None, ALU.min))

            def head_rows_pick(h):
                if not isinstance(h, int) or h > 0:
                    dve.wait_ge(qk_mm, h)
                dve.tensor_scalar(head_rows[:], rows_m[:], ident[0:M_HEADS, bass.ds(h, 1)], None,
                                  ALU.mult).then_inc(rows_ready, 1)

            def head_exponent(h):
                dve.wait_ge(em_ready, h + 1)
                dve.scalar_tensor_tensor(E[:, 0:T], ps[:, 4, 0:T], a_tok[:, 0, bass.ds(h, 1)], neg_future[:],
                                         ALU.add, ALU.add)
                dve.scalar_tensor_tensor(E[:, T:T + P], ps[:, 4, P:T], a_tok[:, 1, bass.ds(h, 1)],
                                         neg_future[:, 0:P], ALU.add, ALU.add).then_inc(e_ready, 1)

            def head_s(h):
                dve.wait_ge(w_ready, h + 1)
                dve.scalar_tensor_tensor(S[:], ps[:, 5, 0:3 * P], float(DK ** -0.5), E[:], ALU.mult,
                                         ALU.mult).then_inc(s_ready, 1)

            def head_o(h):
                dve.wait_ge(og_exp, h + 1)
                link(dve.tensor_scalar(og[:], HG[:], 1.0, None, ALU.add))
                link(dve.reciprocal(og[:], og[:]))

            def head_h(h):
                dve.wait_ge(pv_mm, h + 1)
                link(dve.scalar_tensor_tensor(den[:], ps[:, 7, 0:T], -1.0, em[:], ALU.mult, ALU.max))
                link(dve.tensor_tensor(den[:], ps[:, 7, 0:T], den[:], ALU.max))
                link(dve.reciprocal(den[:], den[:]))
                dve.tensor_tensor(H[:], ps[:, 6].rearrange("p (a t) -> p a t", a=2),
                                  den[:].rearrange("p (a t) -> p a t", a=1).broadcast_to([P, 2, T]),
                                  ALU.mult).then_inc(h_ready, 1)

            def head_var(h):
                dve.wait_ge(h_mm, h + 1)
                dve.tensor_scalar(var[:], ps[:, 7, T:2 * T], 1.0 / DV, EPS, ALU.mult, ALU.add).then_inc(h_var, 1)

            def head_gate(h):
                dve.wait_ge(h_ready, h + 1)
                for j in range(2):
                    g = vecs[:, bass.ds(V_HEADG + 2 * h + j, 1)]
                    ins = dve.scalar_tensor_tensor(HG[:, j], H[:, j], g, og[:, j], ALU.mult, ALU.mult)
                link(ins)
                dve.wait_ge(h_scale, h + 1)
                dve.tensor_tensor(HG[:], HG[:], rh[:].rearrange("p (a t) -> p a t", a=1).broadcast_to([P, 2, T]),
                                  ALU.mult).then_inc(hg_ready, 1)

            def head_lo(h):
                dve.wait_ge(mix_hi, h + 1)
                dve.tensor_tensor(mix[:, bass.ds(2 * h, 2), 1], HG[:], mix[:, bass.ds(2 * h, 2), 0].bitcast(F32),
                                  ALU.subtract).then_inc(mix_ready, 1)

            def head(n, off, c, coff, h, prev):
                for k in range(12):
                    dve_split(dve, n + k + LEAD, off)
                    if prev is not None:
                        if k == 0:
                            head_rows_pick(prev)
                        if k == 1:
                            head_exponent(prev)
                        if k == 2:
                            head_s(prev)
                            head_o(prev)
                        if k == 3:
                            head_h(prev)
                        if k == 5:
                            head_var(prev)
                        if k == 6:
                            head_gate(prev)
                        if k == 7:
                            head_lo(prev)
                    if k % 4 == 3:
                        j = k // 4
                        if prev is None and j == 0:
                            dve.wait_ge(scale_ready, 1)
                        drain(c + j, coff, 2 * ((c + j) % 2))
                        ins = scaled((QK, vT, og)[j], c + j + 1 + coff)
                        ins.then_inc((qk_ready, vT_ready, og_ready)[j], 1)
                    if prev is None and k == 9:
                        dve.wait_ge(a_turned, 1)
                        link(dve.tensor_copy(a_tok[:].rearrange("p a b -> p (a b)"), ps[:, 5, 0:2 * M_HEADS]))

            head(0, 0, 0, 0, 0, None)

            def two_heads(i):
                head(12, 24 * i, 3, 6 * i, 2 * i + 1, 2 * i)
                head(24, 24 * i, 6, 6 * i, 2 * i + 2, 2 * i + 1)
            loop(3, 2 * 6, two_heads)
            head(84, 0, 21, 0, 7, 6)

            def out_proj(n, d, pre):
                def one(nn, off, dd, doff, tile):
                    b = 2 * (dd % 2)
                    dve.wait_ge(halves_used, nn + 4 + off)
                    xt = X[:, bass.ds(tile, 2)]
                    link(dve.tensor_tensor(xt, ps[:, b:b + 2, 0:T], xt, ALU.add))
                    ins = dve.tensor_tensor(xt, ps[:, b:b + 2, T:2 * T], xt, ALU.add)
                    ins.then_inc(psum_free, 1)
                for j in range(2):
                    for k in range(4):
                        for f in pre.get(4 * j + k, ()):
                            f()
                        dve_split(dve, n + 4 * j + k + LEAD, 0)
                    one(n + 4 * j, 0, d + j, 0, 2 * j)

                def body(i):
                    for j in range(2):
                        for k in range(4):
                            dve_split(dve, n + 8 + 4 * j + k + LEAD, 8 * i)
                        one(n + 8 + 4 * j, 8 * i, d + 2 + j, 2 * i, 4 + 4 * i + 2 * j)
                loop(3, 2, body)

            out_proj(H_WOUT0, D_WOUT0, {0: (lambda: head_rows_pick(7), lambda: head_exponent(7), lambda: head_s(7),
                                            lambda: head_o(7), lambda: head_h(7), lambda: head_var(7),
                                            lambda: head_gate(7), lambda: head_lo(7))})

            def ffn(n0, d0, c0, l, done, norm_i, last):
                dve.wait_ge(psum_free, d0)
                norm(norm_i, V_FFNG + KT * l)
                norm_var(norm_i)
                dve.wait_ge(scale_ready, norm_i + 1)

                def conv(dst, tile0, count, signal):
                    dve.wait_ge(tap2_ready, count + 1)
                    for tap in (1, 0):
                        for j in range(2):
                            ins = dve.scalar_tensor_tensor(dst[:, j], pads[:, j, tap:tap + T],
                                                           taps[:, l, tap, bass.ds(tile0 + j, 1)], dst[:, j],
                                                           ALU.mult, ALU.add)
                            if tap == 0 and j == 1 and signal is not None:
                                ins.then_inc(signal, 1)
                            elif j == 1:
                                link(ins)

                def group(n0, off, d0, doff, c0, coff, g):
                    ups = 2 * done + 4 * g
                    for k in range(24):
                        dve_split(dve, n0 + k + LEAD, off)
                        if k < 16 and k % 4 == 3:
                            q = k // 4
                            drain(c0 + q, coff, 2 * q)
                            scaled(pads[:, :, TAPS - 1:], d0 + q + 1 + doff).then_inc(up_ready, 1)
                        if k < 17 and k % 4 == 0 and k:
                            q = k // 4 - 1
                            ab, hq = q % 2, q // 2
                            conv((CA, CB)[ab], ab * (UP_TILES // 2) + g * GROUP + 2 * hq, ups + q,
                                 conv_a if ab == 0 else None)
                            if ab == 1:
                                dve.wait_ge(silu_ready, done + 2 * g + hq + 1)
                                dve.tensor_tensor(G[:], SA[:], CB[:], ALU.mult).then_inc(gated, 1)
                        if k in (9, 17):
                            q = k // 16
                            dve.wait_ge(hid_hi, done + 2 * g + q + 1)
                            dve.tensor_tensor(hid[:, 2 * q:2 * q + 2, 1], G[:], hid[:, 2 * q:2 * q + 2, 0].bitcast(F32),
                                              ALU.subtract).then_inc(hid_ready, 1)
                        if k in (18, 19, 22, 23):
                            u = {18: 0, 19: 1, 22: 2, 23: 3}[k]
                            dve.wait_ge(halves_used, n0 + k + 1 + off)
                            b = 4 * (u % 2)
                            xt = X[:, 4 * u:4 * u + 4]
                            link(dve.tensor_tensor(xt, ps[:, b:b + 4, 0:T], xt, ALU.add))
                            dve.tensor_tensor(xt, ps[:, b:b + 4, T:2 * T], xt, ALU.add).then_inc(psum_free, 1)

                n = GROUPS - 1 if last else GROUPS
                loop(n, 10, lambda g: group(n0, 24 * g, d0, 8 * g, c0, 4 * g, g))
                if last:
                    group(n0 + 24 * n, 0, d0 + 8 * n, 0, c0 + 4 * n, 0, n)

            ffn(H_FFN0, D_FFN0, C_FFN0, 0, 0, 1, False)

            dve.wait_ge(psum_free, D_DSA_QI)
            norm(2, V_MIXG + KT)
            dve.wait_ge(side_hi, 2)
            dve.tensor_tensor(side_w_lo[:, :, 0:80], kw_raw, side_w_hi[:, :, 0:80].bitcast(F32), ALU.subtract)
            dve.tensor_tensor(side_w_lo[:, :, 80:P], kw_raw[:, :, 0:48], side_w_hi[:, :, 80:P].bitcast(F32),
                              ALU.subtract).then_inc(side_split, 1)
            dve.tensor_scalar(qg[:], vecs[:, V_QG:V_QG + 1], float(DH ** -0.5), None, ALU.mult).then_inc(qg_ready, 1)

            def kw_drain():
                dve.wait_ge(side_tail, 2)
                link(dve.tensor_tensor(wiT[0:80], ps[0:80, 4, 0:T], KI[0:80], ALU.add))
                link(dve.tensor_tensor(wiT[0:80], wiT[0:80], rms_scale[0:80], ALU.mult))
                dve.tensor_copy(KI[0:64], wiT[0:64])
                dve.tensor_copy(KI[64:128], wiT[0:64]).then_inc(kw_ready, 1)

            def accumulate(t):
                for b in range(2):
                    w = (b + 1) * P
                    sc = score[:, 0:P] if b == 0 else score[:, P:3 * P]
                    dve.wait_ge(relu_ready, 2 * t + b + 1)
                    for s in range(2):
                        r = relu[:, s, 0:w]
                        wi = WI[:, b, 2 * t + s:2 * t + s + 1]
                        if t == 0 and s == 0:
                            ins = dve.tensor_scalar(sc, r, wi, None, ALU.mult)
                        else:
                            ins = dve.scalar_tensor_tensor(sc, r, wi, sc, ALU.mult, ALU.add)
                        if s == 0:
                            link(ins)
                    ins.then_inc(relu_used, 1)
                    dve.wait_ge(relu_used, 2 * t + b + 1)

            blocks = (slice(0, P), slice(P, 3 * P))

            def topk_round(r):
                for b in range(2):
                    src = score if r == 0 else work
                    link(dve.max(best[:, b], src[:, blocks[b]]))
                    link(dve.match_replace(out=work[:, blocks[b]], in_to_replace=best[:, b], in_values=src[:, blocks[b]],
                                           imm_value=3 * NEG))

            for j in range(5):
                n = H_DSA_QI + 4 * j
                for k in range(4):
                    dve_split(dve, n + k + LEAD, 0)
                    if j == 1 and k == 0:
                        kw_drain()
                    if j == 1 and k == 1:
                        dve.wait_ge(wi_ready, 1)
                    if j and k in (2, 3):
                        accumulate(2 * (j - 1) + k - 2)
                    if k == 3:
                        if j == 0:
                            norm_var(2)
                            dve.wait_ge(scale_ready, 3)
                        drain(C_DSA_QI + j, 0, 2 * (j % 2))
                        ins = scaled(QI[:, 2 * j:2 * j + 2] if j < 4 else KV, D_DSA_QI + j + 1)
                        ins.then_inc(qi_ready if j < 4 else kv_ready, 1)
            link(dve.tensor_tensor(score[:], score[:], mask_q[:], ALU.add))

            def kv_norm():
                dve.wait_ge(va_ready, 1)
                dve.tensor_scalar(var_k[:], ps[:, 4, 0:T], 1.0 / DH, EPS, ALU.mult, ALU.add).then_inc(kv_var, 1)
                dve.wait_ge(kv_scale, 1)
                dve.wait_ge(kv_ready, 1)
                dve.scalar_tensor_tensor(KN[:], KV[:, 0], vecs[:, V_KG:V_KG + 1], rk[:], ALU.mult,
                                         ALU.mult).then_inc(kn_ready, 1)

            def select_mask():
                link(dve.tensor_scalar(work[:], work[:], 2 * NEG, NEG, ALU.is_gt, ALU.mult))
                link(dve.tensor_tensor(score[:], work[:], mask_q[:], ALU.add))

            def q_var_(p):
                dve.wait_ge(q_mm, p + 1)
                dve.tensor_scalar(var2[:], ps[:, 4].rearrange("p (a t) -> p a t", a=2), 1.0 / DH, EPS, ALU.mult,
                                  ALU.add).then_inc(q_var, 1)

            def q_norm(p):
                dve.wait_ge(q_scale, p + 1)
                dve.wait_ge(qg_ready, 1)
                dve.scalar_tensor_tensor(QN[:], QT[:], qg[:, 0:1], rq[:], ALU.mult, ALU.mult).then_inc(qn_ready, 1)

            def softmax_in(p):
                dve.wait_ge(logit_mm, p + 1)
                link(dve.tensor_tensor(LM[:], ps[:, 5:7, 0:3 * P],
                                       score[:].rearrange("p (a t) -> p a t", a=1).broadcast_to([P, 2, 3 * P]), ALU.add))
                for b in range(2):
                    ins = dve.tensor_reduce(mx[:, :, b], LM[:, :, blocks[b]], AX.X, ALU.max)
                link(ins)
                dve.tensor_scalar(mx[:], mx[:], -1.0, None, ALU.mult).then_inc(max_ready, 1)

            def inverse(p):
                dve.wait_ge(exp_ready, p + 1)
                dve.reciprocal(sums[:], sums[:]).then_inc(inv_ready, 1)

            def av_lo(p):
                dve.wait_ge(mix_hi, M_HEADS + p + 1)
                dve.tensor_tensor(mix[:, bass.ds(2 * p, 2), 1], ps[:, 7].rearrange("p (a t) -> p a t", a=2),
                                  mix[:, bass.ds(2 * p, 2), 0].bitcast(F32), ALU.subtract).then_inc(mix_ready, 1)

            def q_frame(n, off, d, c, doff, p, one, two, extra=None):
                for k in range(4):
                    if two and k == 0:
                        inverse(p - 2)
                    dve_split(dve, n + k + LEAD, off)
                    if extra:
                        extra(k)
                    if one and k == 1:
                        q_var_(p - 1)
                    if one and k == 2:
                        q_norm(p - 1)
                    if two and k == 2:
                        av_lo(p - 2)
                    if one and k == 3:
                        softmax_in(p - 1)
                    if k == 3:
                        drain(c, doff, 2 * (d % 2))
                        scaled(QT[:], d + 1 + doff).then_inc(q_ready, 1)

            def frame0(k):
                if k == 1:
                    kv_norm()
                topk_round(2 * k)
                topk_round(2 * k + 1)

            q_frame(H_DSA_Q, 0, D_DSA_Q, C_DSA_Q, 0, 0, False, False, frame0)
            select_mask()
            q_frame(H_DSA_Q + 4, 0, D_DSA_Q + 1, C_DSA_Q + 1, 0, 1, True, False)

            def two_pairs(i):
                q_frame(H_DSA_Q + 8, 8 * i, D_DSA_Q + 2, C_DSA_Q + 2, 2 * i, 2 * i + 2, True, True)
                q_frame(H_DSA_Q + 12, 8 * i, D_DSA_Q + 3, C_DSA_Q + 3, 2 * i, 2 * i + 3, True, True)
            loop(3, 4, two_pairs)

            out_proj(H_WOUT1, D_WOUT1, {0: (lambda: inverse(6), lambda: q_var_(7), lambda: q_norm(7),
                                            lambda: av_lo(6), lambda: softmax_in(7), lambda: inverse(7),
                                            lambda: av_lo(7))})
            ffn(H_FFN1, D_FFN1, C_FFN1, 1, 2 * GROUPS, 3, True)
            for b in range(2):
                for r in range(4):
                    dve.wait_ge(y_turned, 4 * b + r + 1)
                    dve.tensor_copy(x_tok[:, b, 512 * r:512 * (r + 1)], ps[:, 4 * b + r]).then_inc(y_copied, 1)

        @block.gpsimd
        def _(pool):
            pool.dma_start(x_tok, x[0].rearrange("(b p) d -> p b d", p=P)).then_inc(x_in, 16)
            for at, src in ((V_MIXG, mix_norm_g), (V_FFNG, ffn_norm_g), (V_HEADG, mlstm_head_g), (V_QG, dsa_q_g),
                            (V_KG, dsa_k_g)):
                rows = src.shape[0] * src.shape[1] // P
                pool.dma_start(vec_rows[at:at + rows], src.rearrange("l (k p) -> (l k) p", p=P)).then_inc(small_in, 16)
            pool.dma_start(tap_rows, ffn_dw_w.rearrange("l t (j p) -> j (l t) p", p=P)).then_inc(small_in, 16)

            pool.memset(ident[:], 0.0).then_inc(consts_zero, 1)
            pool.memset(neg_future[:], 0.0).then_inc(consts_zero, 1)
            pool.memset(mask_q[:], 0.0).then_inc(consts_zero, 1)
            pool.memset(ones[:], 1.0)
            pool.memset(power[:], -0.5)
            pool.memset(gate_b[:], 0.0).then_inc(gate_zero, 1)
            pool.memset(side_w_hi.bitcast(F32), 0.0)
            pool.memset(side_w_lo.bitcast(F32), 0.0).then_inc(gate_zero, 1)
            pool.wait_ge(consts_zero, 3)
            pool.affine_select(out=ident[:], in_=ident[:], compare_op=ALU.not_equal, fill=1.0, base=0,
                               pattern=[[-1, P]], channel_multiplier=1)
            pool.affine_select(out=neg_future[:], in_=neg_future[:], compare_op=ALU.is_ge, fill=NEG, base=0,
                               pattern=[[1, T]], channel_multiplier=-1)
            for c in (0, 2 * P):
                ins = pool.affine_select(out=mask_q[:, c:c + P], in_=mask_q[:, c:c + P], compare_op=ALU.is_ge, fill=NEG,
                                         base=0, pattern=[[-1, P]], channel_multiplier=1)
            ins.then_inc(consts, 1)

            def inverse_root(dst, src, wait, count, signal):
                pool.wait_ge(wait, count)
                w = power[:, 0:T] if len(src.shape) == 2 else power[:].rearrange("p (a t) -> p a t", a=2)
                pool.tensor_tensor(dst, src, w, ALU.pow).then_inc(signal, 1)

            inverse_root(rms_scale[:], var_x[:], var_ready, 1, scale_ready)
            with pool.Fori(0, M_HEADS) as h:
                inverse_root(rh, var, h_var, h + 1, h_scale)
            inverse_root(rms_scale[:], var_x[:], var_ready, 2, scale_ready)
            pool.dma_start(kw_raw, w_in1[:, :, A_KW:A_KW + 80]).then_inc(kw_in, 16)
            inverse_root(rms_scale[:], var_x[:], var_ready, 3, scale_ready)
            inverse_root(rk, var_k, kv_var, 1, kv_scale)
            with pool.Fori(0, A_HEADS // 2) as p:
                inverse_root(rq, var2, q_var, p + 1, q_scale)
            inverse_root(rms_scale[:], var_x[:], var_ready, 4, scale_ready)


_INS = ["x", "mix_norm_g", "ffn_norm_g", "mlstm_w_in", "mlstm_gate_b", "mlstm_head_g", "mlstm_w_out", "dsa_w_in",
        "dsa_q_g", "dsa_k_g", "dsa_w_out", "ffn_w_up", "ffn_dw_w", "ffn_w_down"]


def kernel(**inputs):
    import concourse.bacc as bacc
    from concourse.bass_utils import run_bass_kernel_spmd

    nc = bacc.Bacc("TRN2", target_bir_lowering=False, num_devices=1)
    arrays, args = {}, []
    for name in _INS:
        a = np.ascontiguousarray(inputs[name])
        arrays[f"in_{name}"] = a
        args.append(nc.dram_tensor(f"in_{name}", a.shape, mybir.dt.from_np(a.dtype), kind="ExternalInput").ap())
    y = nc.dram_tensor("out_y", (1, T, D), F32, kind="ExternalOutput").ap()
    trunk(nc, *args, y)
    r = run_bass_kernel_spmd(nc, [arrays], core_ids=[0])
    return r.results[0]["out_y"]
```

```python
from contextlib import ExitStack

import numpy as np

import concourse.bass as bass
from concourse import mybir

F32 = mybir.dt.float32
F32R = mybir.dt.float32r
ALU = mybir.AluOpType
ACT = mybir.ActivationFunctionType
AX = mybir.AxisListType

P = 128
T = 256
D = 2048
KT = D // P
EPS = 1e-6
M_HEADS, DK, DV = 8, 128, 256
A_HEADS, DH = 16, 128
I_HEADS, I_DIM = 16, 64
TOPK = T // 4
D_FF = 5632
UP_TILES = 2 * D_FF // P
GROUP = 4
GROUPS = D_FF // P // GROUP
TAPS = 3
NEG = -1e30

BLK = 8
LEAD = 3
RING = 4

H_MLSTM = 0
H_WOUT0 = H_MLSTM + 12 * M_HEADS
H_FFN0 = H_WOUT0 + 2 * KT
H_DSA_QI = H_FFN0 + 24 * GROUPS
H_DSA_KV = H_DSA_QI + 16
H_DSA_Q = H_DSA_KV + 4
H_WOUT1 = H_DSA_Q + 2 * A_HEADS
H_FFN1 = H_WOUT1 + 2 * KT
H_END = H_FFN1 + 24 * GROUPS

D_MLSTM = 0
D_WOUT0 = D_MLSTM + 3 * M_HEADS
D_FFN0 = D_WOUT0 + KT // 2
D_DSA_QI = D_FFN0 + 8 * GROUPS
D_DSA_KV = D_DSA_QI + 4
D_DSA_Q = D_DSA_KV + 1
D_WOUT1 = D_DSA_Q + A_HEADS // 2
D_FFN1 = D_WOUT1 + KT // 2

C_MLSTM = 0
C_FFN0 = C_MLSTM + 3 * M_HEADS
C_DSA_QI = C_FFN0 + 4 * GROUPS
C_DSA_KV = C_DSA_QI + 4
C_DSA_Q = C_DSA_KV + 1
C_FFN1 = C_DSA_Q + A_HEADS // 2

M_K, M_V, M_O, M_GATE = M_HEADS * DK, 2 * M_HEADS * DK, 2 * M_HEADS * DK + M_HEADS * DV, 2 * M_HEADS * (DK + DV)
A_KV, A_QI = A_HEADS * DH, A_HEADS * DH + 2 * DH
A_KW = A_QI + I_HEADS * I_DIM

V_MIXG, V_FFNG, V_HEADG, V_QG, V_KG, V_ROWS = 0, 2 * KT, 4 * KT, 5 * KT, 5 * KT + 1, 5 * KT + 2


ROOT_HEADS = 1
ROOT_X = (0, 1 + M_HEADS, 2 + M_HEADS, 4 + M_HEADS + A_HEADS // 2)
ROOT_K = 3 + M_HEADS
ROOT_Q = 4 + M_HEADS


def trunk(nc, x, mix_norm_g, ffn_norm_g, mlstm_w_in, mlstm_gate_b, mlstm_head_g, mlstm_w_out,
          dsa_w_in, dsa_q_g, dsa_k_g, dsa_w_out, ffn_w_up, ffn_dw_w, ffn_w_down, out):
    ctx = ExitStack()
    with ctx:
        def sb(name, shape, dt=F32):
            return ctx.enter_context(nc.sbuf_tensor(name, shape, dt))

        def sem(name):
            return ctx.enter_context(nc.semaphore(name))

        raw = sb("raw", [P, RING, 2 * BLK * P])
        w_hi = sb("w_hi", [P, RING, BLK, P], F32R)
        w_lo = sb("w_lo", [P, RING, BLK, P], F32R)
        X = sb("X", [P, KT, T])
        xs = sb("xs", [P, KT, 2, T], F32R)
        mix = sb("mix", [P, KT, 2, T], F32R)
        hid = sb("hid", [P, GROUP, 2, T], F32R)
        rms_scale = sb("rms_scale", [P, T])
        ident = sb("ident", [P, P])
        ones = sb("ones", [P, T])
        neg_future = sb("neg_future", [P, T])
        mask_q = sb("mask_q", [P, 3 * P])
        vecs = sb("vecs", [P, V_ROWS])
        taps = sb("taps", [P, 2, TAPS, UP_TILES])
        gate_b = sb("gate_b", [40, 1])
        power = sb("power", [P, 4])
        mean_sq = sb("mean_sq", [P, 4])
        root = sb("root", [P, 4])
        diag = sb("diag", [P, 4, P])
        tail = sb("tail", [P, 2, T])
        both = sb("both", [P, 2, T])
        pads = sb("pads", [P, 2, T + TAPS - 1])
        sq = sb("sq", [P, 4, T])
        sq_sum = sb("sq_sum", [P, 4, T])
        scratch = sb("scratch", [P, 7400])

        def part(at, *shape, rows=P):
            n = int(np.prod(shape))
            v = scratch[0:rows, at:at + n]
            if len(shape) == 2:
                v = v.rearrange("p (a b) -> p a b", a=shape[0])
            return v

        x_tok = part(0, 2, D)
        vec_rows = part(4096, P, rows=V_ROWS)
        tap_rows = part(4224, 2 * TAPS, P, rows=UP_TILES)
        QK = part(0, 2, T)
        vT = part(512, 2, T)
        V = part(1024, 2, DV)
        og = part(1536, 2, T)
        rows_m = part(2048, 512, rows=M_HEADS)
        head_rows = part(2560, 512, rows=M_HEADS)
        em = part(3072, T)
        E = part(3328, 3 * P)
        S = part(3712, 3 * P)
        den = part(4096, T)
        H = part(4352, 2, T)
        HG = part(5376, 2, T)
        a_tok = part(5888, 2, M_HEADS)
        gate_raw = part(5904, KT, 16)
        gates = part(6160, T, rows=40)
        gA = part(6416, T, rows=M_HEADS)
        gB = part(6672, T, rows=M_HEADS)
        gC = part(6928, T, rows=M_HEADS)
        gF = part(4352, T, rows=M_HEADS)
        gate_tail = part(4864, T, rows=40)
        kw_raw = part(2048, KT, 80)
        QI = part(1280, 8, T)
        KI = part(3328, T)
        wiT = part(3584, T)
        WI = part(3840, 2, I_HEADS)
        relu = part(3872, 2, T)
        score = part(4384, 3 * P)
        work = part(4768, 3 * P)
        best = part(5152, 2, 8)
        KV = part(5168, 2, T)
        KN = part(5680, T)
        VA = part(5936, 2, DH)
        qg = part(6192, 1)
        QT = part(0, 2, T)
        QN = part(512, 2, T)
        LM = part(2304, 2, 3 * P)
        PT = part(6200, 2, 3 * P)
        mx = part(3072, 2, 2)
        sums = part(3076, 2, 2)
        CA = part(0, 2, T)
        CB = part(512, 2, T)
        SA = part(1024, 2, T)
        G = part(1536, 2, T)

        side_w = [mix[:, 4 * j:4 * j + 4].rearrange("p a b t -> p (a b t)").rearrange("p (k c) -> p k c", k=KT)
                  for j in range(2)]
        side_w_hi, side_w_lo = side_w

        ps = ctx.enter_context(nc.psum_tensor("ps", [P, 8, 512], F32))

        load_done = [sem(f"load_done{i}") for i in range(RING)]
        halves_hi = sem("halves_hi")
        halves_split = sem("halves_split")
        halves_used = sem("halves_used")
        psum_free = sem("psum_free")
        tails = sem("tails")
        chain = sem("chain")
        act_chain = sem("act_chain")
        small_in = sem("small_in")
        x_in = sem("x_in")
        gate_in = sem("gate_in")
        kw_in = sem("kw_in")
        consts_zero = sem("consts_zero")
        consts = sem("consts")
        x_turned = sem("x_turned")
        x_copied = sem("x_copied")
        vecs_turned = sem("vecs_turned")
        vecs_ready = sem("vecs_ready")
        qk_ready = sem("qk_ready")
        xs_hi = sem("xs_hi")
        squares = sem("squares")
        squares_used = sem("squares_used")
        xs_ready = sem("xs_ready")
        sq_ready = sem("sq_ready")
        sums_mm = sem("sums_mm")
        mean_ready = sem("mean_ready")
        root_ready = sem("root_ready")
        diag_ready = sem("diag_ready")
        spread_mm = sem("spread_mm")
        side_hi = sem("side_hi")
        side_split = sem("side_split")
        side_mm = sem("side_mm")
        side_tail = sem("side_tail")
        gate_zero = sem("gate_zero")
        gate_dve = sem("gate_dve")
        gate_act = sem("gate_act")
        a_ready = sem("a_ready")
        a_turned = sem("a_turned")
        a_tok_ready = sem("a_tok_ready")
        vT_ready = sem("vT_ready")
        v_turned = sem("v_turned")
        v_ready = sem("v_ready")
        og_ready = sem("og_ready")
        og_exp = sem("og_exp")
        rows_ready = sem("rows_ready")
        qk_mm = sem("qk_mm")
        em_ready = sem("em_ready")
        e_ready = sem("e_ready")
        w_ready = sem("w_ready")
        s_ready = sem("s_ready")
        pv_mm = sem("pv_mm")
        h_ready = sem("h_ready")
        h_sq = sem("h_sq")
        hg_ready = sem("hg_ready")
        mix_hi = sem("mix_hi")
        mix_ready = sem("mix_ready")
        kw_ready = sem("kw_ready")
        wi_turned = sem("wi_turned")
        wi_ready = sem("wi_ready")
        qi_ready = sem("qi_ready")
        score_mm = sem("score_mm")
        relu_ready = sem("relu_ready")
        relu_used = sem("relu_used")
        kv_ready = sem("kv_ready")
        kv_sq = sem("kv_sq")
        kv_mm = sem("kv_mm")
        va_ready = sem("va_ready")
        kn_ready = sem("kn_ready")
        qg_ready = sem("qg_ready")
        q_ready = sem("q_ready")
        q_sq = sem("q_sq")
        qn_ready = sem("qn_ready")
        logit_mm = sem("logit_mm")
        max_ready = sem("max_ready")
        exp_ready = sem("exp_ready")
        inv_ready = sem("inv_ready")
        probs_ready = sem("probs_ready")
        probs_turned = sem("probs_turned")
        pt_ready = sem("pt_ready")
        av_mm = sem("av_mm")
        up_ready = sem("up_ready")
        tap2_ready = sem("tap2_ready")
        conv_a = sem("conv_a")
        silu_ready = sem("silu_ready")
        gated = sem("gated")
        hid_hi = sem("hid_hi")
        hid_ready = sem("hid_ready")
        y_turned = sem("y_turned")
        y_copied = sem("y_copied")
        stored = sem("stored")

        block = ctx.enter_context(nc.Block())

        w_in0 = mlstm_w_in[0].rearrange("(k p) n -> p k n", p=P)
        w_in1 = dsa_w_in[0].rearrange("(k p) n -> p k n", p=P)
        w_out = [mlstm_w_out[0].rearrange("(k p) n -> p k n", p=P), dsa_w_out[0].rearrange("(k p) n -> p k n", p=P)]
        w_up = [ffn_w_up[l].rearrange("(k p) n -> p k n", p=P) for l in range(2)]
        w_down = [ffn_w_down[l].rearrange("(k p) n -> p k n", p=P) for l in range(2)]

        @block.sync
        def _(sp):
            def load(base, per, i, c, src, cols):
                first = base + c
                number = first + per * i
                assert per % RING == 0
                if first >= RING:
                    sp.wait_ge(halves_split, 2 * (number - RING) + 2)
                dst = raw[:, first % RING].rearrange("p (k n) -> p k n", n=cols)
                sp.dma_start(dst, src).then_inc(load_done[first % RING], 16)

            def pair(base, per, i, c, w, col):
                for hf in range(2):
                    load(base, per, i, c + hf, w[:, BLK * hf:BLK * hf + BLK, bass.ds(col, 2 * P)], 2 * P)

            def two_pairs(base, i, w):
                for hf in range(2):
                    for q in range(2):
                        load(base, 4, i, 2 * hf + q, w[:, BLK * hf:BLK * hf + BLK, bass.ds((2 * i + q) * 2 * P, 2 * P)], 2 * P)

            def head(base, per, i, c, h):
                load(base, per, i, c, w_in0[:, :, bass.ds(h * DK, DK)], DK)
                load(base, per, i, c + 1, w_in0[:, :, bass.ds(M_K + h * DK, DK)], DK)
                pair(base, per, i, c + 2, w_in0, M_V + h * DV)
                pair(base, per, i, c + 4, w_in0, M_O + h * DV)

            def ffn(base, l):
                def group(b, i, g):
                    c = 0
                    for q in range(2):
                        for ab in range(2):
                            pair(b, 12, i, c, w_up[l], ab * D_FF + g * GROUP * P + q * 2 * P)
                            c += 2
                    for q in range(2):
                        for kk in range(2):
                            load(b, 12, i, c, w_down[l][:, bass.ds(g * GROUP + 2 * kk, 2), q * 1024:q * 1024 + 1024], 1024)
                            c += 1
                with sp.Fori(0, GROUPS) as g:
                    group(base, g, g)

            head(0, 12, 0, 0, 0)
            with sp.Fori(0, 3) as i:
                head(6, 12, i, 0, 2 * i + 1)
                head(6, 12, i, 6, 2 * i + 2)
            head(42, 12, 0, 0, 7)
            with sp.Fori(0, 4) as i:
                two_pairs(H_WOUT0 // 2, i, w_out[0])
            ffn(H_FFN0 // 2, 0)
            with sp.Fori(0, 2) as i:
                pair(H_DSA_QI // 2, 4, i, 0, w_in1, A_QI + i * 4 * P)
                pair(H_DSA_QI // 2, 4, i, 2, w_in1, A_QI + i * 4 * P + 2 * P)
            pair(H_DSA_KV // 2, 4, 0, 0, w_in1, A_KV)
            with sp.Fori(0, 4) as i:
                pair(H_DSA_Q // 2, 4, i, 0, w_in1, i * 4 * P)
                pair(H_DSA_Q // 2, 4, i, 2, w_in1, i * 4 * P + 2 * P)
            with sp.Fori(0, 4) as i:
                two_pairs(H_WOUT1 // 2, i, w_out[1])
            ffn(H_FFN1 // 2, 1)
            for b in range(2):
                sp.wait_ge(y_copied, 4 * (b + 1))
                sp.dma_start(out[0, b * P:(b + 1) * P, :], x_tok[:, b]).then_inc(stored, 16)
            sp.wait_ge(stored, 32)

        PAIR, UNIT, DOWN = range(3)

        def layout(n):
            if n < H_WOUT0:
                return UNIT if n % 12 < 4 else PAIR
            for base in (H_FFN0, H_FFN1):
                if base <= n < base + 24 * GROUPS and (n - base) % 24 >= 16:
                    return DOWN
            return PAIR

        def raw_half(n):
            slot, j = n // 2 % RING, n % 2
            if layout(n) == UNIT:
                return raw[:, slot].rearrange("p (j k n) -> p j k n", j=2, k=BLK)[:, j]
            return raw[:, slot].rearrange("p (k u n) -> p k u n", k=2 if layout(n) == DOWN else BLK, u=2)[:, :, j]

        def split_half(t, n):
            v = t[:, n % RING]
            return v.rearrange("p (k d) n -> p k (d n)", k=2) if layout(n) == DOWN else v

        def act_split(act, n, off):
            if n >= H_END:
                return
            load = n // 2
            act.wait_ge(load_done[load % RING], 16 * (load // RING + 1) + off * 2)
            if n >= RING:
                act.wait_ge(halves_used, n - RING + 1 + off)
            act.activation(split_half(w_hi, n), raw_half(n), ACT.Copy).then_inc(halves_hi, 1)

        def dve_split(dve, n, off):
            if n >= H_END:
                return
            dve.wait_ge(halves_hi, n + 1 + off)
            dve.tensor_tensor(split_half(w_lo, n), raw_half(n), split_half(w_hi, n).bitcast(F32), ALU.subtract).then_inc(halves_split, 1)

        @block.tensor
        def _(pe):
            def hi_lo(bank, wh, wl, mv, first, last):
                def wide():
                    return pe.matmul(ps[:, bank], wh, mv.rearrange("p a t -> p (a t)"), start=first, stop=last)

                def narrow():
                    pe.matmul(ps[:, bank, 0:T], wl, mv[:, 0], start=False, stop=False, skip_group_check=True)
                if first:
                    wide()
                    narrow()
                    return None
                narrow()
                return wide()

            def half(n, off, j, bank, mv):
                pe.wait_ge(halves_split, n + 1 + off)
                for b in range(BLK):
                    k = BLK * j + b
                    mm = hi_lo(bank, w_hi[:, n % RING, b], w_lo[:, n % RING, b], mv[:, k], k == 0, k == KT - 1)
                mm.then_inc(halves_used, 1)

            def pair(n, off, d, doff, mv, before=(None,) * 4, wait_mv=None):
                bank = 2 * (d % 2)
                if d >= 2:
                    pe.wait_ge(psum_free, d - 1 + doff)
                for c in range(4):
                    if before[c]:
                        before[c]()
                    if wait_mv:
                        wait_mv(c)
                    unit, j = (c // 2, c % 2) if layout(n) == UNIT else (c % 2, c // 2)
                    half(n + c, off, j, bank + unit, mv)

            def sums(bank, at, columns):
                for c, tiles in enumerate(columns):
                    for j, t in enumerate(tiles):
                        mm = pe.matmul(ps[:, bank, at + c:at + c + 1], t, ones[:, 0:1], start=j == 0,
                                       stop=j == len(tiles) - 1)
                mm.then_inc(sums_mm, 1)

            def spread(bank, at, n, number):
                pe.wait_ge(diag_ready, number + 1)
                pe.matmul(ps[:, bank, at:at + n * P], ones[:, 0:P], diag[:, 0:n].rearrange("p a t -> p (a t)"),
                          start=True, stop=True).then_inc(spread_mm, 1)

            def norm_sum(i):
                pe.wait_ge(sq_ready, i + 1)
                if i in (1, 3):
                    pe.wait_ge(psum_free, D_FFN0 if i == 1 else D_FFN1)
                sums(7, 0, [[sq_sum[:, 0, 0:P]], [sq_sum[:, 0, P:T]]])

            def norm_spread(i):
                spread(7, 0, 2, ROOT_X[i])

            def xs_wait(i):
                def w(c):
                    if c in (0, 2):
                        pe.wait_ge(xs_ready, 4 * i + (2 if c == 0 else 4))
                return w

            pe.wait_ge(consts, 1)
            pe.wait_ge(small_in, 96)
            pe.transpose(ps[:, 0, 0:V_ROWS], vec_rows, ident[0:V_ROWS, 0:V_ROWS])
            for l in range(2):
                for t in range(TAPS):
                    mm = pe.transpose(ps[:, 1 + l, t * UP_TILES:(t + 1) * UP_TILES], tap_rows[:, l * TAPS + t],
                                      ident[0:UP_TILES, 0:UP_TILES])
            mm.then_inc(vecs_turned, 1)
            pe.wait_ge(x_in, 16)
            pe.wait_ge(vecs_ready, 1)
            for r in range(KT // 2):
                for kk in range(2):
                    for b in range(2):
                        k = 2 * r + kk
                        mm = pe.transpose(ps[:, r, kk * T + b * P:kk * T + (b + 1) * P],
                                          x_tok[:, b, k * P:(k + 1) * P], ident[:])
                mm.then_inc(x_turned, 1)

            pe.wait_ge(x_copied, KT // 2)
            pe.wait_ge(side_split, 1)
            for k in range(KT):
                if k % 4 == 0:
                    pe.wait_ge(xs_ready, k // 4 + 1)
                mm = hi_lo(4, side_w_hi[:, k], side_w_lo[:, k], xs[:, k], k == 0, k == KT - 1)
            mm.then_inc(side_mm, 1)

            def causal(bank, c, v0, v1, s):
                pe.matmul(ps[:, bank, c:c + P], v0, s[:, 0:P], start=True, stop=True)
                pe.matmul(ps[:, bank, c + P:c + T], v0, s[:, P:T], start=True, stop=False)
                return pe.matmul(ps[:, bank, c + P:c + T], v1, s[:, T:T + P], start=False, stop=True)

            def head_scores(h):
                pe.wait_ge(rows_ready, h + 1)
                pe.wait_ge(qk_ready, h + 1)
                pe.wait_ge(v_ready, h + 1)
                pe.matmul(ps[:, 4], ones[0:M_HEADS, 0:P], head_rows, start=True, stop=True)
                pe.matmul(ps[:, 5, 0:T], QK[:, 1, 0:P], QK[:, 0], start=True, stop=True)
                pe.matmul(ps[:, 5, T:T + P], QK[:, 1, P:T], QK[:, 0, P:T], start=True, stop=True).then_inc(qk_mm, 1)

            def head_values(h):
                pe.wait_ge(s_ready, h + 1)
                for j in range(2):
                    causal(6, j * T, V[:, 0, j * P:(j + 1) * P], V[:, 1, j * P:(j + 1) * P], S)
                causal(7, 0, ones[:, 0:P], ones[:, 0:P], S).then_inc(pv_mm, 1)

            def head_square(h):
                pe.wait_ge(h_sq, h + 1)
                sums(7, T, [[sq[:, j, b * P:(b + 1) * P] for j in range(2)] for b in range(2)])

            def head_turn_v(h):
                pe.wait_ge(vT_ready, h + 1)
                for s in range(2):
                    for j in range(2):
                        mm = pe.transpose(ps[:, 4, s * DV + j * P:s * DV + (j + 1) * P],
                                          vT[:, j, s * P:(s + 1) * P], ident[:])
                mm.then_inc(v_turned, 1)

            def head(n, off, d, doff, h, prev):
                a = [None] * 12
                if prev is not None:
                    a[1] = lambda: head_scores(prev)
                    a[3] = lambda: head_values(prev)
                    a[5] = lambda: head_square(prev)
                    a[7] = lambda: spread(7, T, 2, ROOT_HEADS + prev)
                a[10] = lambda: head_turn_v(h)
                for c in range(3):
                    pair(n + 4 * c, off, d + c, doff, xs, a[4 * c:4 * c + 4])

            def turn_a():
                pe.wait_ge(a_ready, 1)
                for b in range(2):
                    mm = pe.transpose(ps[:, 5, b * M_HEADS:(b + 1) * M_HEADS], gA[:, b * P:(b + 1) * P],
                                      ident[0:M_HEADS, 0:M_HEADS])
                mm.then_inc(a_turned, 1)

            pair(0, 0, 0, 0, xs, (lambda: norm_sum(0), lambda: norm_spread(0), None, None))
            pair(4, 0, 1, 0, xs)
            pair(8, 0, 2, 0, xs, (None, turn_a, lambda: head_turn_v(0), None))
            with pe.Fori(0, 3) as i:
                head(12, 24 * i, 3, 6 * i, 2 * i + 1, 2 * i)
                head(24, 24 * i, 6, 6 * i, 2 * i + 2, 2 * i + 1)
            head(84, 0, 21, 0, 7, 6)

            def out_proj(n, d, steps):
                def two_pairs(n, off, d, doff, steps):
                    for c in range(8):
                        if c in (0, 2):
                            pe.wait_ge(psum_free, d + c // 2 - 1 + doff)
                        for f in steps.get(c, ()):
                            f()
                        half(n + c, off, c // 4, 2 * ((d + c % 4 // 2) % 2) + c % 2, mix)
                two_pairs(n, 0, d, 0, steps)
                with pe.Fori(0, 3) as i:
                    two_pairs(n + 8, 8 * i, d + 2, 2 * i, {})

            def mixed(count):
                return lambda: pe.wait_ge(mix_ready, count)

            out_proj(H_WOUT0, D_WOUT0, {
                0: (lambda: head_scores(7), mixed(M_HEADS // 2)), 1: (lambda: head_values(7),),
                2: (lambda: head_square(7),), 4: (lambda: spread(7, T, 2, ROOT_HEADS + 7), mixed(M_HEADS))})

            def ffn(n0, d0, norm, done):
                def first(c):
                    if c == 0:
                        pe.wait_ge(xs_ready, 4 * norm + 2)
                    if c == 1:
                        norm_sum(norm)
                    if c == 2:
                        norm_spread(norm)
                        pe.wait_ge(xs_ready, 4 * norm + 4)

                def group(n0, off, d0, doff, g, peel):
                    for q in range(4):
                        pe.wait_ge(psum_free, d0 + (-1, 0, 0, 1)[q] + doff)
                        for c in range(4):
                            if peel and q == 0:
                                first(c)
                            half(n0 + 4 * q + c, off, c // 2, 2 * q + c % 2, xs)
                    for q in range(2):
                        for kk in range(2):
                            if q == 0:
                                pe.wait_ge(hid_ready, done + 2 * g + kk + 1)
                            for u in range(2):
                                n = n0 + 16 + 4 * q + 2 * kk + u
                                if kk == 0:
                                    pe.wait_ge(psum_free, d0 + (2, 4, 5, 6)[2 * q + u] + doff)
                                pe.wait_ge(halves_split, n + 1 + off)
                                for k2 in range(2):
                                    for dt in range(4):
                                        b = 4 * k2 + dt
                                        mm = hi_lo(4 * u + dt, w_hi[:, n % RING, b], w_lo[:, n % RING, b],
                                                   hid[:, 2 * kk + k2], kk == 0 and k2 == 0, kk == 1 and k2 == 1)
                                (mm if mm is not None else None).then_inc(halves_used, 1)

                group(n0, 0, d0, 0, 0, True)
                with pe.Fori(1, GROUPS) as g:
                    group(n0 + 24, 24 * g - 24, d0 + 8, 8 * g - 8, g, False)

            ffn(H_FFN0, D_FFN0, 1, 0)

            def kw_unit():
                pe.wait_ge(side_split, 2)
                pe.wait_ge(psum_free, D_DSA_QI)
                for k in range(KT):
                    mm = hi_lo(4, side_w_hi[:, k], side_w_lo[:, k], xs[:, k], k == 0, k == KT - 1)
                mm.then_inc(side_mm, 1)

            def turn_wi():
                pe.wait_ge(kw_ready, 1)
                for b in range(2):
                    mm = pe.transpose(ps[:, 7, b * I_HEADS:(b + 1) * I_HEADS], wiT[64:80, b * P:(b + 1) * P],
                                      ident[64:80, 64:80])
                mm.then_inc(wi_turned, 1)

            def scores(t):
                pe.wait_ge(qi_ready, t // 2 + 1)
                pe.wait_ge(kw_ready, 1)
                pe.wait_ge(wi_ready, 1)
                if t:
                    pe.wait_ge(relu_ready, 2 * t)
                for b in range(2):
                    w = (b + 1) * P
                    for s in range(2):
                        mm = pe.matmul(ps[:, 4 + 2 * b + s, 0:w], QI[64 * s:64 * s + 64, t, b * P:(b + 1) * P],
                                       KI[64 * s:64 * s + 64, 0:w], start=True, stop=True)
                    mm.then_inc(score_mm, 1)

            for j in range(4):
                t = 2 * (j - 1)
                if j == 0:
                    pair(H_DSA_QI, 0, D_DSA_QI, 0, xs, (None, lambda: norm_sum(2), None, lambda: norm_spread(2)), wait_mv=xs_wait(2))
                    kw_unit()
                else:
                    pair(H_DSA_QI + 4 * j, 0, D_DSA_QI + j, 0, xs,
                         (None, (lambda: turn_wi()) if j == 1 else None, lambda t=t: scores(t), lambda t=t: scores(t + 1)))

            def kv_sum():
                pe.wait_ge(kv_sq, 1)
                sums(4, 0, [[sq[:, 0, b * P:(b + 1) * P]] for b in range(2)])
                for s in range(2):
                    mm = pe.transpose(ps[:, 4, T + s * P:T + (s + 1) * P], KV[:, 1, s * P:(s + 1) * P], ident[:])
                mm.then_inc(kv_mm, 1)

            def q_sum(p):
                pe.wait_ge(q_sq, p + 1)
                sums(4, 0, [[sq[:, a, b * P:(b + 1) * P]] for a in range(2) for b in range(2)])

            def q_spread(p):
                spread(4, 0, 4, ROOT_Q + p)

            def logits(p):
                pe.wait_ge(qn_ready, p + 1)
                pe.wait_ge(kn_ready, 1)
                for a in range(2):
                    pe.matmul(ps[:, 5 + a, 0:P], QN[:, a, 0:P], KN[:, 0:P], start=True, stop=True)
                    mm = pe.matmul(ps[:, 5 + a, P:3 * P], QN[:, a, P:T], KN[:], start=True, stop=True)
                mm.then_inc(logit_mm, 1)

            def turn_probs(p):
                pe.wait_ge(probs_ready, p + 1)
                for a, bank in ((0, 7), (1, 5)):
                    for c in range(3):
                        mm = pe.transpose(ps[:, bank, c * P:(c + 1) * P], LM[:, a, c * P:(c + 1) * P], ident[:])
                mm.then_inc(probs_turned, 1)

            def values(p):
                pe.wait_ge(pt_ready, p + 1)
                pe.wait_ge(va_ready, 1)
                for a in range(2):
                    mm = causal(7, a * T, VA[:, 0], VA[:, 1], PT[:, a])
                mm.then_inc(av_mm, 1)

            pair(H_DSA_KV, 0, D_DSA_KV, 0, xs, (None, None, lambda: scores(6), lambda: scores(7)))
            pair(H_DSA_Q, 0, D_DSA_Q, 0, xs, (None, kv_sum, None, lambda: spread(4, 0, 2, ROOT_K)))
            pair(H_DSA_Q + 4, 0, D_DSA_Q + 1, 0, xs, (None, lambda: q_sum(0), None, lambda: q_spread(0)))

            def q_frame(n, off, d, doff, p):
                pair(n, off, d, doff, xs, (lambda: logits(p - 2), lambda: q_sum(p - 1), lambda: turn_probs(p - 2),
                                           lambda: (values(p - 2), q_spread(p - 1))))

            with pe.Fori(0, 3) as i:
                q_frame(H_DSA_Q + 8, 8 * i, D_DSA_Q + 2, 2 * i, 2 * i + 2)
                q_frame(H_DSA_Q + 12, 8 * i, D_DSA_Q + 3, 2 * i, 2 * i + 3)

            out_proj(H_WOUT1, D_WOUT1, {
                0: (lambda: logits(6), lambda: q_sum(7), mixed(M_HEADS + 4)), 1: (lambda: turn_probs(6),),
                2: (lambda: values(6), lambda: q_spread(7)), 3: (lambda: logits(7),),
                4: (lambda: turn_probs(7), lambda: values(7), mixed(M_HEADS + 8))})
            ffn(H_FFN1, D_FFN1, 3, 2 * GROUPS)

            pe.wait_ge(psum_free, D_FFN1 + 8 * GROUPS)
            for b in range(2):
                for r in range(4):
                    bank = 4 * b + r
                    for k in range(4):
                        mm = pe.transpose(ps[:, bank, k * P:(k + 1) * P], X[:, 4 * r + k, b * P:(b + 1) * P], ident[:])
                    mm.then_inc(y_turned, 1)

        @block.scalar
        def _(act):
            def tail_copy(n, off, d, c, coff, doff, bank):
                act.wait_ge(halves_used, n + 1 + off)
                if c > 0:
                    act.wait_ge(psum_free, d + doff)
                act.activation(tail[:], ps[:, bank:bank + 2, T:2 * T], ACT.Copy).then_inc(tails, 1)

            def norm(i, g0, done, count):
                act.wait_ge(done, count)
                for r in range(4):
                    for k in range(4 * r, 4 * r + 4):
                        ins = act.activation(xs[:, k, 0], X[:, k], ACT.Copy, scale=vecs[:, g0 + k:g0 + k + 1])
                    ins.then_inc(xs_hi, 1)
                    if i or r:
                        act.wait_ge(squares_used, 4 * i + r)
                    act.activation(sq[:], X[:, 4 * r:4 * r + 4], ACT.Square).then_inc(squares, 1)

            act.dma_start(gate_raw, w_in0[:, :, M_GATE:M_GATE + 16]).then_inc(gate_in, 16)
            act.wait_ge(gate_zero, 1)
            act.dma_start(gate_b[0:8, :], mlstm_gate_b[0, 0:8].rearrange("(p a) -> p a", a=1)).then_inc(gate_in, 16)
            act.dma_start(gate_b[32:40, :], mlstm_gate_b[0, 8:16].rearrange("(p a) -> p a", a=1)).then_inc(gate_in, 16)
            for n in range(LEAD):
                act_split(act, n, 0)
            act.wait_ge(gate_in, 48)
            act.wait_ge(gate_zero, 2)
            act.activation(side_w_hi[:, :, 0:8], gate_raw[:, :, 0:8], ACT.Copy)
            act.activation(side_w_hi[:, :, 32:40], gate_raw[:, :, 8:16], ACT.Copy).then_inc(side_hi, 1)
            act.wait_ge(vecs_ready, 1)
            norm(0, V_MIXG, x_copied, KT // 2)
            act.wait_ge(side_mm, 1)
            act.activation(gate_tail, ps[0:40, 4, T:2 * T], ACT.Copy).then_inc(side_tail, 1)
            act.wait_ge(gate_dve, 1)
            act.activation(gC[:], gB[:], ACT.Exp, scale=-1.0).then_inc(act_chain, 1)
            act.wait_ge(act_chain, 1)
            act.activation(gC[:], gC[:], ACT.Ln, bias=1.0).then_inc(gate_act, 1)
            act.wait_ge(gate_dve, 2)
            act.activation(rows_m[:, T:2 * T], gB[:], ACT.Exp, scale=-1.0).then_inc(gate_act, 1)

            def og_neg_exp(h):
                act.wait_ge(og_ready, h + 1)
                act.activation(HG[:], og[:], ACT.Exp, scale=-1.0).then_inc(og_exp, 1)

            def head_weights(h):
                act.wait_ge(qk_mm, h + 1)
                act.activation(em[:], ps[:, 4, T:2 * T], ACT.Copy).then_inc(em_ready, 1)
                act.wait_ge(e_ready, h + 1)
                act.activation(E[:], E[:], ACT.Exp).then_inc(w_ready, 1)

            def head_squares(h):
                act.wait_ge(h_ready, h + 1)
                act.activation(sq[:, 0:2], H[:], ACT.Square).then_inc(h_sq, 1)

            def head_hi(h):
                act.wait_ge(hg_ready, h + 1)
                act.activation(mix[:, bass.ds(2 * h, 2), 0], HG[:], ACT.Copy).then_inc(mix_hi, 1)

            def head_v(h):
                act.wait_ge(v_turned, h + 1)
                act.activation(V[:].rearrange("p a b -> p (a b)"), ps[:, 4], ACT.Copy).then_inc(v_ready, 1)

            def head(n, off, c, coff, h, prev):
                bank0 = c % 2
                for k in range(12):
                    act_split(act, n + k + LEAD, off)
                    if prev is not None:
                        if k == 0:
                            og_neg_exp(prev)
                        if k == 1:
                            head_weights(prev)
                        if k == 3:
                            head_squares(prev)
                    if k % 4 == 3:
                        j = k // 4
                        tail_copy(n + k, off, c + j, c + j, coff, coff, 2 * ((c + j) % 2))
                    if prev is not None and k == 8:
                        head_hi(prev)
                    if k == 10:
                        head_v(h)

            head(0, 0, 0, 0, 0, None)
            with act.Fori(0, 3) as i:
                head(12, 24 * i, 3, 6 * i, 2 * i + 1, 2 * i)
                head(24, 24 * i, 6, 6 * i, 2 * i + 2, 2 * i + 1)
            head(84, 0, 21, 0, 7, 6)

            def out_proj(n, pre):
                for k in range(8):
                    act_split(act, n + k + LEAD, 0)
                    for f in pre.get(k, ()):
                        f()
                with act.Fori(0, 3) as i:
                    for k in range(8):
                        act_split(act, n + 8 + k + LEAD, 8 * i)

            out_proj(H_WOUT0, {0: (lambda: og_neg_exp(7), lambda: head_weights(7)), 1: (lambda: head_squares(7),),
                               3: (lambda: head_hi(7),)})

            def ffn(n0, d0, c0, l, done, norm_i, last):
                norm(norm_i, V_FFNG + KT * l, psum_free, d0)

                def tap2(dst, tile0, count):
                    act.wait_ge(up_ready, count + 1)
                    for j in range(2):
                        ins = act.activation(dst[:, j], pads[:, j, TAPS - 1:], ACT.Copy,
                                             scale=taps[:, l, 2, bass.ds(tile0 + j, 1)])
                    ins.then_inc(tap2_ready, 1)

                def group(n0, off, d0, doff, c0, coff, g):
                    ups = 2 * done + 4 * g
                    for k in range(24):
                        act_split(act, n0 + k + LEAD, off)
                        if k < 16 and k % 4 == 3:
                            q = k // 4
                            tail_copy(n0 + k, off, d0 + q, c0 + q, coff, doff, 2 * q)
                        if k < 17 and k % 4 == 0 and k:
                            q = k // 4 - 1
                            ab, half_q = q % 2, q // 2
                            tap2((CA, CB)[ab], ab * (UP_TILES // 2) + g * GROUP + 2 * half_q, ups + q)
                        if k in (5, 13):
                            act.wait_ge(conv_a, done + 2 * g + k // 8 + 1)
                            act.activation(SA[:], CA[:], ACT.Silu).then_inc(silu_ready, 1)
                        if k in (9, 17):
                            q = k // 16
                            act.wait_ge(gated, done + 2 * g + q + 1)
                            if q == 0:
                                act.wait_ge(halves_used, n0 + off)
                            act.activation(hid[:, 2 * q:2 * q + 2, 0], G[:], ACT.Copy).then_inc(hid_hi, 1)

                n = GROUPS - 1 if last else GROUPS
                with act.Fori(0, n) as g:
                    group(n0, 24 * g, d0, 8 * g, c0, 4 * g, g)
                if last:
                    group(n0 + 24 * n, 0, d0 + 8 * n, 0, c0 + 4 * n, 0, n)

            ffn(H_FFN0, D_FFN0, C_FFN0, 0, 0, 1, False)

            norm(2, V_MIXG + KT, psum_free, D_DSA_QI)
            act.wait_ge(kw_in, 16)
            act.activation(side_w_hi[:, :, 0:80], kw_raw, ACT.Copy)
            act.activation(side_w_hi[:, :, 80:P], kw_raw[:, :, 0:48], ACT.Copy).then_inc(side_hi, 1)

            def kw_tail():
                act.wait_ge(side_mm, 2)
                act.activation(KI[0:80], ps[0:80, 4, T:2 * T], ACT.Copy).then_inc(side_tail, 1)

            def wi_copy():
                act.wait_ge(wi_turned, 1)
                act.activation(WI[:].rearrange("p a b -> p (a b)"), ps[:, 7, 0:2 * I_HEADS], ACT.Copy,
                               scale=float((I_HEADS * I_DIM) ** -0.5)).then_inc(wi_ready, 1)

            def relus(t):
                for b in range(2):
                    act.wait_ge(score_mm, 2 * t + b + 1)
                    if 2 * t + b:
                        act.wait_ge(relu_used, 2 * t + b)
                    w = (b + 1) * P
                    act.activation(relu[:, :, 0:w], ps[:, 4 + 2 * b:6 + 2 * b, 0:w], ACT.Relu).then_inc(relu_ready, 1)

            for j in range(5):
                n = H_DSA_QI + 4 * j
                for k in range(4):
                    act_split(act, n + k + LEAD, 0)
                    if j == 1 and k == 0:
                        kw_tail()
                    if j == 1 and k == 1:
                        wi_copy()
                    if j and k in (2, 3):
                        relus(2 * (j - 1) + k - 2)
                    if k == 3:
                        tail_copy(n + 3, 0, D_DSA_QI + j, C_DSA_QI + j, 0, 0, 2 * (j % 2))
            act.wait_ge(kv_ready, 1)
            act.activation(sq[:, 0], KV[:, 0], ACT.Square).then_inc(kv_sq, 1)

            def va_copy():
                act.wait_ge(kv_mm, 1)
                act.activation(VA[:].rearrange("p a b -> p (a b)"), ps[:, 4, T:2 * T], ACT.Copy).then_inc(va_ready, 1)

            def q_squares(p):
                act.wait_ge(q_ready, p + 1)
                act.activation(sq[:, 0:2], QT[:], ACT.Square).then_inc(q_sq, 1)

            def exps(p):
                act.wait_ge(max_ready, p + 1)
                for a in range(2):
                    for b in range(2):
                        c = slice(0, P) if b == 0 else slice(P, 3 * P)
                        ins = act.activation(LM[:, a, c], LM[:, a, c], ACT.Exp, bias=mx[:, a, b:b + 1],
                                             accum_out=sums[:, a, b:b + 1])
                ins.then_inc(exp_ready, 1)

            def probs(p):
                act.wait_ge(inv_ready, p + 1)
                for a in range(2):
                    for b in range(2):
                        c = slice(0, P) if b == 0 else slice(P, 3 * P)
                        ins = act.activation(LM[:, a, c], LM[:, a, c], ACT.Copy, scale=sums[:, a, b:b + 1])
                ins.then_inc(probs_ready, 1)

            def pt_copy(p):
                act.wait_ge(probs_turned, p + 1)
                act.activation(PT[:, 0], ps[:, 7, 0:3 * P], ACT.Copy)
                act.activation(PT[:, 1], ps[:, 5, 0:3 * P], ACT.Copy).then_inc(pt_ready, 1)

            def av_hi(p):
                act.wait_ge(av_mm, p + 1)
                act.activation(mix[:, bass.ds(2 * p, 2), 0], ps[:, 7].rearrange("p (a t) -> p a t", a=2),
                               ACT.Copy).then_inc(mix_hi, 1)

            def q_frame(n, off, d, c, doff, p, two):
                for k in range(4):
                    act_split(act, n + k + LEAD, off)
                    if two:
                        (exps, probs, pt_copy, av_hi)[k](p - 2)
                    if k == 3:
                        tail_copy(n + 3, off, d, c, doff, doff, 2 * (d % 2))
                        q_squares(p)

            for k in range(4):
                act_split(act, H_DSA_Q + k + LEAD, 0)
                if k == 1:
                    va_copy()
                if k == 3:
                    tail_copy(H_DSA_Q + 3, 0, D_DSA_Q, C_DSA_Q, 0, 0, 2 * (D_DSA_Q % 2))
                    q_squares(0)
            q_frame(H_DSA_Q + 4, 0, D_DSA_Q + 1, C_DSA_Q + 1, 0, 1, False)
            with act.Fori(0, 3) as i:
                q_frame(H_DSA_Q + 8, 8 * i, D_DSA_Q + 2, C_DSA_Q + 2, 2 * i, 2 * i + 2, True)
                q_frame(H_DSA_Q + 12, 8 * i, D_DSA_Q + 3, C_DSA_Q + 3, 2 * i, 2 * i + 3, True)

            out_proj(H_WOUT1, {0: (lambda: exps(6), lambda: probs(6)), 1: (lambda: pt_copy(6), lambda: av_hi(6)),
                               2: (lambda: exps(7), lambda: probs(7)), 3: (lambda: pt_copy(7), lambda: av_hi(7))})
            ffn(H_FFN1, D_FFN1, C_FFN1, 1, 2 * GROUPS, 3, True)

        @block.vector
        def _(dve):
            class Own:
                n = 0
                off = 0
            own = Own()

            def link(ins):
                own.n += 1
                ins.then_inc(chain, 1)
                dve.wait_ge(chain, own.n + own.off)

            def loop(count, per, body, start=0):
                at = own.n
                with dve.Fori(start, start + count) as i:
                    own.off = per * (i - start)
                    body(i)
                assert own.n - at == per, (own.n - at, per)
                own.n = at + per * count
                own.off = 0

            def drain(c, coff, bank):
                dve.wait_ge(tails, c + 1 + coff)
                ins = dve.tensor_tensor(both[:], ps[:, bank:bank + 2, 0:T], tail[:], ALU.add)
                ins.then_inc(psum_free, 1)
                return ins

            def scaled(dst, free_count):
                dve.wait_ge(psum_free, free_count)
                return dve.tensor_tensor(dst, both[:], rms_scale[:].rearrange("p (a t) -> p a t", a=1).broadcast_to([P, 2, T]), ALU.mult)

            def norm(i, g0):
                for r in range(4):
                    dve.wait_ge(xs_hi, 4 * i + r + 1)
                    for k in range(4 * r, 4 * r + 4):
                        ins = dve.scalar_tensor_tensor(xs[:, k, 1], X[:, k], vecs[:, g0 + k:g0 + k + 1],
                                                       xs[:, k, 0].bitcast(F32), ALU.mult, ALU.subtract)
                    ins.then_inc(xs_ready, 1)
                    dve.wait_ge(squares, 4 * i + r + 1)
                    if r == 0:
                        ins = dve.tensor_copy(sq_sum[:], sq[:])
                    else:
                        ins = dve.tensor_tensor(sq_sum[:], sq_sum[:], sq[:], ALU.add)
                    ins.then_inc(squares_used, 1)
                    dve.wait_ge(squares_used, 4 * i + r + 1)
                link(dve.tensor_tensor(sq_sum[:, 0:2], sq_sum[:, 0:2], sq_sum[:, 2:4], ALU.add))
                dve.tensor_tensor(sq_sum[:, 0], sq_sum[:, 0], sq_sum[:, 1], ALU.add).then_inc(sq_ready, 1)

            def mean(src, n, count, number):
                dve.wait_ge(sums_mm, number + 1)
                dve.tensor_scalar(mean_sq[:, 0:n], src, 1.0 / count, EPS, ALU.mult, ALU.add).then_inc(mean_ready, 1)

            def diagonal(n, number):
                dve.wait_ge(root_ready, number + 1)
                dve.tensor_tensor(diag[:, 0:n], ident[:].rearrange("p (a t) -> p a t", a=1).broadcast_to([P, n, P]),
                                  root[:, 0:n].rearrange("p (a t) -> p a t", t=1).broadcast_to([P, n, P]),
                                  ALU.mult).then_inc(diag_ready, 1)

            def norm_root(i):
                mean(ps[:, 7, 0:2], 2, D, ROOT_X[i])
                diagonal(2, ROOT_X[i])

            def norm_scale(i):
                dve.wait_ge(spread_mm, ROOT_X[i] + 1)
                link(dve.tensor_copy(rms_scale[:], ps[:, 7, 0:T]))

            for n in range(LEAD):
                dve_split(dve, n, 0)
            dve.wait_ge(vecs_turned, 1)
            dve.tensor_copy(vecs[:], ps[:, 0, 0:V_ROWS])
            for l in range(2):
                ins = dve.tensor_copy(taps[:, l].rearrange("p a b -> p (a b)"), ps[:, 1 + l, 0:TAPS * UP_TILES])
            ins.then_inc(vecs_ready, 1)
            dve.wait_ge(vecs_ready, 1)
            dve.memset(pads[:, :, 0:TAPS - 1], 0.0)
            for r in range(KT // 2):
                dve.wait_ge(x_turned, r + 1)
                dve.tensor_copy(X[:, 2 * r:2 * r + 2].rearrange("p a t -> p (a t)"), ps[:, r]).then_inc(x_copied, 1)
            dve.wait_ge(x_copied, KT // 2)
            dve.wait_ge(side_hi, 1)
            dve.tensor_tensor(side_w_lo[:, :, 0:8], gate_raw[:, :, 0:8], side_w_hi[:, :, 0:8].bitcast(F32), ALU.subtract)
            dve.tensor_tensor(side_w_lo[:, :, 32:40], gate_raw[:, :, 8:16], side_w_hi[:, :, 32:40].bitcast(F32),
                              ALU.subtract).then_inc(side_split, 1)
            norm(0, V_MIXG)
            norm_root(0)
            norm_scale(0)
            dve.wait_ge(side_tail, 1)
            link(dve.tensor_tensor(gates[:], ps[0:40, 4, 0:T], gate_tail, ALU.add))
            link(dve.tensor_tensor(gates[:], gates[:], rms_scale[0:40], ALU.mult))
            link(dve.tensor_scalar(gates[:], gates[:], gate_b[:, 0:1], None, ALU.add))
            link(dve.tensor_scalar(gA[:], gates[32:40], -1.0, None, ALU.mult))
            link(dve.tensor_copy(gF[:], gates[32:40]))
            dve.tensor_tensor(gB[:], gF[:], gA[:], ALU.max).then_inc(gate_dve, 1)
            dve.wait_ge(gate_act, 1)
            link(dve.scalar_tensor_tensor(gB[:], gF[:], 0.0, gC[:], ALU.min, ALU.subtract))
            link(dve.tensor_tensor_scan(gF[:], ones[0:M_HEADS], gB[:], 0.0, ALU.mult, ALU.add))
            dve.tensor_tensor(gA[:], gates[0:8], gF[:], ALU.subtract).then_inc(a_ready, 1)
            dve.wait_ge(a_ready, 1)
            link(dve.tensor_tensor_scan(gC[:], ones[0:M_HEADS], gA[:], 0.0, ALU.mult, ALU.max))
            dve.tensor_scalar(rows_m[:, 0:T], gC[:], -1.0, None, ALU.mult)
            dve.tensor_tensor(gB[:], gF[:], gC[:], ALU.add).then_inc(gate_dve, 1)
            dve.wait_ge(gate_act, 2)
            link(dve.tensor_scalar(rows_m[:, T:2 * T], rows_m[:, T:2 * T], 1e37, None, ALU.min))

            def head_rows_pick(h):
                if not isinstance(h, int) or h > 0:
                    dve.wait_ge(qk_mm, h)
                dve.tensor_scalar(head_rows[:], rows_m[:], ident[0:M_HEADS, bass.ds(h, 1)], None,
                                  ALU.mult).then_inc(rows_ready, 1)

            def head_exponent(h):
                dve.wait_ge(em_ready, h + 1)
                dve.scalar_tensor_tensor(E[:, 0:T], ps[:, 4, 0:T], a_tok[:, 0, bass.ds(h, 1)], neg_future[:],
                                         ALU.add, ALU.add)
                dve.scalar_tensor_tensor(E[:, T:T + P], ps[:, 4, P:T], a_tok[:, 1, bass.ds(h, 1)],
                                         neg_future[:, 0:P], ALU.add, ALU.add).then_inc(e_ready, 1)

            def head_s(h):
                dve.wait_ge(w_ready, h + 1)
                dve.scalar_tensor_tensor(S[:], ps[:, 5, 0:3 * P], float(DK ** -0.5), E[:], ALU.mult,
                                         ALU.mult).then_inc(s_ready, 1)

            def head_o(h):
                dve.wait_ge(og_exp, h + 1)
                link(dve.tensor_scalar(og[:], HG[:], 1.0, None, ALU.add))
                link(dve.reciprocal(og[:], og[:]))

            def head_h(h):
                dve.wait_ge(pv_mm, h + 1)
                link(dve.scalar_tensor_tensor(den[:], ps[:, 7, 0:T], -1.0, em[:], ALU.mult, ALU.max))
                link(dve.tensor_tensor(den[:], ps[:, 7, 0:T], den[:], ALU.max))
                link(dve.reciprocal(den[:], den[:]))
                dve.tensor_tensor(H[:], ps[:, 6].rearrange("p (a t) -> p a t", a=2),
                                  den[:].rearrange("p (a t) -> p a t", a=1).broadcast_to([P, 2, T]),
                                  ALU.mult).then_inc(h_ready, 1)

            def head_mean(h):
                mean(ps[:, 7, T:T + 2], 2, DV, ROOT_HEADS + h)

            def head_gate(h):
                dve.wait_ge(h_ready, h + 1)
                for j in range(2):
                    g = vecs[:, bass.ds(V_HEADG + 2 * h + j, 1)]
                    ins = dve.scalar_tensor_tensor(HG[:, j], H[:, j], g, og[:, j], ALU.mult, ALU.mult)
                link(ins)
                diagonal(2, ROOT_HEADS + h)

            def head_scale(h):
                dve.wait_ge(spread_mm, ROOT_HEADS + h + 1)
                dve.tensor_tensor(HG[:], HG[:], ps[:, 7, T:2 * T].rearrange("p (a t) -> p a t", a=1).broadcast_to([P, 2, T]),
                                  ALU.mult).then_inc(hg_ready, 1)

            def head_lo(h):
                dve.wait_ge(mix_hi, h + 1)
                dve.tensor_tensor(mix[:, bass.ds(2 * h, 2), 1], HG[:], mix[:, bass.ds(2 * h, 2), 0].bitcast(F32),
                                  ALU.subtract).then_inc(mix_ready, 1)

            def head(n, off, c, coff, h, prev):
                for k in range(12):
                    dve_split(dve, n + k + LEAD, off)
                    if prev is not None:
                        if k == 0:
                            head_rows_pick(prev)
                        if k == 1:
                            head_exponent(prev)
                        if k == 2:
                            head_s(prev)
                            head_o(prev)
                        if k == 3:
                            head_h(prev)
                        if k == 5:
                            head_mean(prev)
                        if k == 6:
                            head_gate(prev)
                        if k == 7:
                            head_scale(prev)
                        if k == 8:
                            head_lo(prev)
                    if k % 4 == 3:
                        j = k // 4
                        drain(c + j, coff, 2 * ((c + j) % 2))
                        ins = scaled((QK, vT, og)[j], c + j + 1 + coff)
                        ins.then_inc((qk_ready, vT_ready, og_ready)[j], 1)
                    if prev is None and k == 9:
                        dve.wait_ge(a_turned, 1)
                        link(dve.tensor_copy(a_tok[:].rearrange("p a b -> p (a b)"), ps[:, 5, 0:2 * M_HEADS]))

            head(0, 0, 0, 0, 0, None)

            def two_heads(i):
                head(12, 24 * i, 3, 6 * i, 2 * i + 1, 2 * i)
                head(24, 24 * i, 6, 6 * i, 2 * i + 2, 2 * i + 1)
            loop(3, 2 * 6, two_heads)
            head(84, 0, 21, 0, 7, 6)

            def out_proj(n, d, pre):
                def one(nn, off, dd, doff, tile):
                    b = 2 * (dd % 2)
                    dve.wait_ge(halves_used, nn + 1 + off)
                    xt = X[:, bass.ds(tile, 2)]
                    link(dve.tensor_tensor(xt, ps[:, b:b + 2, 0:T], xt, ALU.add))
                    ins = dve.tensor_tensor(xt, ps[:, b:b + 2, T:2 * T], xt, ALU.add)
                    ins.then_inc(psum_free, 1)
                for j in range(2):
                    for k in range(4):
                        dve_split(dve, n + 4 * j + k + LEAD, 0)
                        for f in pre.get(4 * j + k, ()):
                            f()
                        if 4 * j + k == 5:
                            one(n + 5, 0, d, 0, 0)
                one(n + 7, 0, d + 1, 0, 2)

                def body(i):
                    for j in range(2):
                        for k in range(4):
                            dve_split(dve, n + 8 + 4 * j + k + LEAD, 8 * i)
                            if 4 * j + k == 5:
                                one(n + 13, 8 * i, d + 2, 2 * i, 4 + 4 * i)
                    one(n + 15, 8 * i, d + 3, 2 * i, 6 + 4 * i)
                loop(3, 2, body)

            out_proj(H_WOUT0, D_WOUT0, {
                0: (lambda: head_rows_pick(7), lambda: head_exponent(7), lambda: head_s(7), lambda: head_o(7)),
                1: (lambda: head_h(7),), 2: (lambda: head_mean(7), lambda: head_gate(7)),
                3: (lambda: head_scale(7), lambda: head_lo(7))})

            def ffn(n0, d0, c0, l, done, norm_i, last):
                dve.wait_ge(psum_free, d0)
                norm(norm_i, V_FFNG + KT * l)
                norm_root(norm_i)
                norm_scale(norm_i)

                def conv(dst, tile0, count, signal):
                    dve.wait_ge(tap2_ready, count + 1)
                    for tap in (1, 0):
                        for j in range(2):
                            ins = dve.scalar_tensor_tensor(dst[:, j], pads[:, j, tap:tap + T],
                                                           taps[:, l, tap, bass.ds(tile0 + j, 1)], dst[:, j],
                                                           ALU.mult, ALU.add)
                            if tap == 0 and j == 1 and signal is not None:
                                ins.then_inc(signal, 1)
                            elif j == 1:
                                link(ins)

                def group(n0, off, d0, doff, c0, coff, g):
                    ups = 2 * done + 4 * g
                    for k in range(24):
                        dve_split(dve, n0 + k + LEAD, off)
                        if k < 16 and k % 4 == 3:
                            q = k // 4
                            drain(c0 + q, coff, 2 * q)
                            scaled(pads[:, :, TAPS - 1:], d0 + q + 1 + doff).then_inc(up_ready, 1)
                        if k < 17 and k % 4 == 0 and k:
                            q = k // 4 - 1
                            ab, hq = q % 2, q // 2
                            conv((CA, CB)[ab], ab * (UP_TILES // 2) + g * GROUP + 2 * hq, ups + q,
                                 conv_a if ab == 0 else None)
                            if ab == 1:
                                dve.wait_ge(silu_ready, done + 2 * g + hq + 1)
                                dve.tensor_tensor(G[:], SA[:], CB[:], ALU.mult).then_inc(gated, 1)
                        if k in (9, 17):
                            q = k // 16
                            dve.wait_ge(hid_hi, done + 2 * g + q + 1)
                            dve.tensor_tensor(hid[:, 2 * q:2 * q + 2, 1], G[:], hid[:, 2 * q:2 * q + 2, 0].bitcast(F32),
                                              ALU.subtract).then_inc(hid_ready, 1)
                        if k in (18, 19, 22, 23):
                            u = {18: 0, 19: 1, 22: 2, 23: 3}[k]
                            dve.wait_ge(halves_used, n0 + k + 1 + off)
                            b = 4 * (u % 2)
                            xt = X[:, 4 * u:4 * u + 4]
                            link(dve.tensor_tensor(xt, ps[:, b:b + 4, 0:T], xt, ALU.add))
                            dve.tensor_tensor(xt, ps[:, b:b + 4, T:2 * T], xt, ALU.add).then_inc(psum_free, 1)

                n = GROUPS - 1 if last else GROUPS
                loop(n, 10, lambda g: group(n0, 24 * g, d0, 8 * g, c0, 4 * g, g))
                if last:
                    group(n0 + 24 * n, 0, d0 + 8 * n, 0, c0 + 4 * n, 0, n)

            ffn(H_FFN0, D_FFN0, C_FFN0, 0, 0, 1, False)

            dve.wait_ge(psum_free, D_DSA_QI)
            norm(2, V_MIXG + KT)
            dve.wait_ge(side_hi, 2)
            dve.tensor_tensor(side_w_lo[:, :, 0:80], kw_raw, side_w_hi[:, :, 0:80].bitcast(F32), ALU.subtract)
            dve.tensor_tensor(side_w_lo[:, :, 80:P], kw_raw[:, :, 0:48], side_w_hi[:, :, 80:P].bitcast(F32),
                              ALU.subtract).then_inc(side_split, 1)
            dve.tensor_scalar(qg[:], vecs[:, V_QG:V_QG + 1], float(DH ** -0.5), None, ALU.mult).then_inc(qg_ready, 1)

            def kw_drain():
                dve.wait_ge(side_tail, 2)
                link(dve.tensor_tensor(wiT[0:80], ps[0:80, 4, 0:T], KI[0:80], ALU.add))
                link(dve.tensor_tensor(wiT[0:80], wiT[0:80], rms_scale[0:80], ALU.mult))
                dve.tensor_copy(KI[0:64], wiT[0:64])
                dve.tensor_copy(KI[64:128], wiT[0:64]).then_inc(kw_ready, 1)

            def accumulate(t):
                for b in range(2):
                    w = (b + 1) * P
                    sc = score[:, 0:P] if b == 0 else score[:, P:3 * P]
                    dve.wait_ge(relu_ready, 2 * t + b + 1)
                    for s in range(2):
                        r = relu[:, s, 0:w]
                        wi = WI[:, b, 2 * t + s:2 * t + s + 1]
                        if t == 0 and s == 0:
                            ins = dve.tensor_scalar(sc, r, wi, None, ALU.mult)
                        else:
                            ins = dve.scalar_tensor_tensor(sc, r, wi, sc, ALU.mult, ALU.add)
                        if s == 0:
                            link(ins)
                    ins.then_inc(relu_used, 1)
                    dve.wait_ge(relu_used, 2 * t + b + 1)

            blocks = (slice(0, P), slice(P, 3 * P))

            def topk_round(r):
                for b in range(2):
                    src = score if r == 0 else work
                    link(dve.max(best[:, b], src[:, blocks[b]]))
                    link(dve.match_replace(out=work[:, blocks[b]], in_to_replace=best[:, b], in_values=src[:, blocks[b]],
                                           imm_value=3 * NEG))

            for j in range(5):
                n = H_DSA_QI + 4 * j
                for k in range(4):
                    dve_split(dve, n + k + LEAD, 0)
                    if j == 0 and k == 1:
                        norm_root(2)
                    if j == 1 and k == 0:
                        kw_drain()
                    if j == 1 and k == 1:
                        dve.wait_ge(wi_ready, 1)
                    if j and k in (2, 3):
                        accumulate(2 * (j - 1) + k - 2)
                    if k == 3:
                        if j == 0:
                            norm_scale(2)
                        drain(C_DSA_QI + j, 0, 2 * (j % 2))
                        ins = scaled(QI[:, 2 * j:2 * j + 2] if j < 4 else KV, D_DSA_QI + j + 1)
                        ins.then_inc(qi_ready if j < 4 else kv_ready, 1)
            link(dve.tensor_tensor(score[:], score[:], mask_q[:], ALU.add))

            def k_root():
                dve.wait_ge(va_ready, 1)
                mean(ps[:, 4, 0:2], 2, DH, ROOT_K)
                diagonal(2, ROOT_K)

            def k_norm():
                dve.wait_ge(spread_mm, ROOT_K + 1)
                dve.wait_ge(kv_ready, 1)
                dve.scalar_tensor_tensor(KN[:], KV[:, 0], vecs[:, V_KG:V_KG + 1], ps[:, 4, 0:T], ALU.mult,
                                         ALU.mult).then_inc(kn_ready, 1)

            def select_mask():
                link(dve.tensor_scalar(work[:], work[:], 2 * NEG, NEG, ALU.is_gt, ALU.mult))
                link(dve.tensor_tensor(score[:], work[:], mask_q[:], ALU.add))

            def q_mean(p):
                mean(ps[:, 4, 0:4], 4, DH, ROOT_Q + p)

            def q_norm(p):
                dve.wait_ge(spread_mm, ROOT_Q + p + 1)
                dve.wait_ge(qg_ready, 1)
                dve.scalar_tensor_tensor(QN[:], QT[:], qg[:, 0:1], ps[:, 4].rearrange("p (a t) -> p a t", a=2),
                                         ALU.mult, ALU.mult).then_inc(qn_ready, 1)

            def softmax_in(p):
                dve.wait_ge(logit_mm, p + 1)
                link(dve.tensor_tensor(LM[:], ps[:, 5:7, 0:3 * P],
                                       score[:].rearrange("p (a t) -> p a t", a=1).broadcast_to([P, 2, 3 * P]), ALU.add))
                for b in range(2):
                    ins = dve.tensor_reduce(mx[:, :, b], LM[:, :, blocks[b]], AX.X, ALU.max)
                link(ins)
                dve.tensor_scalar(mx[:], mx[:], -1.0, None, ALU.mult).then_inc(max_ready, 1)

            def inverse(p):
                dve.wait_ge(exp_ready, p + 1)
                dve.reciprocal(sums[:], sums[:]).then_inc(inv_ready, 1)

            def av_lo(p):
                dve.wait_ge(mix_hi, M_HEADS + p + 1)
                dve.tensor_tensor(mix[:, bass.ds(2 * p, 2), 1], ps[:, 7].rearrange("p (a t) -> p a t", a=2),
                                  mix[:, bass.ds(2 * p, 2), 0].bitcast(F32), ALU.subtract).then_inc(mix_ready, 1)

            def q_frame(n, off, d, c, doff, p, one, two, extra=None):
                for k in range(4):
                    dve_split(dve, n + k + LEAD, off)
                    if two and k == 0:
                        softmax_in(p - 2)
                    if two and k == 1:
                        inverse(p - 2)
                    if one and k == 1:
                        q_mean(p - 1)
                    if one and k == 2:
                        diagonal(4, ROOT_Q + p - 1)
                    if extra:
                        extra(k)
                    if two and k == 3:
                        av_lo(p - 2)
                    if one and k == 3:
                        q_norm(p - 1)
                    if k == 3:
                        drain(c, doff, 2 * (d % 2))
                        scaled(QT[:], d + 1 + doff).then_inc(q_ready, 1)

            def frame0(k):
                if k == 1:
                    k_root()
                if k == 3:
                    k_norm()
                topk_round(k)

            q_frame(H_DSA_Q, 0, D_DSA_Q, C_DSA_Q, 0, 0, False, False, frame0)
            q_frame(H_DSA_Q + 4, 0, D_DSA_Q + 1, C_DSA_Q + 1, 0, 1, True, False, lambda k: topk_round(4 + k))
            select_mask()

            def two_pairs(i):
                q_frame(H_DSA_Q + 8, 8 * i, D_DSA_Q + 2, C_DSA_Q + 2, 2 * i, 2 * i + 2, True, True)
                q_frame(H_DSA_Q + 12, 8 * i, D_DSA_Q + 3, C_DSA_Q + 3, 2 * i, 2 * i + 3, True, True)
            loop(3, 4, two_pairs)

            out_proj(H_WOUT1, D_WOUT1, {
                0: (lambda: softmax_in(6), lambda: q_mean(7), lambda: inverse(6), lambda: diagonal(4, ROOT_Q + 7)),
                1: (lambda: av_lo(6), lambda: q_norm(7)), 2: (lambda: softmax_in(7), lambda: inverse(7)),
                3: (lambda: av_lo(7),)})
            ffn(H_FFN1, D_FFN1, C_FFN1, 1, 2 * GROUPS, 3, True)
            for b in range(2):
                for r in range(4):
                    dve.wait_ge(y_turned, 4 * b + r + 1)
                    dve.tensor_copy(x_tok[:, b, 512 * r:512 * (r + 1)], ps[:, 4 * b + r]).then_inc(y_copied, 1)

        @block.gpsimd
        def _(pool):
            pool.dma_start(x_tok, x[0].rearrange("(b p) d -> p b d", p=P)).then_inc(x_in, 16)
            for at, src in ((V_MIXG, mix_norm_g), (V_FFNG, ffn_norm_g), (V_HEADG, mlstm_head_g), (V_QG, dsa_q_g),
                            (V_KG, dsa_k_g)):
                rows = src.shape[0] * src.shape[1] // P
                pool.dma_start(vec_rows[at:at + rows], src.rearrange("l (k p) -> (l k) p", p=P)).then_inc(small_in, 16)
            pool.dma_start(tap_rows, ffn_dw_w.rearrange("l t (j p) -> j (l t) p", p=P)).then_inc(small_in, 16)

            pool.memset(ident[:], 0.0).then_inc(consts_zero, 1)
            pool.memset(neg_future[:], 0.0).then_inc(consts_zero, 1)
            pool.memset(mask_q[:], 0.0).then_inc(consts_zero, 1)
            pool.memset(ones[:], 1.0)
            pool.memset(power[:], -0.5)
            pool.memset(gate_b[:], 0.0).then_inc(gate_zero, 1)
            pool.memset(side_w_hi.bitcast(F32), 0.0)
            pool.memset(side_w_lo.bitcast(F32), 0.0).then_inc(gate_zero, 1)
            pool.wait_ge(consts_zero, 3)
            pool.affine_select(out=ident[:], in_=ident[:], compare_op=ALU.not_equal, fill=1.0, base=0,
                               pattern=[[-1, P]], channel_multiplier=1)
            pool.affine_select(out=neg_future[:], in_=neg_future[:], compare_op=ALU.is_ge, fill=NEG, base=0,
                               pattern=[[1, T]], channel_multiplier=-1)
            for c in (0, 2 * P):
                ins = pool.affine_select(out=mask_q[:, c:c + P], in_=mask_q[:, c:c + P], compare_op=ALU.is_ge, fill=NEG,
                                         base=0, pattern=[[-1, P]], channel_multiplier=1)
            ins.then_inc(consts, 1)

            def inverse_root(number, n):
                pool.wait_ge(mean_ready, number + 1)
                pool.tensor_tensor(root[:, 0:n], mean_sq[:, 0:n], power[:, 0:n], ALU.pow).then_inc(root_ready, 1)

            inverse_root(ROOT_X[0], 2)
            with pool.Fori(0, M_HEADS) as h:
                inverse_root(ROOT_HEADS + h, 2)
            inverse_root(ROOT_X[1], 2)
            pool.dma_start(kw_raw, w_in1[:, :, A_KW:A_KW + 80]).then_inc(kw_in, 16)
            inverse_root(ROOT_X[2], 2)
            inverse_root(ROOT_K, 2)
            with pool.Fori(0, A_HEADS // 2) as p:
                inverse_root(ROOT_Q + p, 4)
            inverse_root(ROOT_X[3], 2)


_INS = ["x", "mix_norm_g", "ffn_norm_g", "mlstm_w_in", "mlstm_gate_b", "mlstm_head_g", "mlstm_w_out", "dsa_w_in",
        "dsa_q_g", "dsa_k_g", "dsa_w_out", "ffn_w_up", "ffn_dw_w", "ffn_w_down"]


def kernel(**inputs):
    import concourse.bacc as bacc
    from concourse.bass_utils import run_bass_kernel_spmd

    nc = bacc.Bacc("TRN2", target_bir_lowering=False, num_devices=1)
    arrays, args = {}, []
    for name in _INS:
        a = np.ascontiguousarray(inputs[name])
        arrays[f"in_{name}"] = a
        args.append(nc.dram_tensor(f"in_{name}", a.shape, mybir.dt.from_np(a.dtype), kind="ExternalInput").ap())
    y = nc.dram_tensor("out_y", (1, T, D), F32, kind="ExternalOutput").ap()
    trunk(nc, *args, y)
    r = run_bass_kernel_spmd(nc, [arrays], core_ids=[0])
    return r.results[0]["out_y"]
```

```python
from contextlib import ExitStack

import numpy as np

import concourse.bass as bass
from concourse import mybir

F32 = mybir.dt.float32
F32R = mybir.dt.float32r
ALU = mybir.AluOpType
ACT = mybir.ActivationFunctionType
AX = mybir.AxisListType

P = 128
T = 256
D = 2048
KT = D // P
EPS = 1e-6
M_HEADS, DK, DV = 8, 128, 256
A_HEADS, DH = 16, 128
I_HEADS, I_DIM = 16, 64
TOPK = T // 4
D_FF = 5632
UP_TILES = 2 * D_FF // P
GROUP = 4
GROUPS = D_FF // P // GROUP
TAPS = 3
NEG = -1e30

BLK = 8
LEAD = 3
RING = 4

H_MLSTM = 0
H_WOUT0 = H_MLSTM + 12 * M_HEADS
H_FFN0 = H_WOUT0 + 2 * KT
H_DSA_QI = H_FFN0 + 24 * GROUPS
H_DSA_KV = H_DSA_QI + 16
H_DSA_Q = H_DSA_KV + 4
H_WOUT1 = H_DSA_Q + 2 * A_HEADS
H_FFN1 = H_WOUT1 + 2 * KT
H_END = H_FFN1 + 24 * GROUPS

D_MLSTM = 0
D_WOUT0 = D_MLSTM + 3 * M_HEADS
D_FFN0 = D_WOUT0 + KT // 2
D_DSA_QI = D_FFN0 + 8 * GROUPS
D_DSA_KV = D_DSA_QI + 4
D_DSA_Q = D_DSA_KV + 1
D_WOUT1 = D_DSA_Q + A_HEADS // 2
D_FFN1 = D_WOUT1 + KT // 2

C_MLSTM = 0
C_FFN0 = C_MLSTM + 3 * M_HEADS
C_DSA_QI = C_FFN0 + 4 * GROUPS
C_DSA_KV = C_DSA_QI + 4
C_DSA_Q = C_DSA_KV + 1
C_FFN1 = C_DSA_Q + A_HEADS // 2

M_K, M_V, M_O, M_GATE = M_HEADS * DK, 2 * M_HEADS * DK, 2 * M_HEADS * DK + M_HEADS * DV, 2 * M_HEADS * (DK + DV)
A_KV, A_QI = A_HEADS * DH, A_HEADS * DH + 2 * DH
A_KW = A_QI + I_HEADS * I_DIM

V_MIXG, V_FFNG, V_HEADG, V_QG, V_KG, V_ROWS = 0, 2 * KT, 4 * KT, 5 * KT, 5 * KT + 1, 5 * KT + 2


ROOT_HEADS = 1
ROOT_X = (0, 1 + M_HEADS, 2 + M_HEADS, 4 + M_HEADS + A_HEADS // 2)
ROOT_K = 3 + M_HEADS
ROOT_Q = 4 + M_HEADS


END = [(0, 0), (0, 1), (1, 0), (1, 1), (0, 2), (1, 2), (0, 3), (1, 3)]


def trunk(nc, x, mix_norm_g, ffn_norm_g, mlstm_w_in, mlstm_gate_b, mlstm_head_g, mlstm_w_out,
          dsa_w_in, dsa_q_g, dsa_k_g, dsa_w_out, ffn_w_up, ffn_dw_w, ffn_w_down, out):
    ctx = ExitStack()
    with ctx:
        def sb(name, shape, dt=F32):
            return ctx.enter_context(nc.sbuf_tensor(name, shape, dt))

        def sem(name):
            return ctx.enter_context(nc.semaphore(name))

        raw = sb("raw", [P, RING, 2 * BLK * P])
        w_hi = sb("w_hi", [P, RING, BLK, P], F32R)
        w_lo = sb("w_lo", [P, RING, BLK, P], F32R)
        X = sb("X", [P, KT, T])
        xs = sb("xs", [P, KT, 2, T], F32R)
        mix = sb("mix", [P, KT, 2, T], F32R)
        hid = sb("hid", [P, GROUP, 2, T], F32R)
        rms_scale = sb("rms_scale", [P, T])
        ident = sb("ident", [P, P])
        ones = sb("ones", [P, T])
        neg_future = sb("neg_future", [P, T])
        mask_q = sb("mask_q", [P, 3 * P])
        vecs = sb("vecs", [P, V_ROWS])
        taps = sb("taps", [P, 2, TAPS, UP_TILES])
        gate_b = sb("gate_b", [40, 1])
        power = sb("power", [P, 4])
        mean_sq = sb("mean_sq", [P, 4])
        root = sb("root", [P, 4])
        diag = sb("diag", [P, 4, P])
        tail = sb("tail", [P, 2, T])
        both = sb("both", [P, 2, T])
        pads = sb("pads", [P, 2, T + TAPS - 1])
        sq = sb("sq", [P, 4, T])
        sq_sum = sb("sq_sum", [P, 4, T])
        scratch = sb("scratch", [P, 7400])

        def part(at, *shape, rows=P):
            n = int(np.prod(shape))
            v = scratch[0:rows, at:at + n]
            if len(shape) == 2:
                v = v.rearrange("p (a b) -> p a b", a=shape[0])
            return v

        x_tok = part(0, 2, D)
        vec_rows = part(4096, P, rows=V_ROWS)
        tap_rows = part(4224, 2 * TAPS, P, rows=UP_TILES)
        QK = part(0, 2, T)
        vT = part(512, 2, T)
        V = part(1024, 2, DV)
        og = part(1536, 2, T)
        rows_m = part(2048, 512, rows=M_HEADS)
        head_rows = part(2560, 512, rows=M_HEADS)
        em = part(3072, T)
        E = part(3328, 3 * P)
        S = part(3712, 3 * P)
        den = part(4096, T)
        H = part(4352, 2, T)
        HG = part(5376, 2, T)
        a_tok = part(5888, 2, M_HEADS)
        gate_raw = part(5904, KT, 16)
        gates = part(6160, T, rows=40)
        gA = part(6416, T, rows=M_HEADS)
        gB = part(6672, T, rows=M_HEADS)
        gC = part(6928, T, rows=M_HEADS)
        gF = part(4352, T, rows=M_HEADS)
        gate_tail = part(4864, T, rows=40)
        kw_raw = part(2048, KT, 80)
        QI = part(1280, 8, T)
        KI = part(3328, T)
        wiT = part(3584, T)
        WI = part(3840, 2, I_HEADS)
        relu = part(3872, 2, T)
        score = part(4384, 3 * P)
        work = part(4768, 3 * P)
        best = part(5152, 2, 8)
        KV = part(5168, 2, T)
        KN = part(5680, T)
        VA = part(5936, 2, DH)
        qg = part(6192, 1)
        QT = part(0, 2, T)
        QN = part(512, 2, T)
        LM = part(2304, 2, 3 * P)
        PT = part(6200, 2, 3 * P)
        mx = part(3072, 2, 2)
        sums = part(3076, 2, 2)
        CA = part(0, 2, T)
        CB = part(512, 2, T)
        SA = part(1024, 2, T)
        G = part(1536, 2, T)
        down_tail = [part(3328 + 1024 * j, 4, T) for j in range(2)]

        side_w = [mix[:, 4 * j:4 * j + 4].rearrange("p a b t -> p (a b t)").rearrange("p (k c) -> p k c", k=KT)
                  for j in range(2)]
        side_w_hi, side_w_lo = side_w

        ps = ctx.enter_context(nc.psum_tensor("ps", [P, 8, 512], F32))

        load_done = [sem(f"load_done{i}") for i in range(RING)]
        halves_hi = sem("halves_hi")
        halves_split = sem("halves_split")
        pool_split = sem("pool_split")
        halves_used = sem("halves_used")
        psum_free = sem("psum_free")
        tails = sem("tails")
        chain = sem("chain")
        act_chain = sem("act_chain")
        small_in = sem("small_in")
        x_in = sem("x_in")
        gate_in = sem("gate_in")
        kw_in = sem("kw_in")
        consts_zero = sem("consts_zero")
        ident_ready = sem("ident_ready")
        consts = sem("consts")
        fills = sem("fills")
        x_turned = sem("x_turned")
        x_copied = sem("x_copied")
        vecs_turned = sem("vecs_turned")
        vecs_ready = sem("vecs_ready")
        qk_ready = sem("qk_ready")
        xs_hi = sem("xs_hi")
        squares = sem("squares")
        squares_used = sem("squares_used")
        xs_ready = sem("xs_ready")
        sq_ready = sem("sq_ready")
        sums_mm = sem("sums_mm")
        mean_ready = sem("mean_ready")
        root_ready = sem("root_ready")
        diag_ready = sem("diag_ready")
        spread_mm = sem("spread_mm")
        side_hi = sem("side_hi")
        side_split = sem("side_split")
        side_mm = sem("side_mm")
        side_tail = sem("side_tail")
        gate_zero = sem("gate_zero")
        gate_dve = sem("gate_dve")
        gate_act = sem("gate_act")
        a_ready = sem("a_ready")
        a_turned = sem("a_turned")
        vT_ready = sem("vT_ready")
        v_turned = sem("v_turned")
        v_ready = sem("v_ready")
        og_ready = sem("og_ready")
        og_sigmoid = sem("og_sigmoid")
        rows_ready = sem("rows_ready")
        qk_mm = sem("qk_mm")
        em_ready = sem("em_ready")
        e_ready = sem("e_ready")
        w_ready = sem("w_ready")
        s_ready = sem("s_ready")
        pv_mm = sem("pv_mm")
        h_ready = sem("h_ready")
        h_sq = sem("h_sq")
        hg_ready = sem("hg_ready")
        mix_hi = sem("mix_hi")
        mix_ready = sem("mix_ready")
        kw_ready = sem("kw_ready")
        wi_turned = sem("wi_turned")
        wi_ready = sem("wi_ready")
        qi_ready = sem("qi_ready")
        score_mm = sem("score_mm")
        relu_ready = sem("relu_ready")
        relu_used = sem("relu_used")
        kv_ready = sem("kv_ready")
        kv_sq = sem("kv_sq")
        kv_mm = sem("kv_mm")
        va_ready = sem("va_ready")
        kn_ready = sem("kn_ready")
        qg_ready = sem("qg_ready")
        q_ready = sem("q_ready")
        q_sq = sem("q_sq")
        qn_ready = sem("qn_ready")
        logit_mm = sem("logit_mm")
        max_ready = sem("max_ready")
        exp_ready = sem("exp_ready")
        inv_ready = sem("inv_ready")
        probs_ready = sem("probs_ready")
        probs_turned = sem("probs_turned")
        pt_ready = sem("pt_ready")
        av_mm = sem("av_mm")
        up_ready = sem("up_ready")
        tap2_ready = sem("tap2_ready")
        conv_a = sem("conv_a")
        silu_ready = sem("silu_ready")
        gated = sem("gated")
        hid_hi = sem("hid_hi")
        hid_ready = sem("hid_ready")
        tile_tail = sem("tile_tail")
        tile_gated = sem("tile_gated")
        tile_hi = sem("tile_hi")
        tile_lo = sem("tile_lo")
        down_tails = sem("down_tails")
        x_added = sem("x_added")
        y_turned = sem("y_turned")
        y_copied_even = sem("y_copied_even")
        y_copied_odd = sem("y_copied_odd")
        stored = sem("stored")

        block = ctx.enter_context(nc.Block())

        w_in0 = mlstm_w_in[0].rearrange("(k p) n -> p k n", p=P)
        w_in1 = dsa_w_in[0].rearrange("(k p) n -> p k n", p=P)
        w_out = [mlstm_w_out[0].rearrange("(k p) n -> p k n", p=P), dsa_w_out[0].rearrange("(k p) n -> p k n", p=P)]
        w_up = [ffn_w_up[l].rearrange("(k p) n -> p k n", p=P) for l in range(2)]
        w_down = [ffn_w_down[l].rearrange("(k p) n -> p k n", p=P) for l in range(2)]

        @block.sync
        def _(sp):
            def load(base, per, i, c, src, cols):
                first = base + c
                number = first + per * i
                assert per % RING == 0
                if first >= RING:
                    sp.wait_ge(halves_split, 2 * (number - RING) + 2)
                dst = raw[:, first % RING].rearrange("p (k n) -> p k n", n=cols)
                sp.dma_start(dst, src).then_inc(load_done[first % RING], 16)

            def pair(base, per, i, c, w, col):
                for hf in range(2):
                    load(base, per, i, c + hf, w[:, BLK * hf:BLK * hf + BLK, bass.ds(col, 2 * P)], 2 * P)

            def two_pairs(base, i, w):
                for hf in range(2):
                    for q in range(2):
                        load(base, 4, i, 2 * hf + q, w[:, BLK * hf:BLK * hf + BLK, bass.ds((2 * i + q) * 2 * P, 2 * P)], 2 * P)

            def head(base, per, i, c, h):
                load(base, per, i, c, w_in0[:, :, bass.ds(h * DK, DK)], DK)
                load(base, per, i, c + 1, w_in0[:, :, bass.ds(M_K + h * DK, DK)], DK)
                pair(base, per, i, c + 2, w_in0, M_V + h * DV)
                pair(base, per, i, c + 4, w_in0, M_O + h * DV)

            def ffn(base, l):
                def group(b, i, g):
                    c = 0
                    for q in range(2):
                        for ab in range(2):
                            pair(b, 12, i, c, w_up[l], ab * D_FF + g * GROUP * P + q * 2 * P)
                            c += 2
                    for q in range(2):
                        for kk in range(2):
                            load(b, 12, i, c, w_down[l][:, bass.ds(g * GROUP + 2 * kk, 2), q * 1024:q * 1024 + 1024], 1024)
                            c += 1
                with sp.Fori(0, GROUPS) as g:
                    group(base, g, g)

            for at, src in ((V_MIXG, mix_norm_g), (V_FFNG, ffn_norm_g), (V_HEADG, mlstm_head_g), (V_QG, dsa_q_g),
                            (V_KG, dsa_k_g)):
                rows = src.shape[0] * src.shape[1] // P
                sp.dma_start(vec_rows[at:at + rows], src.rearrange("l (k p) -> (l k) p", p=P)).then_inc(small_in, 16)
            sp.dma_start(tap_rows, ffn_dw_w.rearrange("l t (j p) -> j (l t) p", p=P)).then_inc(small_in, 16)
            sp.dma_start(gate_raw, w_in0[:, :, M_GATE:M_GATE + 16]).then_inc(gate_in, 16)
            head(0, 12, 0, 0, 0)
            with sp.Fori(0, 3) as i:
                head(6, 12, i, 0, 2 * i + 1)
                head(6, 12, i, 6, 2 * i + 2)
            head(42, 12, 0, 0, 7)
            with sp.Fori(0, 4) as i:
                two_pairs(H_WOUT0 // 2, i, w_out[0])
            ffn(H_FFN0 // 2, 0)
            with sp.Fori(0, 2) as i:
                pair(H_DSA_QI // 2, 4, i, 0, w_in1, A_QI + i * 4 * P)
                pair(H_DSA_QI // 2, 4, i, 2, w_in1, A_QI + i * 4 * P + 2 * P)
            pair(H_DSA_KV // 2, 4, 0, 0, w_in1, A_KV)
            with sp.Fori(0, 4) as i:
                pair(H_DSA_Q // 2, 4, i, 0, w_in1, i * 4 * P)
                pair(H_DSA_Q // 2, 4, i, 2, w_in1, i * 4 * P + 2 * P)
            with sp.Fori(0, 4) as i:
                two_pairs(H_WOUT1 // 2, i, w_out[1])
            ffn(H_FFN1 // 2, 1)
            for j in range(len(END)):
                b, r = END[j]
                sp.wait_ge((y_copied_even, y_copied_odd)[j % 2], j // 2 + 1)
                sp.dma_start(out[0, b * P:(b + 1) * P, 512 * r:512 * (r + 1)],
                             x_tok[:, b, 512 * r:512 * (r + 1)]).then_inc(stored, 16)
            sp.wait_ge(stored, 16 * len(END))

        PAIR, UNIT, DOWN = range(3)

        def layout(n):
            if n < H_WOUT0:
                return UNIT if n % 12 < 4 else PAIR
            for base in (H_FFN0, H_FFN1):
                if base <= n < base + 24 * GROUPS and (n - base) % 24 >= 16:
                    return DOWN
            return PAIR

        def raw_half(n):
            slot, j = n // 2 % RING, n % 2
            if layout(n) == UNIT:
                return raw[:, slot].rearrange("p (j k n) -> p j k n", j=2, k=BLK)[:, j]
            return raw[:, slot].rearrange("p (k u n) -> p k u n", k=2 if layout(n) == DOWN else BLK, u=2)[:, :, j]

        def split_half(t, n):
            v = t[:, n % RING]
            return v.rearrange("p (k d) n -> p k (d n)", k=2) if layout(n) == DOWN else v

        def act_split(act, n, off):
            if n >= H_END:
                return
            load = n // 2
            act.wait_ge(load_done[load % RING], 16 * (load // RING + 1) + off * 2)
            if n >= RING:
                act.wait_ge(halves_used, n - RING + 1 + off)
            act.activation(split_half(w_hi, n), raw_half(n), ACT.Copy).then_inc(halves_hi, 1)

        def dve_split(dve, n, off, more=0):
            if n >= H_END:
                return
            dve.wait_ge(halves_hi, n + 1 + off)
            dve.tensor_tensor(split_half(w_lo, n), raw_half(n), split_half(w_hi, n).bitcast(F32), ALU.subtract).then_inc(halves_split, 1 + more)

        def norm_add(engine, i):
            for r in range(4):
                engine.wait_ge(squares, 4 * i + r + 1)
                if r == 0:
                    ins = engine.tensor_copy(sq_sum[:], sq[:])
                else:
                    engine.wait_ge(squares_used, 4 * i + r)
                    ins = engine.tensor_tensor(sq_sum[:], sq_sum[:], sq[:], ALU.add)
                ins.then_inc(squares_used, 1)

        @block.tensor
        def _(pe):
            def hi_lo(bank, wh, wl, mv, first, last):
                def wide():
                    return pe.matmul(ps[:, bank], wh, mv.rearrange("p a t -> p (a t)"), start=first, stop=last)

                def narrow():
                    pe.matmul(ps[:, bank, 0:T], wl, mv[:, 0], start=False, stop=False, skip_group_check=True)
                if first:
                    wide()
                    narrow()
                    return None
                narrow()
                return wide()

            def half(n, off, j, bank, mv, within=None):
                pe.wait_ge(halves_split, n + 1 + off)
                for b in range(BLK):
                    if within and within[0] == b:
                        within[1]()
                    k = BLK * j + b
                    mm = hi_lo(bank, w_hi[:, n % RING, b], w_lo[:, n % RING, b], mv[:, k], k == 0, k == KT - 1)
                mm.then_inc(halves_used, 1)

            def pair(n, off, d, doff, mv, before=(None,) * 4, wait_mv=None):
                bank = 2 * (d % 2)
                if d >= 2:
                    pe.wait_ge(psum_free, d - 1 + doff)
                for c in range(4):
                    if before[c]:
                        before[c]()
                    unit, j = (c // 2, c % 2) if layout(n) == UNIT else (c % 2, c // 2)
                    half(n + c, off, j, bank + unit, mv, wait_mv and wait_mv(c))

            def sums(bank, at, columns):
                for c, tiles in enumerate(columns):
                    for j, t in enumerate(tiles):
                        mm = pe.matmul(ps[:, bank, at + c:at + c + 1], t, ones[:, 0:1], start=j == 0,
                                       stop=j == len(tiles) - 1)
                mm.then_inc(sums_mm, 1)

            def spread(bank, at, n, number):
                pe.wait_ge(diag_ready, number + 1)
                pe.matmul(ps[:, bank, at:at + n * P], ones[:, 0:P], diag[:, 0:n].rearrange("p a t -> p (a t)"),
                          start=True, stop=True).then_inc(spread_mm, 1)

            def norm_sum(i):
                pe.wait_ge(sq_ready, i + 1)
                if i:
                    pe.wait_ge(psum_free, (None, D_FFN0, D_DSA_QI, D_FFN1)[i])
                sums(7, 0, [[sq_sum[:, 0, 0:P]], [sq_sum[:, 0, P:T]]])

            def norm_spread(i):
                spread(7, 0, 2, ROOT_X[i])

            def xs_wait(i):
                def w(c):
                    if c in (0, 2):
                        pe.wait_ge(xs_ready, 4 * i + c + 1)
                        return (4, lambda: pe.wait_ge(xs_ready, 4 * i + c + 2))
                return w

            pe.wait_ge(ident_ready, 1)
            pe.wait_ge(small_in, 96)
            pe.transpose(ps[:, 0, 0:V_ROWS], vec_rows, ident[0:V_ROWS, 0:V_ROWS])
            for l in range(2):
                for t in range(TAPS):
                    mm = pe.transpose(ps[:, 1 + l, t * UP_TILES:(t + 1) * UP_TILES], tap_rows[:, l * TAPS + t],
                                      ident[0:UP_TILES, 0:UP_TILES])
            mm.then_inc(vecs_turned, 1)
            pe.wait_ge(x_in, 32)
            pe.wait_ge(fills, 1)
            pe.wait_ge(vecs_ready, 1)
            for r in range(KT // 2):
                for kk in range(2):
                    for b in range(2):
                        k = 2 * r + kk
                        mm = pe.transpose(ps[:, r, kk * T + b * P:kk * T + (b + 1) * P],
                                          x_tok[:, b, k * P:(k + 1) * P], ident[:])
                mm.then_inc(x_turned, 1)

            pe.wait_ge(x_copied, KT // 2)
            pe.wait_ge(side_split, 1)
            for k in range(KT):
                if k % 4 == 0:
                    pe.wait_ge(xs_ready, k // 4 + 1)
                mm = hi_lo(4, side_w_hi[:, k], side_w_lo[:, k], xs[:, k], k == 0, k == KT - 1)
            mm.then_inc(side_mm, 1)

            def causal(bank, c, v0, v1, s):
                pe.matmul(ps[:, bank, c:c + P], v0, s[:, 0:P], start=True, stop=True)
                pe.matmul(ps[:, bank, c + P:c + T], v0, s[:, P:T], start=True, stop=False)
                return pe.matmul(ps[:, bank, c + P:c + T], v1, s[:, T:T + P], start=False, stop=True)

            def head_scores(h):
                pe.wait_ge(rows_ready, h + 1)
                pe.wait_ge(qk_ready, h + 1)
                pe.wait_ge(v_ready, h + 1)
                pe.matmul(ps[:, 4], ones[0:M_HEADS, 0:P], head_rows, start=True, stop=True)
                pe.matmul(ps[:, 5, 0:T], QK[:, 1, 0:P], QK[:, 0], start=True, stop=True)
                pe.matmul(ps[:, 5, T:T + P], QK[:, 1, P:T], QK[:, 0, P:T], start=True, stop=True).then_inc(qk_mm, 1)

            def head_values(h):
                pe.wait_ge(s_ready, h + 1)
                for j in range(2):
                    causal(6, j * T, V[:, 0, j * P:(j + 1) * P], V[:, 1, j * P:(j + 1) * P], S)
                causal(7, 0, ones[:, 0:P], ones[:, 0:P], S).then_inc(pv_mm, 1)

            def head_square(h):
                pe.wait_ge(h_sq, h + 1)
                sums(7, T, [[sq[:, j, b * P:(b + 1) * P] for j in range(2)] for b in range(2)])

            def head_turn_v(h):
                pe.wait_ge(vT_ready, h + 1)
                for s in range(2):
                    for j in range(2):
                        mm = pe.transpose(ps[:, 4, s * DV + j * P:s * DV + (j + 1) * P],
                                          vT[:, j, s * P:(s + 1) * P], ident[:])
                mm.then_inc(v_turned, 1)

            def head(n, off, d, doff, h, prev):
                a = [None] * 12
                if prev is not None:
                    a[1] = lambda: head_scores(prev)
                    a[4] = lambda: head_values(prev)
                    a[6] = lambda: head_square(prev)
                    a[8] = lambda: spread(7, T, 2, ROOT_HEADS + prev)
                a[10] = lambda: head_turn_v(h)
                for c in range(3):
                    pair(n + 4 * c, off, d + c, doff, xs, a[4 * c:4 * c + 4])

            def turn_a():
                pe.wait_ge(a_ready, 1)
                for b in range(2):
                    mm = pe.transpose(ps[:, 5, b * M_HEADS:(b + 1) * M_HEADS], gA[:, b * P:(b + 1) * P],
                                      ident[0:M_HEADS, 0:M_HEADS])
                mm.then_inc(a_turned, 1)

            pair(0, 0, 0, 0, xs)
            pair(4, 0, 1, 0, xs, (lambda: norm_sum(0), lambda: norm_spread(0), None, None))
            pair(8, 0, 2, 0, xs, (None, turn_a, lambda: head_turn_v(0), None))
            with pe.Fori(0, 3) as i:
                head(12, 24 * i, 3, 6 * i, 2 * i + 1, 2 * i)
                head(24, 24 * i, 6, 6 * i, 2 * i + 2, 2 * i + 1)
            head(84, 0, 21, 0, 7, 6)

            def out_proj(n, d, steps):
                def two_pairs(n, off, d, doff, steps):
                    for c in range(8):
                        if c in (0, 2):
                            pe.wait_ge(psum_free, d + c // 2 - 1 + doff)
                        for f in steps.get(c, ()):
                            f()
                        half(n + c, off, c // 4, 2 * ((d + c % 4 // 2) % 2) + c % 2, mix,
                             (6, steps["last"]) if c == 4 and steps else None)
                two_pairs(n, 0, d, 0, steps)
                with pe.Fori(0, 3) as i:
                    two_pairs(n + 8, 8 * i, d + 2, 2 * i, {})

            def mixed(count):
                return lambda: pe.wait_ge(mix_ready, count)

            out_proj(H_WOUT0, D_WOUT0, {
                0: (lambda: head_scores(7), mixed(M_HEADS // 2)), 1: (lambda: head_values(7),),
                2: (lambda: head_square(7),), 4: (lambda: spread(7, T, 2, ROOT_HEADS + 7), mixed(M_HEADS - 1)),
                "last": mixed(M_HEADS)})

            def ffn(n0, d0, norm, done):
                def group(n0, off, d0, doff, g, peel):
                    for q in range(4):
                        if peel and q == 0:
                            pe.wait_ge(psum_free, d0 - 1 + d0 % 2)
                        else:
                            pe.wait_ge(psum_free, d0 + (-1, 0, 0, 1)[q] + doff)
                        for c in range(4):
                            if peel and q == 1 and c == 0:
                                norm_sum(norm)
                            if peel and q == 1 and c == 1:
                                norm_spread(norm)
                            half(n0 + 4 * q + c, off, c // 2, 2 * q + c % 2, xs,
                                 xs_wait(norm)(c) if peel and q == 0 else None)
                    for q in range(2):
                        for kk in range(2):
                            if q == 0 and kk == 0:
                                pe.wait_ge(hid_ready, done + 2 * g + 1)
                            if q == 0 and kk == 1:
                                pe.wait_ge(tile_lo, done // 2 + g + 1)
                            for u in range(2):
                                n = n0 + 16 + 4 * q + 2 * kk + u
                                if kk == 0:
                                    pe.wait_ge(psum_free, d0 + (2, 4, 5, 6)[2 * q + u] + doff)
                                if (q, kk, u) == (0, 1, 0):
                                    pe.wait_ge(pool_split, done + 2 * g + 1)
                                elif (q, kk, u) == (1, 0, 0):
                                    pe.wait_ge(pool_split, done + 2 * g + 2)
                                else:
                                    pe.wait_ge(halves_split, n + 1 + off)
                                for k2 in range(2):
                                    if q == 0 and kk == 1 and k2 == 1 and u == 0:
                                        pe.wait_ge(hid_ready, done + 2 * g + 2)
                                    for dt in range(4):
                                        b = 4 * k2 + dt
                                        mm = hi_lo(4 * u + dt, w_hi[:, n % RING, b], w_lo[:, n % RING, b],
                                                   hid[:, 2 * kk + k2], kk == 0 and k2 == 0, kk == 1 and k2 == 1)
                                mm.then_inc(halves_used, 1)

                group(n0, 0, d0, 0, 0, True)
                with pe.Fori(1, GROUPS) as g:
                    group(n0 + 24, 24 * g - 24, d0 + 8, 8 * g - 8, g, False)

            ffn(H_FFN0, D_FFN0, 1, 0)

            def kw_unit():
                pe.wait_ge(side_split, 2)
                pe.wait_ge(psum_free, D_DSA_QI)
                for k in range(KT):
                    mm = hi_lo(4, side_w_hi[:, k], side_w_lo[:, k], xs[:, k], k == 0, k == KT - 1)
                mm.then_inc(side_mm, 1)

            def turn_wi():
                pe.wait_ge(kw_ready, 1)
                for b in range(2):
                    mm = pe.transpose(ps[:, 7, b * I_HEADS:(b + 1) * I_HEADS], wiT[64:80, b * P:(b + 1) * P],
                                      ident[64:80, 64:80])
                mm.then_inc(wi_turned, 1)

            def scores(t):
                pe.wait_ge(qi_ready, t // 2 + 1)
                pe.wait_ge(kw_ready, 1)
                pe.wait_ge(wi_ready, 1)
                if t:
                    pe.wait_ge(relu_ready, 2 * t)
                for b in range(2):
                    w = (b + 1) * P
                    for s in range(2):
                        mm = pe.matmul(ps[:, 4 + 2 * b + s, 0:w], QI[64 * s:64 * s + 64, t, b * P:(b + 1) * P],
                                       KI[64 * s:64 * s + 64, 0:w], start=True, stop=True)
                    mm.then_inc(score_mm, 1)

            for j in range(4):
                t = 2 * (j - 1)
                if j == 0:
                    pair(H_DSA_QI, 0, D_DSA_QI, 0, xs, wait_mv=xs_wait(2))
                    norm_sum(2)
                    kw_unit()
                    norm_spread(2)
                else:
                    pair(H_DSA_QI + 4 * j, 0, D_DSA_QI + j, 0, xs,
                         (None, (lambda: turn_wi()) if j == 1 else None, lambda t=t: scores(t), lambda t=t: scores(t + 1)))

            def kv_sum():
                pe.wait_ge(kv_sq, 1)
                sums(4, 0, [[sq[:, 0, b * P:(b + 1) * P]] for b in range(2)])
                for s in range(2):
                    mm = pe.transpose(ps[:, 4, T + s * P:T + (s + 1) * P], KV[:, 1, s * P:(s + 1) * P], ident[:])
                mm.then_inc(kv_mm, 1)

            def q_sum(p):
                pe.wait_ge(q_sq, p + 1)
                sums(4, 0, [[sq[:, a, b * P:(b + 1) * P]] for a in range(2) for b in range(2)])

            def q_spread(p):
                spread(4, 0, 4, ROOT_Q + p)

            def logits(p):
                pe.wait_ge(qn_ready, p + 1)
                pe.wait_ge(kn_ready, 1)
                if not isinstance(p, int) or p > 0:
                    pe.wait_ge(pt_ready, p)
                for a in range(2):
                    pe.matmul(ps[:, 5 + a, 0:P], QN[:, a, 0:P], KN[:, 0:P], start=True, stop=True)
                    mm = pe.matmul(ps[:, 5 + a, P:3 * P], QN[:, a, P:T], KN[:], start=True, stop=True)
                mm.then_inc(logit_mm, 1)

            def turn_probs(p):
                pe.wait_ge(probs_ready, p + 1)
                if not isinstance(p, int) or p > 0:
                    pe.wait_ge(mix_ready, M_HEADS + p)
                for a, bank in ((0, 7), (1, 5)):
                    for c in range(3):
                        mm = pe.transpose(ps[:, bank, c * P:(c + 1) * P], LM[:, a, c * P:(c + 1) * P], ident[:])
                mm.then_inc(probs_turned, 1)

            def values(p):
                pe.wait_ge(pt_ready, p + 1)
                pe.wait_ge(va_ready, 1)
                for a in range(2):
                    mm = causal(7, a * T, VA[:, 0], VA[:, 1], PT[:, a])
                mm.then_inc(av_mm, 1)

            pair(H_DSA_KV, 0, D_DSA_KV, 0, xs, (None, None, lambda: scores(6), lambda: scores(7)))
            pair(H_DSA_Q, 0, D_DSA_Q, 0, xs, (None, kv_sum, None, lambda: spread(4, 0, 2, ROOT_K)))

            def q_frame(n, off, d, doff, p, lags=3):
                def before_half(c):
                    def f():
                        if c == 0 and lags > 2:
                            turn_probs(p - 3)
                        if c == 1 and lags > 1:
                            logits(p - 2)
                        if c == 1:
                            q_sum(p - 1)
                        if c == 2 and lags > 2:
                            values(p - 3)
                        if c == 3:
                            q_spread(p - 1)
                    return f
                pair(n, off, d, doff, xs, [before_half(c) for c in range(4)])

            for p in range(1, 4):
                q_frame(H_DSA_Q + 4 * p, 0, D_DSA_Q + p, 0, p, p)
            with pe.Fori(0, 2) as i:
                q_frame(H_DSA_Q + 16, 8 * i, D_DSA_Q + 4, 2 * i, 2 * i + 4)
                q_frame(H_DSA_Q + 20, 8 * i, D_DSA_Q + 5, 2 * i, 2 * i + 5)

            out_proj(H_WOUT1, D_WOUT1, {
                0: (lambda: turn_probs(5), mixed(M_HEADS + 4)), 1: (lambda: logits(6), lambda: q_sum(7)),
                2: (lambda: values(5),), 3: (lambda: q_spread(7), lambda: turn_probs(6), lambda: logits(7)),
                4: (lambda: values(6), lambda: turn_probs(7), lambda: values(7), mixed(M_HEADS + 7)),
                "last": mixed(M_HEADS + 8)})
            ffn(H_FFN1, D_FFN1, 3, 2 * GROUPS)

            for b, r in END:
                pe.wait_ge(x_added, 8 * GROUPS - 3 + r)
                pe.wait_ge(psum_free, D_FFN1 + 8 * GROUPS - 1 + b)
                for k in range(4):
                    mm = pe.transpose(ps[:, 4 * b + r, k * P:(k + 1) * P], X[:, 4 * r + k, b * P:(b + 1) * P], ident[:])
                mm.then_inc(y_turned, 1)

        @block.scalar
        def _(act):
            def tail_copy(n, off, d, c, coff, doff, bank):
                act.wait_ge(halves_used, n + 1 + off)
                if c > 0:
                    act.wait_ge(psum_free, d + doff)
                act.activation(tail[:], ps[:, bank:bank + 2, T:2 * T], ACT.Copy).then_inc(tails, 1)

            def norm_hi(i, g0, r):
                for k in range(4):
                    ins = act.activation(xs[:, bass.ds(4 * r + k, 1), 0], X[:, bass.ds(4 * r + k, 1)], ACT.Copy,
                                         scale=vecs[:, bass.ds(g0 + 4 * r + k, 1)])
                ins.then_inc(xs_hi, 1)

            def sq_free(i, r):
                if not isinstance(r, int) or i + r > 0:
                    act.wait_ge(squares_used, 4 * i + r)

            def norm_sq(i, r):
                if isinstance(r, int):
                    sq_free(i, r)
                act.activation(sq[:], X[:, bass.ds(4 * r, 4)], ACT.Square).then_inc(squares, 1)

            for b in range(2):
                act.dma_start(x_tok[:, b], x[0, b * P:(b + 1) * P, :]).then_inc(x_in, 16)
            act.wait_ge(gate_zero, 1)
            act.dma_start(gate_b[0:8, :], mlstm_gate_b[0, 0:8].rearrange("(p a) -> p a", a=1)).then_inc(gate_in, 16)
            act.dma_start(gate_b[32:40, :], mlstm_gate_b[0, 8:16].rearrange("(p a) -> p a", a=1)).then_inc(gate_in, 16)
            act.wait_ge(gate_in, 48)
            act.wait_ge(gate_zero, 2)
            act.activation(side_w_hi[:, :, 0:8], gate_raw[:, :, 0:8], ACT.Copy)
            act.activation(side_w_hi[:, :, 32:40], gate_raw[:, :, 8:16], ACT.Copy).then_inc(side_hi, 1)
            act.wait_ge(vecs_ready, 1)
            for r in range(4):
                act.wait_ge(x_copied, 2 * r + 2)
                norm_hi(0, V_MIXG, r)
            for n in range(LEAD):
                act_split(act, n, 0)
            for r in range(4):
                norm_sq(0, r)
            act.wait_ge(side_mm, 1)
            act.activation(gate_tail, ps[0:40, 4, T:2 * T], ACT.Copy).then_inc(side_tail, 1)

            def gates_softplus():
                act.wait_ge(gate_dve, 1)
                act.activation(gC[:], gB[:], ACT.Exp, scale=-1.0).then_inc(act_chain, 1)
                act.wait_ge(act_chain, 1)
                act.activation(gC[:], gC[:], ACT.Ln, bias=1.0).then_inc(gate_act, 1)

            def gates_exp():
                act.wait_ge(gate_dve, 2)
                act.activation(rows_m[:, T:2 * T], gB[:], ACT.Exp, scale=-1.0).then_inc(gate_act, 1)

            def output_gate(h):
                act.wait_ge(og_ready, h + 1)
                act.activation(og[:], og[:], ACT.Sigmoid).then_inc(og_sigmoid, 1)

            def head_weights(h):
                act.wait_ge(qk_mm, h + 1)
                act.activation(em[:], ps[:, 4, T:2 * T], ACT.Copy).then_inc(em_ready, 1)
                act.wait_ge(e_ready, h + 1)
                act.activation(E[:], E[:], ACT.Exp).then_inc(w_ready, 1)

            def head_squares(h):
                act.wait_ge(h_ready, h + 1)
                act.activation(sq[:, 0:2], H[:], ACT.Square).then_inc(h_sq, 1)

            def head_hi(h):
                act.wait_ge(hg_ready, h + 1)
                act.activation(mix[:, bass.ds(2 * h, 2), 0], HG[:], ACT.Copy).then_inc(mix_hi, 1)

            def head_v(h):
                act.wait_ge(v_turned, h + 1)
                act.activation(V[:].rearrange("p a b -> p (a b)"), ps[:, 4], ACT.Copy).then_inc(v_ready, 1)

            def head(n, off, c, coff, h, prev):
                bank0 = c % 2
                for k in range(12):
                    act_split(act, n + k + LEAD, off)
                    if prev is None and k == 5:
                        gates_softplus()
                    if prev is None and k == 7:
                        gates_exp()
                    if prev is not None:
                        if k == 0:
                            output_gate(prev)
                        if k == 1:
                            head_weights(prev)
                        if k == 4:
                            head_squares(prev)
                    if k % 4 == 3:
                        j = k // 4
                        tail_copy(n + k, off, c + j, c + j, coff, coff, 2 * ((c + j) % 2))
                    if prev is not None and k == 9:
                        head_hi(prev)
                    if k == 10:
                        head_v(h)

            head(0, 0, 0, 0, 0, None)
            with act.Fori(0, 3) as i:
                head(12, 24 * i, 3, 6 * i, 2 * i + 1, 2 * i)
                head(24, 24 * i, 6, 6 * i, 2 * i + 2, 2 * i + 1)
            head(84, 0, 21, 0, 7, 6)

            def out_proj(n, d, i_norm, g0, pre):
                for k in range(8):
                    act_split(act, n + k + LEAD, 0)
                    for f in pre.get(k, ()):
                        f()
                with act.Fori(0, 3) as i:
                    for k in range(8):
                        if k == 1:
                            act.wait_ge(psum_free, d + 2 + 2 * i)
                        if k == 2:
                            sq_free(i_norm, i)
                        act_split(act, n + 8 + k + LEAD, 8 * i)
                        if k == 1:
                            norm_hi(i_norm, g0, i)
                        if k == 2:
                            norm_sq(i_norm, i)
                act.wait_ge(psum_free, d + 8)
                norm_hi(i_norm, g0, 3)

            out_proj(H_WOUT0, D_WOUT0, 1, V_FFNG, {0: (lambda: output_gate(7), lambda: head_weights(7)), 1: (lambda: head_squares(7),),
                               3: (lambda: head_hi(7),)})

            def ffn(n0, d0, c0, l, done, norm_i):
                def tap2(dst, tile0):
                    for j in range(2):
                        ins = act.activation(dst[:, j], pads[:, j, TAPS - 1:], ACT.Copy,
                                             scale=taps[:, l, 2, bass.ds(tile0 + j, 1)])
                    ins.then_inc(tap2_ready, 1)

                def group(n0, off, d0, doff, c0, coff, g, first=False, last=False):
                    pairs = done + 2 * g
                    a_tile = g * GROUP
                    b_tile = UP_TILES // 2 + g * GROUP
                    for k in range(24):
                        if k == 15:
                            act.wait_ge(halves_used, n0 + 15 + off)
                            act.wait_ge(psum_free, d0 + 3 + doff)
                            act.activation(tail[:, 0], ps[:, 6, T:2 * T], ACT.Copy).then_inc(tile_tail, 1)
                        if k == 16:
                            act.wait_ge(halves_used, n0 + 16 + off)
                            act.activation(tail[:, 1], ps[:, 7, T:2 * T], ACT.Copy).then_inc(tails, 1)
                            act.wait_ge(tile_gated, done // 2 + g + 1)
                            act.activation(hid[:, 2, 0], G[:, 0], ACT.Copy).then_inc(tile_hi, 1)
                            act.wait_ge(gated, pairs + 2)
                            act.activation(hid[:, 3, 0], G[:, 1], ACT.Copy).then_inc(hid_hi, 1)
                        act_split(act, n0 + k + LEAD, off)
                        if k in (3, 7, 11):
                            q = k // 4
                            tail_copy(n0 + k, off, d0 + q, c0 + q, coff, doff, 2 * q)
                        if k in (4, 8, 12):
                            q = k // 4 - 1
                            act.wait_ge(up_ready, 3 * (done // 2 + g) + q + 1)
                            tap2((CA, CB, CA)[q], (a_tile, b_tile, a_tile + 2)[q])
                        if k in (5, 13):
                            act.wait_ge(conv_a, pairs + k // 8 + 1)
                            act.activation(SA[:], CA[:], ACT.Silu).then_inc(silu_ready, 1)
                        if k == 9:
                            act.wait_ge(gated, pairs + 1)
                            act.wait_ge(halves_used, n0 + off)
                            act.activation(hid[:, 0:2, 0], G[:], ACT.Copy).then_inc(hid_hi, 1)
                        if k in (18, 19, 22, 23):
                            u = {18: 0, 19: 1, 22: 2, 23: 3}[k]
                            act.wait_ge(halves_used, n0 + k + 1 + off)
                            if u >= 2:
                                act.wait_ge(x_added, 2 * done + 4 * g + u - 1)
                            act.activation(down_tail[u % 2], ps[:, 4 * (u % 2):4 * (u % 2) + 4, T:2 * T],
                                           ACT.Copy).then_inc(down_tails, 1)
                        if first and k == 0:
                            norm_sq(norm_i, 3)
                        if first and l == 0 and k == 10:
                            act.wait_ge(kw_in, 16)
                            act.activation(side_w_hi[:, :, 0:80], kw_raw, ACT.Copy)
                            act.activation(side_w_hi[:, :, 80:P], kw_raw[:, :, 0:48], ACT.Copy).then_inc(side_hi, 1)
                        if last and l == 0 and k >= 20:
                            r = {20: 0, 22: 1}.get(k)
                            if r is not None:
                                act.wait_ge(x_added, 4 * GROUPS - 3 + r)
                                norm_hi(2, V_MIXG + KT, r)
                            if k in (21, 23):
                                norm_sq(2, k // 2 - 10)

                group(n0, 0, d0, 0, c0, 0, 0, first=True)
                with act.Fori(1, GROUPS - 1) as g:
                    group(n0 + 24, 24 * g - 24, d0 + 8, 8 * g - 8, c0 + 4, 4 * g - 4, g)
                n = GROUPS - 1
                group(n0 + 24 * n, 0, d0 + 8 * n, 0, c0 + 4 * n, 0, n, last=True)

            ffn(H_FFN0, D_FFN0, C_FFN0, 0, 0, 1)

            for r in (2, 3):
                act.wait_ge(x_added, 4 * GROUPS - 3 + r)
                norm_hi(2, V_MIXG + KT, r)
                norm_sq(2, r)

            def kw_tail():
                act.wait_ge(side_mm, 2)
                act.activation(KI[0:80], ps[0:80, 4, T:2 * T], ACT.Copy).then_inc(side_tail, 1)

            def wi_copy():
                act.wait_ge(wi_turned, 1)
                act.activation(WI[:].rearrange("p a b -> p (a b)"), ps[:, 7, 0:2 * I_HEADS], ACT.Copy,
                               scale=float((I_HEADS * I_DIM) ** -0.5)).then_inc(wi_ready, 1)

            def relus(t):
                for b in range(2):
                    act.wait_ge(score_mm, 2 * t + b + 1)
                    if 2 * t + b:
                        act.wait_ge(relu_used, 2 * t + b)
                    w = (b + 1) * P
                    act.activation(relu[:, :, 0:w], ps[:, 4 + 2 * b:6 + 2 * b, 0:w], ACT.Relu).then_inc(relu_ready, 1)

            for j in range(5):
                n = H_DSA_QI + 4 * j
                for k in range(4):
                    act_split(act, n + k + LEAD, 0)
                    if j == 1 and k == 0:
                        kw_tail()
                    if j == 1 and k == 1:
                        wi_copy()
                    if j and k in (2, 3):
                        relus(2 * (j - 1) + k - 2)
                    if k == 3:
                        tail_copy(n + 3, 0, D_DSA_QI + j, C_DSA_QI + j, 0, 0, 2 * (j % 2))
            act.wait_ge(kv_ready, 1)
            act.activation(sq[:, 0], KV[:, 0], ACT.Square).then_inc(kv_sq, 1)

            def va_copy():
                act.wait_ge(kv_mm, 1)
                act.activation(VA[:].rearrange("p a b -> p (a b)"), ps[:, 4, T:2 * T], ACT.Copy).then_inc(va_ready, 1)

            def q_squares(p):
                act.wait_ge(q_ready, p + 1)
                act.activation(sq[:, 0:2], QT[:], ACT.Square).then_inc(q_sq, 1)

            def exps(p):
                act.wait_ge(max_ready, p + 1)
                for a in range(2):
                    for b in range(2):
                        c = slice(0, P) if b == 0 else slice(P, 3 * P)
                        ins = act.activation(LM[:, a, c], LM[:, a, c], ACT.Exp, bias=mx[:, a, b:b + 1],
                                             accum_out=sums[:, a, b:b + 1])
                ins.then_inc(exp_ready, 1)

            def probs(p):
                act.wait_ge(inv_ready, p + 1)
                for a in range(2):
                    for b in range(2):
                        c = slice(0, P) if b == 0 else slice(P, 3 * P)
                        ins = act.activation(LM[:, a, c], LM[:, a, c], ACT.Copy, scale=sums[:, a, b:b + 1])
                ins.then_inc(probs_ready, 1)

            def pt_copy(p):
                act.wait_ge(probs_turned, p + 1)
                act.activation(PT[:, 0], ps[:, 7, 0:3 * P], ACT.Copy)
                act.activation(PT[:, 1], ps[:, 5, 0:3 * P], ACT.Copy).then_inc(pt_ready, 1)

            def av_hi(p):
                act.wait_ge(av_mm, p + 1)
                act.activation(mix[:, bass.ds(2 * p, 2), 0], ps[:, 7].rearrange("p (a t) -> p a t", a=2),
                               ACT.Copy).then_inc(mix_hi, 1)

            def q_frame(n, off, d, c, doff, p, lags=3):
                for k in range(4):
                    act_split(act, n + k + LEAD, off)
                    if k == 0 and lags > 2:
                        pt_copy(p - 3)
                    if k == 0:
                        q_squares(p - 1)
                    if k == 1 and lags > 1:
                        exps(p - 2)
                    if k == 2 and lags > 1:
                        probs(p - 2)
                    if k == 2 and lags > 2:
                        av_hi(p - 3)
                    if k == 3:
                        tail_copy(n + 3, off, d, c, doff, doff, 2 * (d % 2))

            for k in range(4):
                act_split(act, H_DSA_Q + k + LEAD, 0)
                if k == 1:
                    va_copy()
                if k == 3:
                    tail_copy(H_DSA_Q + 3, 0, D_DSA_Q, C_DSA_Q, 0, 0, 2 * (D_DSA_Q % 2))
            for p in range(1, 4):
                q_frame(H_DSA_Q + 4 * p, 0, D_DSA_Q + p, C_DSA_Q + p, 0, p, p)
            with act.Fori(0, 2) as i:
                q_frame(H_DSA_Q + 16, 8 * i, D_DSA_Q + 4, C_DSA_Q + 4, 2 * i, 2 * i + 4)
                q_frame(H_DSA_Q + 20, 8 * i, D_DSA_Q + 5, C_DSA_Q + 5, 2 * i, 2 * i + 5)

            out_proj(H_WOUT1, D_WOUT1, 3, V_FFNG + KT, {0: (lambda: pt_copy(5), lambda: q_squares(7)), 1: (lambda: exps(6),),
                               2: (lambda: probs(6), lambda: av_hi(5), lambda: pt_copy(6)),
                               3: (lambda: exps(7), lambda: probs(7), lambda: av_hi(6), lambda: pt_copy(7), lambda: av_hi(7))})
            ffn(H_FFN1, D_FFN1, C_FFN1, 1, 2 * GROUPS, 3)
            for j, (b, r) in enumerate(END):
                if j % 2:
                    act.wait_ge(y_turned, j + 1)
                    act.activation(x_tok[:, b, 512 * r:512 * (r + 1)], ps[:, 4 * b + r], ACT.Copy).then_inc(y_copied_odd, 1)

        @block.vector
        def _(dve):
            class Own:
                n = 0
                off = 0
            own = Own()

            def link(ins):
                own.n += 1
                ins.then_inc(chain, 1)
                dve.wait_ge(chain, own.n + own.off)

            def loop(count, per, body, start=0):
                at = own.n
                with dve.Fori(start, start + count) as i:
                    own.off = per * (i - start)
                    body(i)
                assert own.n - at == per, (own.n - at, per)
                own.n = at + per * count
                own.off = 0

            def drain(c, coff, bank):
                dve.wait_ge(tails, c + 1 + coff)
                ins = dve.tensor_tensor(both[:], ps[:, bank:bank + 2, 0:T], tail[:], ALU.add)
                ins.then_inc(psum_free, 1)
                return ins

            def scaled(dst, free_count):
                dve.wait_ge(psum_free, free_count)
                return dve.tensor_tensor(dst, both[:], rms_scale[:].rearrange("p (a t) -> p a t", a=1).broadcast_to([P, 2, T]), ALU.mult)

            def norm_lo(i, g0, r):
                dve.wait_ge(xs_hi, 4 * i + r + 1)
                for k in range(4):
                    tile = bass.ds(4 * r + k, 1)
                    ins = dve.scalar_tensor_tensor(xs[:, tile, 1], X[:, tile], vecs[:, bass.ds(g0 + 4 * r + k, 1)],
                                                   xs[:, tile, 0].bitcast(F32), ALU.mult, ALU.subtract)
                ins.then_inc(xs_ready, 1)

            def norm_total(i):
                dve.wait_ge(squares_used, 4 * i + 4)
                link(dve.tensor_tensor(sq_sum[:, 0:2], sq_sum[:, 0:2], sq_sum[:, 2:4], ALU.add))
                dve.tensor_tensor(sq_sum[:, 0], sq_sum[:, 0], sq_sum[:, 1], ALU.add).then_inc(sq_ready, 1)
                mean(ps[:, 7, 0:2], 2, D, ROOT_X[i])

            def mean(src, n, count, number):
                dve.wait_ge(sums_mm, number + 1)
                dve.tensor_scalar(mean_sq[:, 0:n], src, 1.0 / count, EPS, ALU.mult, ALU.add).then_inc(mean_ready, 1)

            def diagonal(n, number):
                dve.wait_ge(root_ready, number + 1)
                dve.tensor_tensor(diag[:, 0:n], ident[:].rearrange("p (a t) -> p a t", a=1).broadcast_to([P, n, P]),
                                  root[:, 0:n].rearrange("p (a t) -> p a t", t=1).broadcast_to([P, n, P]),
                                  ALU.mult).then_inc(diag_ready, 1)

            def norm_scale(i):
                diagonal(2, ROOT_X[i])
                dve.wait_ge(spread_mm, ROOT_X[i] + 1)
                link(dve.tensor_copy(rms_scale[:], ps[:, 7, 0:T]))

            dve.memset(gate_b[:], 0.0).then_inc(gate_zero, 1)
            dve.memset(ones[:], 1.0)
            dve.memset(power[:], -0.5).then_inc(fills, 1)
            dve.memset(pads[:, :, 0:TAPS - 1], 0.0)
            dve.memset(side_w_hi.bitcast(F32), 0.0)
            dve.memset(side_w_lo.bitcast(F32), 0.0).then_inc(gate_zero, 1)
            dve.wait_ge(vecs_turned, 1)
            dve.tensor_copy(vecs[:], ps[:, 0, 0:V_ROWS])
            for l in range(2):
                ins = dve.tensor_copy(taps[:, l].rearrange("p a b -> p (a b)"), ps[:, 1 + l, 0:TAPS * UP_TILES])
            ins.then_inc(vecs_ready, 1)
            dve.wait_ge(vecs_ready, 1)
            for r in range(KT // 2):
                dve.wait_ge(x_turned, r + 1)
                dve.tensor_copy(X[:, 2 * r:2 * r + 2].rearrange("p a t -> p (a t)"), ps[:, r]).then_inc(x_copied, 1)
            dve.wait_ge(x_copied, KT // 2)
            dve.wait_ge(side_hi, 1)
            dve.tensor_tensor(side_w_lo[:, :, 0:8], gate_raw[:, :, 0:8], side_w_hi[:, :, 0:8].bitcast(F32), ALU.subtract)
            dve.tensor_tensor(side_w_lo[:, :, 32:40], gate_raw[:, :, 8:16], side_w_hi[:, :, 32:40].bitcast(F32),
                              ALU.subtract).then_inc(side_split, 1)
            for r in range(4):
                norm_lo(0, V_MIXG, r)
            for n in range(LEAD):
                dve_split(dve, n, 0)
            norm_add(dve, 0)
            def gates_forget():
                dve.wait_ge(side_tail, 1)
                link(dve.tensor_tensor(gates[:], ps[0:40, 4, 0:T], gate_tail, ALU.add))
                link(dve.tensor_tensor(gates[:], gates[:], rms_scale[0:40], ALU.mult))
                link(dve.tensor_scalar(gates[:], gates[:], gate_b[:, 0:1], None, ALU.add))
                link(dve.tensor_scalar(gA[:], gates[32:40], -1.0, None, ALU.mult))
                link(dve.tensor_copy(gF[:], gates[32:40]))
                dve.tensor_tensor(gB[:], gF[:], gA[:], ALU.max).then_inc(gate_dve, 1)

            def gates_scan():
                dve.wait_ge(gate_act, 1)
                link(dve.scalar_tensor_tensor(gB[:], gF[:], 0.0, gC[:], ALU.min, ALU.subtract))
                link(dve.tensor_tensor_scan(gF[:], ones[0:M_HEADS], gB[:], 0.0, ALU.mult, ALU.add))
                dve.tensor_tensor(gA[:], gates[0:8], gF[:], ALU.subtract).then_inc(a_ready, 1)
                dve.wait_ge(a_ready, 1)
                link(dve.tensor_tensor_scan(gC[:], ones[0:M_HEADS], gA[:], 0.0, ALU.mult, ALU.max))
                dve.tensor_scalar(rows_m[:, 0:T], gC[:], -1.0, None, ALU.mult)
                dve.tensor_tensor(gB[:], gF[:], gC[:], ALU.add).then_inc(gate_dve, 1)

            def gates_rows():
                dve.wait_ge(gate_act, 2)
                link(dve.tensor_scalar(rows_m[:, T:2 * T], rows_m[:, T:2 * T], 1e37, None, ALU.min))
                dve.wait_ge(consts, 1)

            def head_rows_pick(h):
                if not isinstance(h, int) or h > 0:
                    dve.wait_ge(qk_mm, h)
                dve.tensor_scalar(head_rows[:], rows_m[:], ident[0:M_HEADS, bass.ds(h, 1)], None,
                                  ALU.mult).then_inc(rows_ready, 1)

            def head_exponent(h):
                dve.wait_ge(em_ready, h + 1)
                dve.scalar_tensor_tensor(E[:, 0:T], ps[:, 4, 0:T], a_tok[:, 0, bass.ds(h, 1)], neg_future[:],
                                         ALU.add, ALU.add)
                dve.scalar_tensor_tensor(E[:, T:T + P], ps[:, 4, P:T], a_tok[:, 1, bass.ds(h, 1)],
                                         neg_future[:, 0:P], ALU.add, ALU.add).then_inc(e_ready, 1)

            def head_s(h):
                dve.wait_ge(w_ready, h + 1)
                dve.scalar_tensor_tensor(S[:], ps[:, 5, 0:3 * P], float(DK ** -0.5), E[:], ALU.mult,
                                         ALU.mult).then_inc(s_ready, 1)

            def head_h(h):
                dve.wait_ge(pv_mm, h + 1)
                link(dve.scalar_tensor_tensor(den[:], ps[:, 7, 0:T], -1.0, em[:], ALU.mult, ALU.max))
                link(dve.tensor_tensor(den[:], ps[:, 7, 0:T], den[:], ALU.max))
                link(dve.reciprocal(den[:], den[:]))
                dve.tensor_tensor(H[:], ps[:, 6].rearrange("p (a t) -> p a t", a=2),
                                  den[:].rearrange("p (a t) -> p a t", a=1).broadcast_to([P, 2, T]),
                                  ALU.mult).then_inc(h_ready, 1)

            def head_mean(h):
                mean(ps[:, 7, T:T + 2], 2, DV, ROOT_HEADS + h)

            def head_gate(h):
                dve.wait_ge(h_ready, h + 1)
                dve.wait_ge(og_sigmoid, h + 1)
                for j in range(2):
                    g = vecs[:, bass.ds(V_HEADG + 2 * h + j, 1)]
                    ins = dve.scalar_tensor_tensor(HG[:, j], H[:, j], g, og[:, j], ALU.mult, ALU.mult)
                link(ins)

            def head_scale(h):
                dve.wait_ge(spread_mm, ROOT_HEADS + h + 1)
                dve.tensor_tensor(HG[:], HG[:], ps[:, 7, T:2 * T].rearrange("p (a t) -> p a t", a=1).broadcast_to([P, 2, T]),
                                  ALU.mult).then_inc(hg_ready, 1)

            def head_lo(h):
                dve.wait_ge(mix_hi, h + 1)
                dve.tensor_tensor(mix[:, bass.ds(2 * h, 2), 1], HG[:], mix[:, bass.ds(2 * h, 2), 0].bitcast(F32),
                                  ALU.subtract).then_inc(mix_ready, 1)

            def head(n, off, c, coff, h, prev):
                for k in range(12):
                    dve_split(dve, n + k + LEAD, off)
                    if prev is None:
                        if k == 2:
                            norm_total(0)
                        if k == 3:
                            norm_scale(0)
                        if k == 5:
                            gates_forget()
                        if k == 6:
                            gates_scan()
                        if k == 8:
                            gates_rows()
                    if prev is not None:
                        if k == 1:
                            head_exponent(prev)
                        if k == 2:
                            head_s(prev)
                        if k == 4:
                            head_h(prev)
                        if k == 6:
                            head_mean(prev)
                        if k == 7:
                            diagonal(2, ROOT_HEADS + prev)
                        if k == 8:
                            head_gate(prev)
                            head_scale(prev)
                        if k == 9:
                            head_lo(prev)
                    if k == 10:
                        head_rows_pick(h)
                    if k % 4 == 3:
                        j = k // 4
                        drain(c + j, coff, 2 * ((c + j) % 2))
                        ins = scaled((QK, vT, og)[j], c + j + 1 + coff)
                        ins.then_inc((qk_ready, vT_ready, og_ready)[j], 1)
                    if prev is None and k == 9:
                        dve.wait_ge(a_turned, 1)
                        link(dve.tensor_copy(a_tok[:].rearrange("p a b -> p (a b)"), ps[:, 5, 0:2 * M_HEADS]))

            head(0, 0, 0, 0, 0, None)

            def two_heads(i):
                head(12, 24 * i, 3, 6 * i, 2 * i + 1, 2 * i)
                head(24, 24 * i, 6, 6 * i, 2 * i + 2, 2 * i + 1)
            loop(3, 2 * 4, two_heads)
            head(84, 0, 21, 0, 7, 6)

            def out_proj(n, d, i_norm, g0, pre):
                def one(nn, off, dd, doff, tile):
                    b = 2 * (dd % 2)
                    dve.wait_ge(halves_used, nn + 1 + off)
                    xt = X[:, bass.ds(tile, 2)]
                    link(dve.tensor_tensor(xt, ps[:, b:b + 2, 0:T], xt, ALU.add))
                    ins = dve.tensor_tensor(xt, ps[:, b:b + 2, T:2 * T], xt, ALU.add)
                    ins.then_inc(psum_free, 1)
                for j in range(2):
                    for k in range(4):
                        dve_split(dve, n + 4 * j + k + LEAD, 0)
                        for f in pre.get(4 * j + k, ()):
                            f()
                        if 4 * j + k == 5:
                            one(n + 5, 0, d, 0, 0)
                one(n + 7, 0, d + 1, 0, 2)

                def body(i):
                    for j in range(2):
                        for k in range(4):
                            dve_split(dve, n + 8 + 4 * j + k + LEAD, 8 * i)
                            if 4 * j + k == 1:
                                norm_lo(i_norm, g0, i)
                            if 4 * j + k == 5:
                                one(n + 13, 8 * i, d + 2, 2 * i, 4 + 4 * i)
                    one(n + 15, 8 * i, d + 3, 2 * i, 6 + 4 * i)
                loop(3, 2, body)
                norm_lo(i_norm, g0, 3)

            out_proj(H_WOUT0, D_WOUT0, 1, V_FFNG, {
                0: (lambda: head_exponent(7), lambda: head_s(7)),
                1: (lambda: head_h(7),), 2: (lambda: head_mean(7), lambda: head_gate(7), lambda: diagonal(2, ROOT_HEADS + 7)),
                3: (lambda: head_scale(7), lambda: head_lo(7))})

            def ffn(n0, d0, c0, l, done, norm_i):
                def conv(dst, tile0):
                    for tap in (1, 0):
                        for j in range(2):
                            ins = dve.scalar_tensor_tensor(dst[:, j], pads[:, j, tap:tap + T],
                                                           taps[:, l, tap, bass.ds(tile0 + j, 1)], dst[:, j],
                                                           ALU.mult, ALU.add)
                        if tap == 1:
                            link(ins)
                    return ins

                def hid_lo(tile, j):
                    return dve.tensor_tensor(hid[:, tile, 1], G[:, j], hid[:, tile, 0].bitcast(F32), ALU.subtract)

                def taps3(j, tile):
                    w = [taps[:, l, tap, bass.ds(tile, 1)] for tap in range(TAPS)]
                    link(dve.tensor_scalar(CB[:, j], pads[:, j, 2:2 + T], w[2], None, ALU.mult))
                    link(dve.scalar_tensor_tensor(CB[:, j], pads[:, j, 1:1 + T], w[1], CB[:, j], ALU.mult, ALU.add))
                    link(dve.scalar_tensor_tensor(CB[:, j], pads[:, j, 0:T], w[0], CB[:, j], ALU.mult, ALU.add))
                    return dve.tensor_tensor(G[:, j], SA[:, j], CB[:, j], ALU.mult)

                def down_free(count, u):
                    dve.wait_ge(down_tails, count + 1)
                    b = 4 * (u % 2)
                    xt = X[:, 4 * u:4 * u + 4]
                    dve.tensor_tensor(xt, ps[:, b:b + 4, 0:T], xt, ALU.add).then_inc(psum_free, 1)

                def down_add(free_count, u):
                    dve.wait_ge(psum_free, free_count)
                    xt = X[:, 4 * u:4 * u + 4]
                    dve.tensor_tensor(xt, down_tail[u % 2], xt, ALU.add).then_inc(x_added, 1)

                def group(n0, off, d0, doff, c0, coff, g, first=False, last=False):
                    pairs = done + 2 * g
                    a_tile = g * GROUP
                    b_tile = UP_TILES // 2 + g * GROUP
                    for k in range(24):
                        if k == 15:
                            dve.wait_ge(tile_tail, done // 2 + g + 1)
                            link(dve.tensor_tensor(both[:, 0], ps[:, 6, 0:T], tail[:, 0], ALU.add))
                            link(dve.tensor_tensor(pads[:, 0, TAPS - 1:], both[:, 0], rms_scale[:], ALU.mult))
                            dve.wait_ge(silu_ready, pairs + 2)
                            taps3(0, b_tile + 2).then_inc(tile_gated, 1)
                            dve.wait_ge(tails, c0 + 4 + coff)
                            dve.tensor_tensor(both[:, 1], ps[:, 7, 0:T], tail[:, 1], ALU.add).then_inc(psum_free, 1)
                            dve.wait_ge(psum_free, d0 + 4 + doff)
                            link(dve.tensor_tensor(pads[:, 1, TAPS - 1:], both[:, 1], rms_scale[:], ALU.mult))
                            dve.wait_ge(tile_hi, done // 2 + g + 1)
                            hid_lo(2, 0).then_inc(tile_lo, 1)
                            taps3(1, b_tile + 3).then_inc(gated, 1)
                            dve.wait_ge(hid_hi, pairs + 2)
                            hid_lo(3, 1).then_inc(hid_ready, 1)
                        if k == 19:
                            down_free(2 * pairs + 1, 1)
                            down_add(d0 + 5 + doff, 0)
                        if k == 20:
                            down_add(d0 + 6 + doff, 1)
                        if k == 23:
                            down_add(d0 + 7 + doff, 2)
                        if k == 16:
                            dve.wait_ge(pool_split, pairs + 1)
                            dve_split(dve, n0 + 19, off, more=1)
                        elif k == 18:
                            down_free(2 * pairs, 0)
                            dve.wait_ge(pool_split, pairs + 2)
                            dve_split(dve, n0 + 21, off, more=1)
                        elif k not in (15, 17):
                            dve_split(dve, n0 + k + LEAD, off)
                        if first and k == 2:
                            norm_total(norm_i)
                        if first and k == 3:
                            norm_scale(norm_i)
                        if first and l == 0 and k == 10:
                            kw_lo()
                        if k in (3, 7, 11):
                            q = k // 4
                            drain(c0 + q, coff, 2 * q)
                            scaled(pads[:, :, TAPS - 1:], d0 + q + 1 + doff).then_inc(up_ready, 1)
                        if k in (4, 8, 12):
                            q = k // 4 - 1
                            dve.wait_ge(tap2_ready, 3 * (done // 2 + g) + q + 1)
                            ins = conv((CA, CB, CA)[q], (a_tile, b_tile, a_tile + 2)[q])
                            if q == 1:
                                link(ins)
                                dve.wait_ge(silu_ready, pairs + 1)
                                dve.tensor_tensor(G[:], SA[:], CB[:], ALU.mult).then_inc(gated, 1)
                            else:
                                ins.then_inc(conv_a, 1)
                        if k == 9:
                            dve.wait_ge(hid_hi, pairs + 1)
                            dve.tensor_tensor(hid[:, 0:2, 1], G[:], hid[:, 0:2, 0].bitcast(F32),
                                              ALU.subtract).then_inc(hid_ready, 1)
                        if k == 22:
                            down_free(2 * pairs + 2, 2)
                        if last and l == 0 and k in (21, 22):
                            norm_lo(2, V_MIXG + KT, k - 21)
                        if k == 23:
                            down_free(2 * pairs + 3, 3)
                            down_add(d0 + 8 + doff, 3)

                group(n0, 0, d0, 0, c0, 0, 0, first=True)
                loop(GROUPS - 2, 13, lambda g: group(n0 + 24, 24 * g - 24, d0 + 8, 8 * g - 8, c0 + 4, 4 * g - 4, g), start=1)
                n = GROUPS - 1
                group(n0 + 24 * n, 0, d0 + 8 * n, 0, c0 + 4 * n, 0, n, last=True)

            def kw_lo():
                dve.wait_ge(side_hi, 2)
                dve.tensor_tensor(side_w_lo[:, :, 0:80], kw_raw, side_w_hi[:, :, 0:80].bitcast(F32), ALU.subtract)
                dve.tensor_tensor(side_w_lo[:, :, 80:P], kw_raw[:, :, 0:48], side_w_hi[:, :, 80:P].bitcast(F32),
                                  ALU.subtract).then_inc(side_split, 1)

            ffn(H_FFN0, D_FFN0, C_FFN0, 0, 0, 1)

            dve.tensor_scalar(qg[:], vecs[:, V_QG:V_QG + 1], float(DH ** -0.5), None, ALU.mult).then_inc(qg_ready, 1)
            for r in (2, 3):
                norm_lo(2, V_MIXG + KT, r)

            def kw_drain():
                dve.wait_ge(side_tail, 2)
                link(dve.tensor_tensor(wiT[0:80], ps[0:80, 4, 0:T], KI[0:80], ALU.add))
                link(dve.tensor_tensor(wiT[0:80], wiT[0:80], rms_scale[0:80], ALU.mult))
                dve.tensor_copy(KI[0:64], wiT[0:64])
                dve.tensor_copy(KI[64:128], wiT[0:64]).then_inc(kw_ready, 1)

            def accumulate(t):
                for b in range(2):
                    w = (b + 1) * P
                    sc = score[:, 0:P] if b == 0 else score[:, P:3 * P]
                    dve.wait_ge(relu_ready, 2 * t + b + 1)
                    for s in range(2):
                        r = relu[:, s, 0:w]
                        wi = WI[:, b, 2 * t + s:2 * t + s + 1]
                        if t == 0 and s == 0:
                            ins = dve.tensor_scalar(sc, r, wi, None, ALU.mult)
                        else:
                            ins = dve.scalar_tensor_tensor(sc, r, wi, sc, ALU.mult, ALU.add)
                        if s == 0:
                            link(ins)
                    ins.then_inc(relu_used, 1)
                    dve.wait_ge(relu_used, 2 * t + b + 1)

            blocks = (slice(0, P), slice(P, 3 * P))

            def topk_round(r):
                for b in range(2):
                    src = score if r == 0 else work
                    link(dve.max(best[:, b], src[:, blocks[b]]))
                    link(dve.match_replace(out=work[:, blocks[b]], in_to_replace=best[:, b], in_values=src[:, blocks[b]],
                                           imm_value=3 * NEG))

            for j in range(5):
                n = H_DSA_QI + 4 * j
                for k in range(4):
                    dve_split(dve, n + k + LEAD, 0)
                    if j == 0 and k == 2:
                        norm_total(2)
                    if j == 1 and k == 0:
                        kw_drain()
                    if j == 1 and k == 1:
                        dve.wait_ge(wi_ready, 1)
                    if j and k in (2, 3):
                        accumulate(2 * (j - 1) + k - 2)
                    if k == 3:
                        if j == 0:
                            norm_scale(2)
                        drain(C_DSA_QI + j, 0, 2 * (j % 2))
                        ins = scaled(QI[:, 2 * j:2 * j + 2] if j < 4 else KV, D_DSA_QI + j + 1)
                        ins.then_inc(qi_ready if j < 4 else kv_ready, 1)
            link(dve.tensor_tensor(score[:], score[:], mask_q[:], ALU.add))

            def k_root():
                dve.wait_ge(va_ready, 1)
                mean(ps[:, 4, 0:2], 2, DH, ROOT_K)
                diagonal(2, ROOT_K)

            def k_norm():
                dve.wait_ge(spread_mm, ROOT_K + 1)
                dve.wait_ge(kv_ready, 1)
                dve.scalar_tensor_tensor(KN[:], KV[:, 0], vecs[:, V_KG:V_KG + 1], ps[:, 4, 0:T], ALU.mult,
                                         ALU.mult).then_inc(kn_ready, 1)

            def select_mask():
                link(dve.tensor_scalar(work[:], work[:], 2 * NEG, NEG, ALU.is_gt, ALU.mult))
                link(dve.tensor_tensor(score[:], work[:], mask_q[:], ALU.add))

            def q_mean(p):
                mean(ps[:, 4, 0:4], 4, DH, ROOT_Q + p)

            def q_norm(p):
                dve.wait_ge(spread_mm, ROOT_Q + p + 1)
                dve.wait_ge(qg_ready, 1)
                dve.scalar_tensor_tensor(QN[:], QT[:], qg[:, 0:1], ps[:, 4].rearrange("p (a t) -> p a t", a=2),
                                         ALU.mult, ALU.mult).then_inc(qn_ready, 1)

            def softmax_in(p):
                dve.wait_ge(logit_mm, p + 1)
                link(dve.tensor_tensor(LM[:], ps[:, 5:7, 0:3 * P],
                                       score[:].rearrange("p (a t) -> p a t", a=1).broadcast_to([P, 2, 3 * P]), ALU.add))
                for b in range(2):
                    ins = dve.tensor_reduce(mx[:, :, b], LM[:, :, blocks[b]], AX.X, ALU.max)
                link(ins)
                dve.tensor_scalar(mx[:], mx[:], -1.0, None, ALU.mult).then_inc(max_ready, 1)

            def inverse(p):
                dve.wait_ge(exp_ready, p + 1)
                dve.reciprocal(sums[:], sums[:]).then_inc(inv_ready, 1)

            def av_lo(p):
                dve.wait_ge(mix_hi, M_HEADS + p + 1)
                dve.tensor_tensor(mix[:, bass.ds(2 * p, 2), 1], ps[:, 7].rearrange("p (a t) -> p a t", a=2),
                                  mix[:, bass.ds(2 * p, 2), 0].bitcast(F32), ALU.subtract).then_inc(mix_ready, 1)

            def q_frame(n, off, d, c, doff, p, lags=3, extra=None):
                for k in range(4):
                    if k == 3 and lags > 2:
                        av_lo(p - 3)
                    dve_split(dve, n + k + LEAD, off)
                    if k == 1 and lags > 0:
                        q_mean(p - 1)
                    if k == 1 and lags > 1:
                        softmax_in(p - 2)
                    if k == 2 and lags > 0:
                        diagonal(4, ROOT_Q + p - 1)
                    if k == 2 and lags > 1:
                        inverse(p - 2)
                    if extra:
                        extra(k)
                    if k == 3 and lags > 0:
                        q_norm(p - 1)
                    if k == 3:
                        drain(c, doff, 2 * (d % 2))
                        scaled(QT[:], d + 1 + doff).then_inc(q_ready, 1)

            def frame0(k):
                if k == 1:
                    k_root()
                if k == 3:
                    k_norm()
                else:
                    topk_round(k)

            q_frame(H_DSA_Q, 0, D_DSA_Q, C_DSA_Q, 0, 0, 0, frame0)
            q_frame(H_DSA_Q + 4, 0, D_DSA_Q + 1, C_DSA_Q + 1, 0, 1, 1, lambda k: topk_round(3 + k))

            def mask_last(k):
                if k == 0:
                    topk_round(7)
                    select_mask()

            q_frame(H_DSA_Q + 8, 0, D_DSA_Q + 2, C_DSA_Q + 2, 0, 2, 2, mask_last)
            q_frame(H_DSA_Q + 12, 0, D_DSA_Q + 3, C_DSA_Q + 3, 0, 3)

            def two_pairs(i):
                q_frame(H_DSA_Q + 16, 8 * i, D_DSA_Q + 4, C_DSA_Q + 4, 2 * i, 2 * i + 4)
                q_frame(H_DSA_Q + 20, 8 * i, D_DSA_Q + 5, C_DSA_Q + 5, 2 * i, 2 * i + 5)
            loop(2, 4, two_pairs)

            out_proj(H_WOUT1, D_WOUT1, 3, V_FFNG + KT, {
                0: (lambda: q_mean(7), lambda: softmax_in(6)), 1: (lambda: diagonal(4, ROOT_Q + 7), lambda: inverse(6)),
                2: (lambda: av_lo(5), lambda: q_norm(7)),
                3: (lambda: softmax_in(7), lambda: inverse(7), lambda: av_lo(6), lambda: av_lo(7))})
            ffn(H_FFN1, D_FFN1, C_FFN1, 1, 2 * GROUPS, 3)
            for j, (b, r) in enumerate(END):
                if j % 2 == 0:
                    dve.wait_ge(y_turned, j + 1)
                    dve.tensor_copy(x_tok[:, b, 512 * r:512 * (r + 1)], ps[:, 4 * b + r]).then_inc(y_copied_even, 1)

        @block.gpsimd
        def _(pool):
            pool.memset(ident[:], 0.0).then_inc(consts_zero, 1)
            pool.wait_ge(consts_zero, 1)
            pool.affine_select(out=ident[:], in_=ident[:], compare_op=ALU.not_equal, fill=1.0, base=0,
                               pattern=[[-1, P]], channel_multiplier=1).then_inc(ident_ready, 1)
            pool.memset(neg_future[:], 0.0).then_inc(consts_zero, 1)
            pool.memset(mask_q[:], 0.0).then_inc(consts_zero, 1)
            pool.wait_ge(consts_zero, 3)
            pool.affine_select(out=neg_future[:], in_=neg_future[:], compare_op=ALU.is_ge, fill=NEG, base=0,
                               pattern=[[1, T]], channel_multiplier=-1)
            for c in (0, 2 * P):
                ins = pool.affine_select(out=mask_q[:, c:c + P], in_=mask_q[:, c:c + P], compare_op=ALU.is_ge, fill=NEG,
                                         base=0, pattern=[[-1, P]], channel_multiplier=1)
            ins.then_inc(consts, 1)
            pool.wait_ge(fills, 1)

            def inverse_root(number, n):
                pool.wait_ge(mean_ready, number + 1)
                pool.tensor_tensor(root[:, 0:n], mean_sq[:, 0:n], power[:, 0:n], ALU.pow).then_inc(root_ready, 1)

            inverse_root(ROOT_X[0], 2)
            with pool.Fori(0, M_HEADS) as h:
                inverse_root(ROOT_HEADS + h, 2)
            norm_add(pool, 1)
            pool.dma_start(kw_raw, w_in1[:, :, A_KW:A_KW + 80]).then_inc(kw_in, 16)
            inverse_root(ROOT_X[1], 2)

            def ffn(n0):
                with pool.Fori(0, GROUPS) as g:
                    for n in (n0 + 18, n0 + 20):
                        pool.wait_ge(halves_hi, n + 1 + 24 * g)
                        pool.tensor_tensor(split_half(w_lo, n), raw_half(n), split_half(w_hi, n).bitcast(F32),
                                           ALU.subtract).then_inc(pool_split, 1)

            ffn(H_FFN0)
            norm_add(pool, 2)
            inverse_root(ROOT_X[2], 2)
            inverse_root(ROOT_K, 2)
            with pool.Fori(0, A_HEADS // 2) as p:
                inverse_root(ROOT_Q + p, 4)
            norm_add(pool, 3)
            inverse_root(ROOT_X[3], 2)
            ffn(H_FFN1)


_INS = ["x", "mix_norm_g", "ffn_norm_g", "mlstm_w_in", "mlstm_gate_b", "mlstm_head_g", "mlstm_w_out", "dsa_w_in",
        "dsa_q_g", "dsa_k_g", "dsa_w_out", "ffn_w_up", "ffn_dw_w", "ffn_w_down"]


def kernel(**inputs):
    import concourse.bacc as bacc
    from concourse.bass_utils import run_bass_kernel_spmd

    nc = bacc.Bacc("TRN2", target_bir_lowering=False, num_devices=1)
    arrays, args = {}, []
    for name in _INS:
        a = np.ascontiguousarray(inputs[name])
        arrays[f"in_{name}"] = a
        args.append(nc.dram_tensor(f"in_{name}", a.shape, mybir.dt.from_np(a.dtype), kind="ExternalInput").ap())
    y = nc.dram_tensor("out_y", (1, T, D), F32, kind="ExternalOutput").ap()
    trunk(nc, *args, y)
    r = run_bass_kernel_spmd(nc, [arrays], core_ids=[0])
    return r.results[0]["out_y"]
```
